# Optimizing a Trainium2 kernel written in Bass

```python
import jax
import jax.numpy as jnp
from jax import lax
import numpy as np
import jax, jax.numpy as jnp

D_MODEL = 1024
BATCH = 1
SEQ = 256
DEPTH = 2

N_MIXERS = 2
RET_HEADS = 4
RET_QK_DIM = D_MODEL // RET_HEADS
RET_V_DIM = 2 * RET_QK_DIM
RET_CHUNK = 128
RET_IN_DIM = 2 * RET_HEADS * RET_QK_DIM + 2 * RET_HEADS * RET_V_DIM
NSA_HEADS = 16
NSA_GROUPS = 4
NSA_HPG = NSA_HEADS // NSA_GROUPS
NSA_HEAD_DIM = D_MODEL // NSA_HEADS
NSA_KV_DIM = NSA_GROUPS * NSA_HEAD_DIM
NSA_IN_DIM = D_MODEL + 6 * NSA_KV_DIM + 3 * NSA_HEADS
CMP_BLOCK = 32
CMP_STRIDE = 16
CMP_HIDDEN = 256
SEL_BLOCK = 64
SEL_TOP = 16
WINDOW = 512
Q_BLOCK = 128
FORCED_SCORE = 1e4
INVALID_SCORE = -1.0
D_FF = 2816
FFN_RES = 0.5
DN_ALPHA = (2 * DEPTH) ** 0.25
DN_BETA = (8 * DEPTH) ** -0.25
LN_EPS = 1e-5
GN_EPS = 1e-6
NEG_INF = -1e30
ADA_GAIN = 0.1
N_RET_LAYERS = (DEPTH + 1) // 2
N_NSA_LAYERS = DEPTH // 2


def layer_norm(x, g, b):
    xf = x.astype(jnp.float32)
    mu = jnp.mean(xf, -1, keepdims=True)
    var = jnp.mean(jnp.square(xf - mu), -1, keepdims=True)
    return ((xf - mu) * lax.rsqrt(var + LN_EPS) * g + b).astype(x.dtype)

def modulate(x, shift, scale):
    return x * (1.0 + scale[:, None, :]) + shift[:, None, :]

def post_norm_residual(x, y, gate, res_w, g, b):
    return layer_norm(DN_ALPHA * x + res_w * (1.0 + gate[:, None, :]) * y, g, b)

def swiglu(h, w_in, w_out):
    a, u = jnp.split(h @ w_in, 2, axis=-1)
    return (jax.nn.silu(a) * u) @ w_out

def masked_softmax(s, mask, axis):
    p = jax.nn.softmax(jnp.where(mask, s, NEG_INF), axis=axis)
    return p * mask

def retention(h, w_in, w_out):
    B, S, _ = h.shape
    C = RET_CHUNK
    n = S // C
    qk = RET_HEADS * RET_QK_DIM
    q, k, v, g = jnp.split(h @ w_in, [qk, 2 * qk, 2 * qk + RET_HEADS * RET_V_DIM], axis=-1)

    def heads(t, d):
        return t.reshape(B, n, C, RET_HEADS, d).transpose(1, 0, 3, 2, 4).astype(jnp.float32)

    qc = heads(q, RET_QK_DIM)
    kc = heads(k, RET_QK_DIM) * (RET_QK_DIM ** -0.5)
    vc = heads(v, RET_V_DIM)
    log_g = jnp.log(1.0 - jnp.exp2(-5.0 - jnp.arange(RET_HEADS, dtype=jnp.float32)))
    i = jnp.arange(C, dtype=jnp.float32)
    diff = i[:, None] - i[None, :]
    decay_intra = jnp.where(diff >= 0, jnp.exp(log_g[:, None, None] * jnp.maximum(diff, 0.0)), 0.0)
    decay_q = jnp.exp(log_g[:, None] * (i + 1.0))[:, :, None]
    decay_k = jnp.exp(log_g[:, None] * (C - 1.0 - i))[:, :, None]
    decay_state = jnp.exp(log_g * C)[:, None, None]

    def step(state, inp):
        qi, ki, vi = inp
        scores = jnp.einsum('bhcd,bhkd->bhck', qi, ki) * decay_intra
        o = jnp.einsum('bhck,bhke->bhce', scores, vi) + jnp.einsum('bhcd,bhde->bhce', qi * decay_q, state)
        state = decay_state * state + jnp.einsum('bhcd,bhce->bhde', ki * decay_k, vi)
        return state, o

    state0 = jnp.zeros((B, RET_HEADS, RET_QK_DIM, RET_V_DIM), jnp.float32)
    _, o = lax.scan(step, state0, (qc, kc, vc))
    mu = jnp.mean(o, -1, keepdims=True)
    var = jnp.mean(jnp.square(o - mu), -1, keepdims=True)
    o = (o - mu) * lax.rsqrt(var + GN_EPS)
    o = o.transpose(1, 0, 3, 2, 4).reshape(B, S, RET_HEADS * RET_V_DIM)
    return (o * jax.nn.silu(g.astype(jnp.float32))).astype(h.dtype) @ w_out

def alibi_slopes(n):
    return jnp.exp2(-8.0 * jnp.arange(1, n + 1, dtype=jnp.float32) / n)

def cmp_to_sel_overlap(n_cmp, n_sel):
    c0 = np.arange(n_cmp) * CMP_STRIDE
    s0 = np.arange(n_sel) * SEL_BLOCK
    lo = np.maximum(c0[:, None], s0[None, :])
    hi = np.minimum(c0[:, None] + CMP_BLOCK, s0[None, :] + SEL_BLOCK)
    return (np.clip(hi - lo, 0, None) / CMP_BLOCK).astype(np.float32)

def compress(t, pe, w1, w2):
    B, S, G, dh = t.shape
    n_cmp = (S - CMP_BLOCK) // CMP_STRIDE + 1
    idx = jnp.arange(n_cmp)[:, None] * CMP_STRIDE + jnp.arange(CMP_BLOCK)[None, :]
    blocks = t[:, idx] + pe[None, None, :, None, :]
    blocks = blocks.transpose(0, 1, 3, 2, 4).reshape(B, n_cmp, G, CMP_BLOCK * dh)
    return jax.nn.gelu(blocks @ w1) @ w2

def nsa(h, w_in, w_out, pe_k, pe_v, ck_w1, ck_w2, cv_w1, cv_w2):
    B, S, D = h.shape
    G, HPG, dh, kv = NSA_GROUPS, NSA_HPG, NSA_HEAD_DIM, NSA_KV_DIM
    splits = [D + j * kv for j in range(7)]
    q, kc, vc, ks, vs, kw, vw, gates = jnp.split(h @ w_in, splits, axis=-1)
    q = q.reshape(B, S, G, HPG, dh) * (dh ** -0.5)
    kc = compress(kc.reshape(B, S, G, dh), pe_k, ck_w1, ck_w2)
    vc = compress(vc.reshape(B, S, G, dh), pe_v, cv_w1, cv_w2)
    n_cmp = kc.shape[1]
    n_sel = S // SEL_BLOCK
    top = min(SEL_TOP, n_sel)
    ks = ks.reshape(B, n_sel, SEL_BLOCK, G, dh).transpose(0, 3, 1, 2, 4)
    vs = vs.reshape(B, n_sel, SEL_BLOCK, G, dh).transpose(0, 3, 1, 2, 4)
    pad = ((0, 0), (WINDOW, 0), (0, 0), (0, 0))
    kw = jnp.pad(kw.reshape(B, S, G, dh), pad)
    vw = jnp.pad(vw.reshape(B, S, G, dh), pad)
    gates = jax.nn.sigmoid(gates.astype(jnp.float32)).reshape(B, S, G, HPG, 3)
    slopes = alibi_slopes(NSA_HEADS).reshape(G, HPG)
    cmp_end = jnp.arange(n_cmp) * CMP_STRIDE + CMP_BLOCK - 1
    overlap = jnp.asarray(cmp_to_sel_overlap(n_cmp, n_sel))
    blk = jnp.arange(n_sel)
    n_qb = S // Q_BLOCK
    span = WINDOW + Q_BLOCK

    def block_fn(bq):
        b = bq // n_qb
        q0 = (bq % n_qb) * Q_BLOCK
        t = q0 + jnp.arange(Q_BLOCK)
        qi = lax.dynamic_slice(q, (b, q0, 0, 0, 0), (1, Q_BLOCK, G, HPG, dh))[0]
        kcb, vcb = kc[b], vc[b]
        dist_c = t[:, None] - cmp_end[None, :]
        s = jnp.einsum('qghd,ngd->ghqn', qi, kcb).astype(jnp.float32) - slopes[:, :, None, None] * dist_c.astype(jnp.float32)
        p_cmp = masked_softmax(s, dist_c >= 0, -1)
        o_cmp = jnp.einsum('ghqn,ngd->qghd', p_cmp, vcb)
        imp = jnp.einsum('ghqn,nj->gqj', p_cmp, overlap)
        cur = (t // SEL_BLOCK)[:, None]
        forced = (blk == 0) | (blk == cur) | (blk == cur - 1)
        valid = blk[None, :] * SEL_BLOCK <= t[:, None]
        score = jnp.where(valid, jnp.where(forced, FORCED_SCORE, imp), INVALID_SCORE)
        _, sel = lax.top_k(score, top)
        k_g = jax.vmap(lambda kk, ii: kk[ii])(ks[b], sel)
        v_g = jax.vmap(lambda vv, ii: vv[ii])(vs[b], sel)
        pos = sel[..., None] * SEL_BLOCK + jnp.arange(SEL_BLOCK)
        dist_s = t[None, :, None, None] - pos
        s = jnp.einsum('qghd,gqnkd->ghqnk', qi, k_g).astype(jnp.float32) - slopes[:, :, None, None, None] * dist_s[:, None].astype(jnp.float32)
        p = masked_softmax(s, (dist_s >= 0)[:, None], (-2, -1))
        o_sel = jnp.einsum('ghqnk,gqnkd->qghd', p, v_g)
        kwb = lax.dynamic_slice(kw, (b, q0, 0, 0), (1, span, G, dh))[0]
        vwb = lax.dynamic_slice(vw, (b, q0, 0, 0), (1, span, G, dh))[0]
        s_pos = q0 - WINDOW + jnp.arange(span)
        dist_w = t[:, None] - s_pos[None, :]
        mask_w = (dist_w >= 0) & (dist_w < WINDOW) & (s_pos >= 0)[None, :]
        s = jnp.einsum('qghd,kgd->ghqk', qi, kwb).astype(jnp.float32) - slopes[:, :, None, None] * dist_w.astype(jnp.float32)
        p = masked_softmax(s, mask_w, -1)
        o_win = jnp.einsum('ghqk,kgd->qghd', p, vwb)
        gb = lax.dynamic_slice(gates, (b, q0, 0, 0, 0), (1, Q_BLOCK, G, HPG, 3))[0]
        o = gb[..., 0:1] * o_cmp + gb[..., 1:2] * o_sel + gb[..., 2:3] * o_win
        return o.astype(h.dtype)

    o = lax.map(block_fn, jnp.arange(B * n_qb))
    return o.reshape(B, S, D) @ w_out

def first_inputs(seed: int = 0) -> dict:
    key = jax.random.key(seed)
    ks = jax.random.split(key, 20)

    def w(k, shape, fan_in, gain=1.0):
        return jax.random.normal(k, shape, jnp.float32) * (gain * fan_in ** -0.5)

    D = D_MODEL
    dh = NSA_HEAD_DIM
    return {
        'x': jax.random.normal(ks[0], (BATCH, SEQ, D), jnp.float32),
        'c': jax.random.normal(ks[1], (BATCH, D), jnp.float32),
        'ada_w': w(ks[2], (DEPTH, D, 9 * D), D, ADA_GAIN),
        'ada_b': 0.01 * jax.random.normal(ks[3], (DEPTH, 9 * D), jnp.float32),
        'ln_g': 1.0 + 0.02 * jax.random.normal(ks[4], (DEPTH, 3, D), jnp.float32),
        'ln_b': 0.02 * jax.random.normal(ks[5], (DEPTH, 3, D), jnp.float32),
        'ffn_w_in': w(ks[6], (DEPTH, 2, D, 2 * D_FF), D),
        'ffn_w_out': w(ks[7], (DEPTH, 2, D_FF, D), D_FF, DN_BETA),
        'ret_w_in': w(ks[8], (N_RET_LAYERS, D, RET_IN_DIM), D),
        'ret_w_out': w(ks[9], (N_RET_LAYERS, RET_HEADS * RET_V_DIM, D), RET_HEADS * RET_V_DIM, DN_BETA),
        'nsa_w_in': w(ks[10], (N_NSA_LAYERS, D, NSA_IN_DIM), D),
        'nsa_w_out': w(ks[11], (N_NSA_LAYERS, D, D), D, DN_BETA),
        'nsa_pe_k': 0.1 * jax.random.normal(ks[12], (N_NSA_LAYERS, CMP_BLOCK, dh), jnp.float32),
        'nsa_pe_v': 0.1 * jax.random.normal(ks[13], (N_NSA_LAYERS, CMP_BLOCK, dh), jnp.float32),
        'nsa_ck_w1': w(ks[14], (N_NSA_LAYERS, CMP_BLOCK * dh, CMP_HIDDEN), CMP_BLOCK * dh),
        'nsa_ck_w2': w(ks[15], (N_NSA_LAYERS, CMP_HIDDEN, dh), CMP_HIDDEN),
        'nsa_cv_w1': w(ks[16], (N_NSA_LAYERS, CMP_BLOCK * dh, CMP_HIDDEN), CMP_BLOCK * dh),
        'nsa_cv_w2': w(ks[17], (N_NSA_LAYERS, CMP_HIDDEN, dh), CMP_HIDDEN),
    }

def first_block(x, c, ada_w, ada_b, ln_g, ln_b, ffn_w_in, ffn_w_out, ret_w_in, ret_w_out,
              nsa_w_in, nsa_w_out, nsa_pe_k, nsa_pe_v, nsa_ck_w1, nsa_ck_w2, nsa_cv_w1, nsa_cv_w2):
    c_act = jax.nn.silu(c)
    for i in range(DEPTH):
        mod = c_act @ ada_w[i] + ada_b[i]
        sh0, sc0, g0, sh1, sc1, g1, sh2, sc2, g2 = jnp.split(mod, 9, axis=-1)
        y = swiglu(modulate(x, sh0, sc0), ffn_w_in[i, 0], ffn_w_out[i, 0])
        x = post_norm_residual(x, y, g0, FFN_RES, ln_g[i, 0], ln_b[i, 0])
        h = modulate(x, sh1, sc1)
        j = i // N_MIXERS
        if i % N_MIXERS == 0:
            y = retention(h, ret_w_in[j], ret_w_out[j])
        else:
            y = nsa(h, nsa_w_in[j], nsa_w_out[j], nsa_pe_k[j], nsa_pe_v[j],
                    nsa_ck_w1[j], nsa_ck_w2[j], nsa_cv_w1[j], nsa_cv_w2[j])
        x = post_norm_residual(x, y, g1, 1.0, ln_g[i, 1], ln_b[i, 1])
        y = swiglu(modulate(x, sh2, sc2), ffn_w_in[i, 1], ffn_w_out[i, 1])
        x = post_norm_residual(x, y, g2, FFN_RES, ln_g[i, 2], ln_b[i, 2])
    return x


CHUNK = 64
EPS = 1e-6
CONV_CH = D_MODEL // 2
CONV_WIDTH = 31
GLA_HEADS = 4
GLA_DK = D_MODEL // 16
GLA_DV = D_MODEL // 8
GLA_GATE_RANK = 16
GLA_GATE_TAU = 16.0
FOX_HEADS = 16
FOX_HD = D_MODEL // FOX_HEADS
PEER_HEADS = 8
PEER_NKEYS = 128
PEER_N = PEER_NKEYS * PEER_NKEYS
PEER_QDIM = 256
PEER_TOPK = 16
PEER_TOKEN_BLOCK = 128

EVEN_IN = 2 * CONV_CH + 2 * GLA_HEADS * GLA_DK + 2 * GLA_HEADS * GLA_DV + GLA_GATE_RANK
ODD_IN = 3 * FOX_HEADS * FOX_HD + FOX_HEADS


def rms_norm(x, g):
    xf = x.astype(jnp.float32)
    y = xf * lax.rsqrt(jnp.mean(xf * xf, axis=-1, keepdims=True) + EPS)
    return (y * g.astype(jnp.float32)).astype(x.dtype)

def layer_norm_2(x, g, b):
    xf = x.astype(jnp.float32)
    mu = jnp.mean(xf, axis=-1, keepdims=True)
    xc = xf - mu
    y = xc * lax.rsqrt(jnp.mean(xc * xc, axis=-1, keepdims=True) + EPS)
    return (y * g.astype(jnp.float32) + b.astype(jnp.float32)).astype(x.dtype)

def conformer_conv(val, gate, conv_w, conv_b, ln_g, ln_b):
    u = val * jax.nn.sigmoid(gate)
    w = conv_w.astype(u.dtype)[:, None, :]
    y = lax.conv_general_dilated(u, w, window_strides=(1,), padding=[(CONV_WIDTH - 1, 0)],
                                 dimension_numbers=('NWC', 'WIO', 'NWC'),
                                 feature_group_count=u.shape[-1])
    y = y + conv_b.astype(y.dtype)
    return jax.nn.silu(layer_norm_2(y, ln_g, ln_b))

def gla_chunked(q, k, v, log_a):
    B, S, H, dk = q.shape
    dv = v.shape[-1]
    n = S // CHUNK

    def to_chunks(t):
        return t.reshape(B, n, CHUNK, H, t.shape[-1]).transpose(1, 0, 3, 2, 4)

    qc, kc, vc, gc = to_chunks(q * (dk ** -0.5)), to_chunks(k), to_chunks(v), to_chunks(log_a)
    causal = jnp.tril(jnp.ones((CHUNK, CHUNK), dtype=bool))

    def step(state, inp):
        qi, ki, vi, gi = inp
        b = jnp.cumsum(gi, axis=2)
        b_last = b[:, :, -1:, :]
        o_inter = jnp.einsum('bhtk,bhkv->bhtv', qi * jnp.exp(b), state)
        diff = b[:, :, :, None, :] - b[:, :, None, :, :]
        decay = jnp.exp(jnp.where(causal[:, :, None], diff, -jnp.inf))
        attn = jnp.einsum('bhtk,bhsk,bhtsk->bhts', qi, ki, decay)
        o = o_inter + jnp.einsum('bhts,bhsv->bhtv', attn, vi)
        k_dec = ki * jnp.exp(b_last - b)
        new_state = state * jnp.exp(b_last[:, :, 0, :, None]) + jnp.einsum('bhsk,bhsv->bhkv', k_dec, vi)
        return new_state, o

    s0 = jnp.zeros((B, H, dk, dv), jnp.float32)
    _, o = lax.scan(step, s0, (qc, kc, vc, gc))
    return o.transpose(1, 0, 3, 2, 4).reshape(B, S, H, dv)

def even_mix(h, w_in, conv_w, conv_b, ln_g, ln_b, gate_w2, gate_b, gla_norm_g, w_out):
    B, S, _ = h.shape
    hk = GLA_HEADS * GLA_DK
    hv = GLA_HEADS * GLA_DV
    p = h @ w_in
    cuts = [int(c) for c in np.cumsum([CONV_CH, CONV_CH, hk, hk, hv, hv])]
    a_val, a_gate, q, k, v, r, glr = jnp.split(p, cuts, axis=-1)
    y_a = conformer_conv(a_val, a_gate, conv_w, conv_b, ln_g, ln_b)
    f32 = jnp.float32
    log_a = jax.nn.log_sigmoid((glr @ gate_w2 + gate_b).astype(f32)) / GLA_GATE_TAU
    o = gla_chunked(q.reshape(B, S, GLA_HEADS, GLA_DK).astype(f32),
                    k.reshape(B, S, GLA_HEADS, GLA_DK).astype(f32),
                    v.reshape(B, S, GLA_HEADS, GLA_DV).astype(f32),
                    log_a.reshape(B, S, GLA_HEADS, GLA_DK))
    o = rms_norm(o, gla_norm_g).reshape(B, S, hv).astype(h.dtype)
    y_b = o * jax.nn.silu(r)
    return jnp.concatenate([y_a, y_b], axis=-1) @ w_out

def fox_mix(h, w_in, fgate_b, q_g, k_g, w_out):
    B, S, _ = h.shape
    hd = FOX_HEADS * FOX_HD
    p = h @ w_in
    q, k, v, fz = jnp.split(p, [hd, 2 * hd, 3 * hd], axis=-1)
    q = rms_norm(q.reshape(B, S, FOX_HEADS, FOX_HD), q_g).transpose(0, 2, 1, 3)
    k = rms_norm(k.reshape(B, S, FOX_HEADS, FOX_HD), k_g).transpose(0, 2, 1, 3)
    v = v.reshape(B, S, FOX_HEADS, FOX_HD).transpose(0, 2, 1, 3)
    f32 = jnp.float32
    log_f = jax.nn.log_sigmoid(fz.astype(f32) + fgate_b.astype(f32))
    c = jnp.cumsum(log_f, axis=1).transpose(0, 2, 1)
    scale = FOX_HD ** -0.5
    pos = jnp.arange(S)
    outs = []
    for i in range(S // Q_BLOCK):
        lo, hi = i * Q_BLOCK, (i + 1) * Q_BLOCK
        logits = jnp.einsum('bhqd,bhkd->bhqk', q[:, :, lo:hi], k[:, :, :hi]).astype(f32) * scale
        logits = logits + c[:, :, lo:hi, None] - c[:, :, None, :hi]
        mask = pos[lo:hi, None] >= pos[None, :hi]
        probs = jax.nn.softmax(jnp.where(mask, logits, -jnp.inf), axis=-1)
        outs.append(jnp.einsum('bhqk,bhkd->bhqd', probs.astype(v.dtype), v[:, :, :hi]))
    o = jnp.concatenate(outs, axis=2).transpose(0, 2, 1, 3).reshape(B, S, hd)
    return o @ w_out

def peer_ffn(h, wq, keys, u, v):
    B, S, D = h.shape
    f32 = jnp.float32
    half = PEER_QDIM // 2
    q = (h @ wq).reshape(B, S, PEER_HEADS, 2, half).astype(f32)
    s1 = jnp.einsum('bshd,hnd->bshn', q[..., 0, :], keys[:, 0].astype(f32))
    s2 = jnp.einsum('bshd,hnd->bshn', q[..., 1, :], keys[:, 1].astype(f32))
    v1, i1 = lax.top_k(s1, PEER_TOPK)
    v2, i2 = lax.top_k(s2, PEER_TOPK)
    cand = (v1[..., :, None] + v2[..., None, :]).reshape(B, S, PEER_HEADS, PEER_TOPK * PEER_TOPK)
    sc, j = lax.top_k(cand, PEER_TOPK)
    e1 = jnp.take_along_axis(i1, j // PEER_TOPK, axis=-1)
    e2 = jnp.take_along_axis(i2, j % PEER_TOPK, axis=-1)
    experts = e1 * PEER_NKEYS + e2
    gates = jax.nn.softmax(sc, axis=-1)
    nb = (B * S) // PEER_TOKEN_BLOCK
    ne = PEER_HEADS * PEER_TOPK
    hb = h.reshape(nb, PEER_TOKEN_BLOCK, D)
    eb = experts.reshape(nb, PEER_TOKEN_BLOCK, ne)
    gb = gates.reshape(nb, PEER_TOKEN_BLOCK, ne).astype(h.dtype)

    def block(args):
        ht, et, gt = args
        act = jax.nn.gelu(jnp.einsum('td,ted->te', ht, u[et]), approximate=False)
        return jnp.einsum('te,ted->td', gt * act, v[et])

    out = lax.map(block, (hb, eb, gb))
    return out.reshape(B, S, D)

def second_inputs(seed: int = 0) -> dict:
    key = jax.random.key(seed)
    ks = iter(jax.random.split(key, 32))
    n_even = (DEPTH + 1) // 2
    n_odd = DEPTH // 2
    f32 = jnp.float32
    D = D_MODEL

    def nrm(shape, scale):
        return jax.random.normal(next(ks), shape, f32) * scale

    def gain(shape):
        return 1.0 + 0.05 * jax.random.normal(next(ks), shape, f32)

    return {
        'x': nrm((BATCH, SEQ, D), 1.0),
        'ev_norm_mix': gain((n_even, D)),
        'ev_w_in': nrm((n_even, D, EVEN_IN), D ** -0.5),
        'ev_conv_w': nrm((n_even, CONV_WIDTH, CONV_CH), CONV_WIDTH ** -0.5),
        'ev_conv_b': nrm((n_even, CONV_CH), 0.02),
        'ev_conv_ln_g': gain((n_even, CONV_CH)),
        'ev_conv_ln_b': nrm((n_even, CONV_CH), 0.02),
        'ev_gate_w2': nrm((n_even, GLA_GATE_RANK, GLA_HEADS * GLA_DK), GLA_GATE_RANK ** -0.5),
        'ev_gate_b': nrm((n_even, GLA_HEADS * GLA_DK), 0.1),
        'ev_gla_norm_g': gain((n_even, GLA_DV)),
        'ev_w_out': nrm((n_even, CONV_CH + GLA_HEADS * GLA_DV, D), (CONV_CH + GLA_HEADS * GLA_DV) ** -0.5),
        'od_norm_mix': gain((n_odd, D)),
        'od_w_in': nrm((n_odd, D, ODD_IN), D ** -0.5),
        'od_fgate_b': jax.random.uniform(next(ks), (n_odd, FOX_HEADS), f32, minval=1.0, maxval=4.0),
        'od_q_norm_g': gain((n_odd, FOX_HD)),
        'od_k_norm_g': gain((n_odd, FOX_HD)),
        'od_w_out': nrm((n_odd, FOX_HEADS * FOX_HD, D), (FOX_HEADS * FOX_HD) ** -0.5),
        'ffn_norm': gain((DEPTH, D)),
        'peer_wq': nrm((DEPTH, D, PEER_HEADS * PEER_QDIM), D ** -0.5),
        'peer_keys': nrm((DEPTH, PEER_HEADS, 2, PEER_NKEYS, PEER_QDIM // 2), (PEER_QDIM // 2) ** -0.5),
        'peer_u': nrm((DEPTH, PEER_N, D), D ** -0.5),
        'peer_v': nrm((DEPTH, PEER_N, D), (PEER_HEADS * PEER_TOPK) ** -0.5),
    }

def second_block(x, ev_norm_mix, ev_w_in, ev_conv_w, ev_conv_b, ev_conv_ln_g, ev_conv_ln_b,
              ev_gate_w2, ev_gate_b, ev_gla_norm_g, ev_w_out,
              od_norm_mix, od_w_in, od_fgate_b, od_q_norm_g, od_k_norm_g, od_w_out,
              ffn_norm, peer_wq, peer_keys, peer_u, peer_v):
    for layer in range(DEPTH):
        j = layer // 2
        if layer % 2 == 0:
            h = rms_norm(x, ev_norm_mix[j])
            x = x + even_mix(h, ev_w_in[j], ev_conv_w[j], ev_conv_b[j], ev_conv_ln_g[j], ev_conv_ln_b[j],
                             ev_gate_w2[j], ev_gate_b[j], ev_gla_norm_g[j], ev_w_out[j])
        else:
            h = rms_norm(x, od_norm_mix[j])
            x = x + fox_mix(h, od_w_in[j], od_fgate_b[j], od_q_norm_g[j], od_k_norm_g[j], od_w_out[j])
        h = rms_norm(x, ffn_norm[layer])
        x = x + peer_ffn(h, peer_wq[layer], peer_keys[layer], peer_u[layer], peer_v[layer])
    return x


DEPTH_3 = 1

MIX_WIDTH = D_MODEL
HEAD_DIM = 64
ATTN_WIDTH = MIX_WIDTH // 2
GMLP_WIDTH = MIX_WIDTH - ATTN_WIDTH
N_ATTN_HEADS = ATTN_WIDTH // HEAD_DIM
N_GMLP_HEADS = GMLP_WIDTH // HEAD_DIM
GMLP_HEAD_DIM = GMLP_WIDTH // N_GMLP_HEADS
IN_PROJ_WIDTH = 3 * ATTN_WIDTH + 2 * GMLP_WIDTH
MOBA_BLOCK = 256
MOBA_TOPK = 3
Q_CHUNK = 32
GMLP_CHUNK = 128
ROPE_THETA = 10000.0
NORM_EPS = 1e-6
N_MOD = 9
NEG_INF_3 = -1e30


def rmsnorm(x, g):
    xf = x.astype(jnp.float32)
    y = xf * lax.rsqrt(jnp.mean(xf * xf, axis=-1, keepdims=True) + NORM_EPS)
    return (y * g.astype(jnp.float32)).astype(x.dtype)

def layernorm(x, g, b):
    xf = x.astype(jnp.float32)
    mu = jnp.mean(xf, axis=-1, keepdims=True)
    var = jnp.mean(jnp.square(xf - mu), axis=-1, keepdims=True)
    y = (xf - mu) * lax.rsqrt(var + NORM_EPS)
    return (y * g.astype(jnp.float32) + b.astype(jnp.float32)).astype(x.dtype)

def modulate_3(x, shift, scale):
    return x * (1 + scale[:, None, :]) + shift[:, None, :]

def swiglu_3(x, w_gu, w_down):
    g, u = jnp.split(x @ w_gu, 2, axis=-1)
    return (jax.nn.silu(g) * u) @ w_down

def rope(x, pos):
    half = x.shape[-1] // 2
    inv_freq = ROPE_THETA ** (-jnp.arange(half, dtype=jnp.float32) / half)
    ang = pos[:, None] * inv_freq[None, :]
    cos = jnp.cos(ang)[None, :, None, :]
    sin = jnp.sin(ang)[None, :, None, :]
    xf = x.astype(jnp.float32)
    x1, x2 = xf[..., :half], xf[..., half:]
    return jnp.concatenate([x1 * cos - x2 * sin, x2 * cos + x1 * sin], axis=-1).astype(x.dtype)

def moba_attention(q, k, v):
    B, S, H, dh = q.shape
    n_blk = -(-S // MOBA_BLOCK)
    s_pad = n_blk * MOBA_BLOCK
    k_sel = min(MOBA_TOPK, n_blk)
    pad = ((0, 0), (0, s_pad - S), (0, 0), (0, 0))
    q, k, v = (jnp.pad(t, pad).transpose(0, 2, 1, 3) for t in (q, k, v))
    kb = k.reshape(B, H, n_blk, MOBA_BLOCK, dh)
    vb = v.reshape(B, H, n_blk, MOBA_BLOCK, dh)
    k_mean = jnp.mean(kb.astype(jnp.float32), axis=3)
    n_chunks = s_pad // Q_CHUNK
    q_chunks = q.reshape(B, H, n_chunks, Q_CHUNK, dh).transpose(2, 0, 1, 3, 4)
    scale = dh ** -0.5
    b_idx = jnp.arange(B)[:, None, None, None]
    h_idx = jnp.arange(H)[None, :, None, None]
    blk_ids = jnp.arange(n_blk)

    def one_chunk(args):
        qc, ci = args
        q_pos = ci * Q_CHUNK + jnp.arange(Q_CHUNK)
        own = q_pos[0] // MOBA_BLOCK
        gate = jnp.einsum('bhqd,bhnd->bhqn', qc.astype(jnp.float32), k_mean)
        gate = jnp.where(blk_ids < own, gate, NEG_INF_3)
        _, top_idx = lax.top_k(gate, k_sel)
        sel_valid = jnp.arange(k_sel) < own
        own_idx = jnp.broadcast_to(own, top_idx.shape[:-1] + (1,)).astype(top_idx.dtype)
        idx = jnp.concatenate([top_idx, own_idx], axis=-1)
        kg = kb[b_idx, h_idx, idx]
        vg = vb[b_idx, h_idx, idx]
        s = jnp.einsum('bhqd,bhqnkd->bhqnk', qc, kg).astype(jnp.float32) * scale
        key_pos = own * MOBA_BLOCK + jnp.arange(MOBA_BLOCK)
        own_mask = key_pos[None, :] <= q_pos[:, None]
        sel_mask = jnp.broadcast_to(sel_valid[None, :, None], (Q_CHUNK, k_sel, MOBA_BLOCK))
        mask = jnp.concatenate([sel_mask, own_mask[:, None, :]], axis=1)
        s = jnp.where(mask, s, NEG_INF_3)
        p = jax.nn.softmax(s.reshape(B, H, Q_CHUNK, -1), axis=-1).reshape(s.shape)
        return jnp.einsum('bhqnk,bhqnkd->bhqd', p.astype(vg.dtype), vg)

    out = lax.map(one_chunk, (q_chunks, jnp.arange(n_chunks)))
    out = out.transpose(1, 0, 3, 2, 4).reshape(B, s_pad, H, dh)[:, :S]
    return out.reshape(B, S, H * dh)

def gmlp_spatial_gating(u, v, ln_g, ln_b, w_s, b_s):
    B, S, _ = u.shape
    v = layernorm(v, ln_g, ln_b)
    n_c = S // GMLP_CHUNK
    causal = jnp.tril(jnp.ones((GMLP_CHUNK, GMLP_CHUNK), dtype=bool))
    w = jnp.where(causal[None], w_s, 0)
    vc = v.reshape(B, n_c, GMLP_CHUNK, N_GMLP_HEADS, GMLP_HEAD_DIM)
    mixed = jnp.einsum('hts,bnshd->bnthd', w, vc) + b_s.T[None, None, :, :, None]
    return u * mixed.reshape(B, S, GMLP_WIDTH)

def third_inputs(seed: int = 0) -> dict:
    key = jax.random.key(seed)
    ks = jax.random.split(key, 20)
    f32 = jnp.float32
    nrm = lambda k, shape, s: jax.random.normal(k, shape, f32) * s
    L, D = DEPTH_3, D_MODEL
    return {
        "x": nrm(ks[0], (BATCH, SEQ, D), 1.0),
        "c": nrm(ks[1], (BATCH, D), 1.0),
        "w_ada": nrm(ks[2], (L, D, N_MOD * D), 0.5 * D ** -0.5),
        "b_ada": nrm(ks[3], (L, N_MOD * D), 0.01),
        "norm_ffn1": 1.0 + nrm(ks[4], (L, D), 0.01),
        "w_ffn1_gu": nrm(ks[5], (L, D, 2 * D_FF), D ** -0.5),
        "w_ffn1_down": nrm(ks[6], (L, D_FF, D), D_FF ** -0.5),
        "norm_mix": 1.0 + nrm(ks[7], (L, D), 0.01),
        "w_in": nrm(ks[8], (L, D, IN_PROJ_WIDTH), D ** -0.5),
        "gmlp_ln_g": 1.0 + nrm(ks[9], (L, GMLP_WIDTH), 0.01),
        "gmlp_ln_b": nrm(ks[10], (L, GMLP_WIDTH), 0.01),
        "gmlp_w_s": nrm(ks[11], (L, N_GMLP_HEADS, GMLP_CHUNK, GMLP_CHUNK), GMLP_CHUNK ** -0.5),
        "gmlp_b_s": 1.0 + nrm(ks[12], (L, N_GMLP_HEADS, GMLP_CHUNK), 0.01),
        "g_attn_out": 1.0 + nrm(ks[13], (L, ATTN_WIDTH), 0.01),
        "g_gmlp_out": 1.0 + nrm(ks[14], (L, GMLP_WIDTH), 0.01),
        "w_out": nrm(ks[15], (L, MIX_WIDTH, D), MIX_WIDTH ** -0.5),
        "norm_ffn2": 1.0 + nrm(ks[16], (L, D), 0.01),
        "w_ffn2_gu": nrm(ks[17], (L, D, 2 * D_FF), D ** -0.5),
        "w_ffn2_down": nrm(ks[18], (L, D_FF, D), D_FF ** -0.5),
        "norm_final": 1.0 + nrm(ks[19], (D,), 0.01),
    }

def third_block(x, c, w_ada, b_ada, norm_ffn1, w_ffn1_gu, w_ffn1_down, norm_mix, w_in,
              gmlp_ln_g, gmlp_ln_b, gmlp_w_s, gmlp_b_s, g_attn_out, g_gmlp_out, w_out,
              norm_ffn2, w_ffn2_gu, w_ffn2_down, norm_final):
    B, S, D = x.shape
    pos = jnp.arange(S, dtype=jnp.float32)
    c_act = jax.nn.silu(c)
    h = x
    for l in range(DEPTH_3):
        mod = c_act @ w_ada[l] + b_ada[l]
        (sh1, sc1, gt1, sh2, sc2, gt2, sh3, sc3, gt3) = jnp.split(mod, N_MOD, axis=-1)

        y = modulate_3(rmsnorm(h, norm_ffn1[l]), sh1, sc1)
        h = h + 0.5 * gt1[:, None, :] * swiglu_3(y, w_ffn1_gu[l], w_ffn1_down[l])

        y = modulate_3(rmsnorm(h, norm_mix[l]), sh2, sc2)
        proj = y @ w_in[l]
        q, k, v, gu, gv = jnp.split(
            proj, np.cumsum([ATTN_WIDTH, ATTN_WIDTH, ATTN_WIDTH, GMLP_WIDTH]).tolist(), axis=-1)
        q = rope(q.reshape(B, S, N_ATTN_HEADS, HEAD_DIM), pos)
        k = rope(k.reshape(B, S, N_ATTN_HEADS, HEAD_DIM), pos)
        v = v.reshape(B, S, N_ATTN_HEADS, HEAD_DIM)
        attn_out = moba_attention(q, k, v)
        gmlp_out = gmlp_spatial_gating(jax.nn.gelu(gu), jax.nn.gelu(gv), gmlp_ln_g[l],
                                       gmlp_ln_b[l], gmlp_w_s[l], gmlp_b_s[l])
        merged = jnp.concatenate([rmsnorm(attn_out, g_attn_out[l]),
                                  rmsnorm(gmlp_out, g_gmlp_out[l])], axis=-1)
        h = h + gt2[:, None, :] * (merged @ w_out[l])

        y = modulate_3(rmsnorm(h, norm_ffn2[l]), sh3, sc3)
        h = h + 0.5 * gt3[:, None, :] * swiglu_3(y, w_ffn2_gu[l], w_ffn2_down[l])
    return rmsnorm(h, norm_final)


_first_inputs = third_inputs


def third_inputs(seed=0):
    import zlib

    import numpy as np

    out = dict(_first_inputs(seed))
    spreads = {}
    factors = {'b_ada': 4.248,
     'norm_ffn1': 8.0,
     'norm_mix': 8.0,
     'gmlp_ln_g': 8.0,
     'gmlp_ln_b': 8.0,
     'gmlp_b_s': 8.0,
     'g_attn_out': 8.0,
     'g_gmlp_out': 8.0,
     'norm_ffn2': 8.0,
     'norm_final': 5.68}
    for name, (base, spread) in spreads.items():
        noise = np.random.default_rng([zlib.crc32(name.encode()), seed]).standard_normal(out[name].shape)
        drawn = base * np.exp(spread * noise) if base else spread * noise
        out[name] = __import__('jax').numpy.asarray(drawn.astype(out[name].dtype))
    for name, factor in factors.items():
        out[name] = (out[name] * factor).astype(out[name].dtype)
    return out


_narrow_inputs = third_inputs


def third_inputs(seed=0):

    out = dict(_narrow_inputs(seed))
    wider = {'gmlp_ln_g': 12.0,
     'gmlp_ln_b': 12.0,
     'gmlp_b_s': 12.0,
     'g_attn_out': 12.0,
     'g_gmlp_out': 12.0,
     'norm_ffn2': 6.98,
     'norm_final': 6.66}
    for name, times in wider.items():
        mean = out[name].mean()
        out[name] = (mean + times * (out[name] - mean)).astype(out[name].dtype)
    return out


def setup_inputs(seed=0):
    out = dict(first_inputs(seed))
    for name, value in second_inputs(seed + 1).items():
        if name != "x":
            out[name + "_2"] = value
    for name, value in third_inputs(seed + 2).items():
        if name != "x":
            out[name + "_3"] = value
    return out


def reference(
    x, c, ada_w, ada_b, ln_g, ln_b, ffn_w_in, ffn_w_out, ret_w_in, ret_w_out, nsa_w_in,
    nsa_w_out, nsa_pe_k, nsa_pe_v, nsa_ck_w1, nsa_ck_w2, nsa_cv_w1, nsa_cv_w2, ev_norm_mix_2,
    ev_w_in_2, ev_conv_w_2, ev_conv_b_2, ev_conv_ln_g_2, ev_conv_ln_b_2, ev_gate_w2_2,
    ev_gate_b_2, ev_gla_norm_g_2, ev_w_out_2, od_norm_mix_2, od_w_in_2, od_fgate_b_2,
    od_q_norm_g_2, od_k_norm_g_2, od_w_out_2, ffn_norm_2, peer_wq_2, peer_keys_2, peer_u_2,
    peer_v_2, c_3, w_ada_3, b_ada_3, norm_ffn1_3, w_ffn1_gu_3, w_ffn1_down_3, norm_mix_3,
    w_in_3, gmlp_ln_g_3, gmlp_ln_b_3, gmlp_w_s_3, gmlp_b_s_3, g_attn_out_3, g_gmlp_out_3,
    w_out_3, norm_ffn2_3, w_ffn2_gu_3, w_ffn2_down_3, norm_final_3,
):
    x = first_block(
        x, c, ada_w, ada_b, ln_g, ln_b, ffn_w_in, ffn_w_out, ret_w_in, ret_w_out, nsa_w_in,
        nsa_w_out, nsa_pe_k, nsa_pe_v, nsa_ck_w1, nsa_ck_w2, nsa_cv_w1, nsa_cv_w2,
    )
    x = second_block(
        x, ev_norm_mix_2, ev_w_in_2, ev_conv_w_2, ev_conv_b_2, ev_conv_ln_g_2, ev_conv_ln_b_2,
        ev_gate_w2_2, ev_gate_b_2, ev_gla_norm_g_2, ev_w_out_2, od_norm_mix_2, od_w_in_2,
        od_fgate_b_2, od_q_norm_g_2, od_k_norm_g_2, od_w_out_2, ffn_norm_2, peer_wq_2,
        peer_keys_2, peer_u_2, peer_v_2,
    )
    return third_block(
        x, c_3, w_ada_3, b_ada_3, norm_ffn1_3, w_ffn1_gu_3, w_ffn1_down_3, norm_mix_3, w_in_3,
        gmlp_ln_g_3, gmlp_ln_b_3, gmlp_w_s_3, gmlp_b_s_3, g_attn_out_3, g_gmlp_out_3, w_out_3,
        norm_ffn2_3, w_ffn2_gu_3, w_ffn2_down_3, norm_final_3,
    )


_drawn_inputs = setup_inputs


def setup_inputs(seed=0):
    import zlib

    import numpy as np

    out = dict(_drawn_inputs(seed))
    spreads = {}
    factors = {'nsa_pe_k': 5.427, 'gmlp_ln_g_3': 3.455, 'gmlp_ln_b_3': 3.399}
    for name, (base, spread) in spreads.items():
        noise = np.random.default_rng([zlib.crc32(name.encode()), seed]).standard_normal(out[name].shape)
        drawn = base * np.exp(spread * noise) if base else spread * noise
        out[name] = jnp.asarray(drawn.astype(out[name].dtype))
    for name, factor in factors.items():
        out[name] = (out[name] * factor).astype(out[name].dtype)
    return out
```

```python
from contextlib import ExitStack

import numpy as np

import concourse.bass as bass
from concourse import mybir

F32 = mybir.dt.float32
U32 = mybir.dt.uint32
ALU = mybir.AluOpType
ACT = mybir.ActivationFunctionType
AX = mybir.AxisListType.X

P = 128
S = 256
TT = S // P
D = 1024
DC = D // P
D_FF = 2816
FC = D_FF // P
DEPTH = 2
SLOT = 2048
RING = 7
BANK = 512
NB = 4
LN_EPS = 1e-5
EPS = 1e-6
NEG = -1e30
DN_ALPHA = (2 * DEPTH) ** 0.25


class Signal:

    def __init__(self, ctx, nc, name):
        self.name, self.sem = name, ctx.enter_context(nc.semaphore(name))
        self.sent = self.seen = 0

    def send(self):
        self.sent += 1
        return 1

    def take(self, n=1):
        self.seen += n
        return self.seen

    def skip(self, n):
        self.seen += n


class Chip:

    def __init__(self, ctx, nc):
        self.ctx, self.nc = ctx, nc

        def sb(name, shape, dt=F32):
            return ctx.enter_context(nc.sbuf_tensor(name, shape, dt))

        self.x = sb("x_tok", [P, TT, D])
        self.h_tok = sb("h_tok", [P, TT, D])
        self.h_t = sb("h_feat", [P, DC, S])
        self.mod = sb("mod_rows", [P, 3, D])
        self.c_bc = sb("c_rep", [P, DC, P])
        self.ring = sb("weight_ring", [P, RING, SLOT])
        self.const = sb("constants", [P, N_CONST])
        self.small = sb("small", [P, 256])
        self.work = sb("work", [P, N_WORK])
        self.acc = ctx.enter_context(nc.psum_tensor("acc", [P, 4, BANK], F32))
        self.bank = ctx.enter_context(nc.psum_tensor("bank", [P, NB, BANK], F32))

        self.banks_for_scalar = Signal(ctx, nc, "banks_for_scalar")
        self.banks_for_vector = Signal(ctx, nc, "banks_for_vector")
        self.scalar_for_tensor = Signal(ctx, nc, "scalar_for_tensor")
        self.vector_for_tensor = Signal(ctx, nc, "vector_for_tensor")
        self.scalar_for_vector = Signal(ctx, nc, "scalar_for_vector")
        self.vector_for_scalar = Signal(ctx, nc, "vector_for_scalar")
        self.gpsimd_for_vector = Signal(ctx, nc, "gpsimd_for_vector")
        self.gpsimd_for_tensor = Signal(ctx, nc, "gpsimd_for_tensor")
        self.tensor_for_gpsimd = Signal(ctx, nc, "tensor_for_gpsimd")
        self.gate_onehots_for_tensor = Signal(ctx, nc, "gate_onehots_for_tensor")
        self.signals = [self.banks_for_scalar,
                        self.banks_for_vector,
                        self.scalar_for_tensor,
                        self.vector_for_tensor,
                        self.scalar_for_vector,
                        self.vector_for_scalar,
                        self.gpsimd_for_vector,
                        self.gpsimd_for_tensor,
                        self.tensor_for_gpsimd,
                        self.gate_onehots_for_tensor]
        self.dve_step = ctx.enter_context(nc.semaphore("dve_step"))
        self.act_step = ctx.enter_context(nc.semaphore("act_step"))
        self.pool_step = ctx.enter_context(nc.semaphore("pool_step"))
        self.steps = {"dve": 0, "act": 0, "pool": 0}
        self.phase_done = ctx.enter_context(nc.semaphore("phase_done"))
        self.slot_landed = [ctx.enter_context(nc.semaphore(f"slot_landed{i}")) for i in range(RING)]
        self.slots_used = ctx.enter_context(nc.semaphore("slots_used"))
        self.loaded = ctx.enter_context(nc.semaphore("inputs_loaded"))
        self.stored = ctx.enter_context(nc.semaphore("output_stored"))
        self.n_slots = 0
        self.pending = 0

    def c(self, name):
        a, n = CONST_AT[name]
        return self.const[:, a:a + n]

    def slots(self, n):
        a = self.n_slots
        self.n_slots += n
        return a

    def slot(self, s):
        return self.ring[:, s % RING, :]

    def loads(self, s):
        return 16 * (s // RING + 1)

    def mm(self, out, lhs, rhs, start, stop, last=False):
        ins = self.nc.tensor.matmul(out, lhs, rhs, start=start, stop=stop)
        if self.pending and not last:
            ins.then_inc(self.slots_used, self.pending)
            self.pending = 0
        return ins

    def slots_through(self, n=1):
        self.pending += n

    def phase_end(self, eng, index):
        if eng is self.nc.tensor and self.pending:
            eng.drain().then_inc(self.slots_used, self.pending)
            self.pending = 0
        eng.drain().then_inc(self.phase_done, 1)
        eng.wait_ge(self.phase_done, 4 * (index + 1))

    def step(self, engine):
        self.steps[engine] += 1
        return self.steps[engine]


class Stage:
    def __init__(self, k):
        self.k = k

    def tensor(self, pe):
        pass

    def vector(self, dve):
        pass

    def scalar(self, act):
        pass

    def gpsimd(self, pool):
        pass



RET_HEADS = 4
RET_QK = D // RET_HEADS
RET_V = 2 * RET_QK
N_CMP = (S - 32) // 16 + 1
NSA_HEADS, NSA_GROUPS, HD = 16, 4, 64


def constants():
    p = np.arange(P)
    q = np.arange(S)
    tok = p[:, None, None] + P * np.arange(TT)[None, :, None]
    out = {}
    out["ident"] = np.eye(P)
    out["causal_t"] = (tok <= q[None, None, :]).reshape(P, -1)
    out["mask"] = np.where(tok >= q[None, None, :], 0.0, NEG).reshape(P, -1)
    out["dist"] = np.where(tok >= q[None, None, :], tok - q[None, None, :], 1e32).reshape(P, -1)
    out["iota"] = np.broadcast_to(np.arange(P), (P, P))
    end = np.arange(N_CMP) * 16 + 31
    d = tok - end[None, None, :]
    out["cmp_dist"] = np.where(d >= 0, d, 1e32).reshape(P, -1)
    out["cmp_mask"] = (d >= 0).reshape(P, -1)
    inv = (10000.0 ** (-np.arange(32, dtype=np.float32) / 32)).astype(np.float32)
    ang = tok.astype(np.float32) * inv[None, None, :]
    out["cos"] = np.cos(ang).reshape(P, -1)
    out["sin"] = np.sin(ang).reshape(P, -1)
    return {k: np.ascontiguousarray(v, dtype=np.float32) for k, v in out.items()}


CONSTS = constants()
CONST_AT, N_CONST = {}, 0
for _n, _v in CONSTS.items():
    CONST_AT[_n] = (N_CONST, _v.shape[1])
    N_CONST += _v.shape[1]
N_WORK = 26000



class Silu_c(Stage):

    def __init__(self, k, which):
        super().__init__(k)
        self.s = k.slots(1)
        self.which = which

    def scalar(self, act):
        k = self.k
        act.wait_ge(k.slot_landed[(self.s) % RING], k.loads(self.s))
        cs = k.small[:, 0:DC]
        act.activation(cs, k.slot(self.s)[:, 0:DC], ACT.Silu).then_inc(k.act_step, 1)
        act.wait_ge(k.act_step, k.step("act"))
        for j in range(DC):
            ins = act.activation(k.c_bc[:, j, :], k.c("ident"), ACT.Identity, bias=cs[:, j:j + 1], scale=0.0)
        ins.then_inc(k.scalar_for_tensor.sem, k.scalar_for_tensor.send())

    def tensor(self, pe):
        k = self.k
        pe.wait_ge(k.scalar_for_tensor.sem, k.scalar_for_tensor.take())
        pe.sem_inc(k.slots_used, 1)



class Modulation(Stage):

    def __init__(self, k, gate_scale, gate_one):
        super().__init__(k)
        self.gate_scale, self.gate_one = gate_scale, gate_one
        self.s = k.slots(12)
        self.sb = k.slots(2)

    def tensor(self, pe):
        k = self.k
        for b in range(6):
            if b >= NB:
                pe.wait_ge(k.vector_for_tensor.sem, k.vector_for_tensor.take())
            for kk in range(DC):
                s = self.s + 2 * b + kk // 4
                if kk % 4 == 0:
                    pe.wait_ge(k.slot_landed[(s) % RING], k.loads(s))
                mm = k.mm(k.bank[:, b % NB, :], k.c_bc[:, kk, :],
                          k.slot(s)[:, (kk % 4) * 512:(kk % 4 + 1) * 512],
                          start=kk == 0, stop=kk == DC - 1, last=kk == DC - 1)
                if kk % 4 == 3:
                    k.slots_through()
            mm.then_inc(k.banks_for_vector.sem, k.banks_for_vector.send())
        pe.wait_ge(k.vector_for_tensor.sem, k.vector_for_tensor.take(NB))
        pe.wait_ge(k.vector_for_tensor.sem, k.vector_for_tensor.take())
        k.slots_through(2)

    def vector(self, dve):
        k = self.k
        for b in range(6):
            part, half = b // 2, b % 2
            dve.wait_ge(k.banks_for_vector.sem, k.banks_for_vector.take())
            dst = k.mod[:, part, half * 512:(half + 1) * 512]
            dve.tensor_copy(dst, k.bank[:, b % NB, :]).then_inc(k.vector_for_tensor.sem, k.vector_for_tensor.send())
        dve.wait_ge(k.slot_landed[(self.sb) % RING], k.loads(self.sb))
        dve.wait_ge(k.slot_landed[(self.sb + 1) % RING], k.loads(self.sb + 1))
        dve.tensor_tensor(k.mod[:, 0, :], k.mod[:, 0, :], k.slot(self.sb)[:, 0:D], ALU.add).then_inc(k.dve_step, 1)
        dve.wait_ge(k.dve_step, k.step("dve"))
        dve.scalar_tensor_tensor(k.mod[:, 1, :], k.mod[:, 1, :], 1.0, k.slot(self.sb)[:, D:2 * D],
                                            ALU.add, ALU.add).then_inc(k.dve_step, 1)
        dve.wait_ge(k.dve_step, k.step("dve"))
        dve.scalar_tensor_tensor(k.mod[:, 2, :], k.mod[:, 2, :], 1.0 if self.gate_one else 0.0,
                                            k.slot(self.sb + 1)[:, 0:D], ALU.add, ALU.add).then_inc(k.dve_step, 1)
        dve.wait_ge(k.dve_step, k.step("dve"))
        dve.tensor_scalar(k.mod[:, 2, :], k.mod[:, 2, :], self.gate_scale, None, ALU.mult).then_inc(k.vector_for_tensor.sem, k.vector_for_tensor.send())


def rms_rows(k, dve, src_tiles, n, eps, stat):
    for t, src in enumerate(src_tiles):
        ins = dve.scalar_tensor_tensor(k.h_tok[:, t, 0:n], src, 1.0, src, ALU.mult, ALU.mult,
                                       accum_out=stat[:, t:t + 1])
    ins.then_inc(k.dve_step, 1)
    dve.wait_ge(k.dve_step, k.step("dve"))
    T = len(src_tiles)
    inverse_root(k, dve, dve.tensor_scalar(stat[:, 0:T], stat[:, 0:T], 1.0 / n, eps, ALU.mult, ALU.add),
                 stat[:, 0:T])


def inverse_root(k, dve, ins, stat):
    ins.then_inc(k.vector_for_scalar.sem, k.vector_for_scalar.send())
    dve.wait_ge(k.scalar_for_vector.sem, k.scalar_for_vector.take())
    dve.reciprocal(stat, stat).then_inc(k.dve_step, 1)
    dve.wait_ge(k.dve_step, k.step("dve"))


def take_root(k, act, stat):
    act.wait_ge(k.vector_for_scalar.sem, k.vector_for_scalar.take())
    act.activation(stat, stat, ACT.Sqrt).then_inc(k.scalar_for_vector.sem, k.scalar_for_vector.send())


class Pre(Stage):

    def __init__(self, k, norm, modulated, dst=None):
        super().__init__(k)
        self.norm, self.modulated = norm, modulated
        self.s = k.slots(1) if norm else None
        self.dst = dst

    def tensor(self, pe):
        if self.norm:
            pe.wait_ge(self.k.vector_for_tensor.sem, self.k.vector_for_tensor.take())
            self.k.slots_through()

    def scalar(self, act):
        if self.norm:
            take_root(self.k, act, self.k.small[:, 16:18])

    def vector(self, dve):
        k = self.k
        src, dst = k.x, k.h_tok if self.dst is None else self.dst
        if self.norm:
            stat = k.small[:, 16:18]
            rms_rows(k, dve, [k.x[:, t, :] for t in range(TT)], D, EPS, stat)
            dve.wait_ge(k.slot_landed[(self.s) % RING], k.loads(self.s))
            for t in range(TT):
                ins = dve.scalar_tensor_tensor(dst[:, t, :], k.x[:, t, :], stat[:, t:t + 1],
                                               k.slot(self.s)[:, 0:D], ALU.mult, ALU.mult)
            ins.then_inc(k.vector_for_tensor.sem, k.vector_for_tensor.send())
            src = dst
        if self.modulated:
            if self.norm:
                dve.wait_ge(k.vector_for_tensor.sem, k.vector_for_tensor.sent)
            for t in range(TT):
                ins = dve.tensor_tensor(dst[:, t, :], src[:, t, :], k.mod[:, 1, :], ALU.mult)
            ins.then_inc(k.dve_step, 1)
            dve.wait_ge(k.dve_step, k.step("dve"))
            for t in range(TT):
                dve.tensor_tensor(dst[:, t, :], dst[:, t, :], k.mod[:, 0, :], ALU.add)


class ToFeatures(Stage):

    def __init__(self, k, src, dst, chunks):
        super().__init__(k)
        self.src, self.dst, self.chunks = src, dst, chunks
        self.steps = [(t, c, min(4, chunks - c)) for c in range(0, chunks, 4) for t in range(TT)]

    def tensor(self, pe):
        k = self.k
        for i, (t, c, n) in enumerate(self.steps):
            if i >= NB:
                read = k.vector_for_tensor if i % 2 == 0 else k.scalar_for_tensor
                pe.wait_ge(read.sem, read.take())
            for j in range(n):
                mm = pe.transpose(k.bank[:, i % NB, j * P:(j + 1) * P],
                                  self.src[:, t, (c + j) * P:(c + j + 1) * P], k.c("ident"))
            done = k.banks_for_vector if i % 2 == 0 else k.banks_for_scalar
            mm.then_inc(done.sem, done.send())
        for i in range(max(0, len(self.steps) - NB), len(self.steps)):
            (k.vector_for_tensor if i % 2 == 0 else k.scalar_for_tensor).skip(1)

    def evacuate(self, eng, parity):
        k = self.k
        taken, sent = (k.banks_for_vector, k.vector_for_tensor) if parity == 0 else (k.banks_for_scalar, k.scalar_for_tensor)
        for i, (t, c, n) in enumerate(self.steps):
            if i % 2 != parity:
                continue
            eng.wait_ge(taken.sem, taken.take())
            dst = self.dst[:, c:c + n, t * P:(t + 1) * P]
            src = k.bank[:, i % NB, 0:n * P].rearrange("p (c q) -> p c q", q=P)
            ins = eng.tensor_copy(dst, src) if parity == 0 else eng.activation(dst, src, ACT.Copy)
            ins.then_inc(sent.sem, sent.send())

    def vector(self, dve):
        self.evacuate(dve, 0)

    def scalar(self, act):
        self.evacuate(act, 1)


class FfnIn(Stage):

    def __init__(self, k):
        super().__init__(k)
        self.s = k.slots(FC)
        self.hidden = k.work[:, 0:FC * S].rearrange("p (c t) -> p c t", t=S)
        self.act_out = k.work[:, FC * S:FC * S + 2 * S].rearrange("p (b t) -> p b t", t=S)

    def tensor(self, pe):
        k = self.k
        for j in range(FC):
            if j >= NB:
                pe.wait_ge(k.vector_for_tensor.sem, k.vector_for_tensor.take())
            pe.wait_ge(k.slot_landed[(self.s + j) % RING], k.loads(self.s + j))
            for au in range(2):
                for kk in range(DC):
                    mm = k.mm(k.bank[:, j % NB, au * S:(au + 1) * S],
                              k.slot(self.s + j)[:, (au * DC + kk) * P:(au * DC + kk + 1) * P],
                              k.h_t[:, kk, :], start=kk == 0, stop=kk == DC - 1,
                              last=au == 1 and kk == DC - 1)
            mm.then_inc(k.banks_for_scalar.sem, k.banks_for_scalar.send())
            k.slots_through()
        k.vector_for_tensor.skip(NB)

    def scalar(self, act):
        k = self.k
        for j in range(FC):
            act.wait_ge(k.banks_for_scalar.sem, k.banks_for_scalar.take())
            if j >= 2:
                act.wait_ge(k.vector_for_scalar.sem, k.vector_for_scalar.take())
            act.activation(self.act_out[:, j % 2, :], k.bank[:, j % NB, 0:S], ACT.Silu).then_inc(k.scalar_for_vector.sem, k.scalar_for_vector.send())
        k.vector_for_scalar.skip(2)

    def vector(self, dve):
        k = self.k
        for j in range(FC):
            dve.wait_ge(k.scalar_for_vector.sem, k.scalar_for_vector.take())
            ins = dve.tensor_tensor(self.hidden[:, j, :], self.act_out[:, j % 2, :],
                                    k.bank[:, j % NB, S:2 * S], ALU.mult)
            ins.then_inc(k.vector_for_tensor.sem, k.vector_for_tensor.send())
            dve.wait_ge(k.vector_for_tensor.sem, k.vector_for_tensor.sent)
            dve.drain().then_inc(k.vector_for_scalar.sem, k.vector_for_scalar.send())


class OutProj(Stage):

    def __init__(self, k, y, chunks):
        super().__init__(k)
        self.y, self.chunks = y, chunks
        self.s = k.slots(chunks // 2)

    def tensor(self, pe):
        k = self.k
        for c in range(self.chunks):
            s = self.s + c // 2
            if c % 2 == 0:
                pe.wait_ge(k.slot_landed[(s) % RING], k.loads(s))
            for t in range(TT):
                for half in range(2):
                    k.mm(k.acc[:, 2 * t + half, :], self.y[:, c, t * P:(t + 1) * P],
                         k.slot(s)[:, (c % 2) * D + half * 512:(c % 2) * D + (half + 1) * 512],
                         start=c == 0, stop=c == self.chunks - 1)
            if c % 2 == 1:
                k.slots_through()


class Post(Stage):

    def __init__(self, k, norm, gated):
        super().__init__(k)
        self.norm, self.gated = norm, gated
        self.s = k.slots(1) if norm else None

    def tensor(self, pe):
        if self.norm:
            pe.wait_ge(self.k.vector_for_tensor.sem, self.k.vector_for_tensor.take())
            self.k.slots_through()

    def scalar(self, act):
        if self.norm:
            take_root(self.k, act, self.k.small[:, 44:46])

    def vector(self, dve):
        k = self.k
        y = k.acc[:, :, :].rearrange("p (t h) n -> p t (h n)", t=TT)
        for t in range(TT):
            if self.gated:
                ins = dve.tensor_tensor(k.h_tok[:, t, :], y[:, t, :], k.mod[:, 2, :], ALU.mult)
        if self.gated:
            ins.then_inc(k.dve_step, 1)
            dve.wait_ge(k.dve_step, k.step("dve"))
        for t in range(TT):
            add = k.h_tok[:, t, :] if self.gated else y[:, t, :]
            ins = dve.scalar_tensor_tensor(k.x[:, t, :], k.x[:, t, :], DN_ALPHA if self.norm else 1.0, add,
                                           ALU.mult, ALU.add)
        ins.then_inc(k.dve_step, 1)
        dve.wait_ge(k.dve_step, k.step("dve"))
        if not self.norm:
            return
        stats, mv = k.small[:, 16:40].rearrange("p (t c s) -> p t c s", t=TT, c=2), k.small[:, 40:44]
        for t in range(TT):
            for c in range(2):
                ins = dve.bn_stats(stats[:, t, c, :], k.x[:, t, c * 512:(c + 1) * 512])
        ins.then_inc(k.dve_step, 1)
        dve.wait_ge(k.dve_step, k.step("dve"))
        for t in range(TT):
            ins = dve.bn_aggr(mv[:, 2 * t:2 * t + 2], k.small[:, 16 + 12 * t:28 + 12 * t])
        ins.then_inc(k.dve_step, 1)
        dve.wait_ge(k.dve_step, k.step("dve"))
        rstd = k.small[:, 44:46]
        var = mv.rearrange("p (t two) -> p t two", two=2)[:, :, 1]
        inverse_root(k, dve, dve.tensor_scalar(rstd, var, LN_EPS, None, ALU.add), rstd)
        for t in range(TT):
            ins = dve.tensor_scalar(k.x[:, t, :], k.x[:, t, :], mv[:, 2 * t:2 * t + 1], rstd[:, t:t + 1],
                                    ALU.subtract, ALU.mult)
        ins.then_inc(k.dve_step, 1)
        dve.wait_ge(k.dve_step, k.step("dve"))
        dve.wait_ge(k.slot_landed[(self.s) % RING], k.loads(self.s))
        for t in range(TT):
            ins = dve.tensor_tensor(k.x[:, t, :], k.x[:, t, :], k.slot(self.s)[:, 0:D], ALU.mult)
        ins.then_inc(k.dve_step, 1)
        dve.wait_ge(k.dve_step, k.step("dve"))
        for t in range(TT):
            ins = dve.tensor_tensor(k.x[:, t, :], k.x[:, t, :], k.slot(self.s)[:, D:2 * D], ALU.add)
        ins.then_inc(k.vector_for_tensor.sem, k.vector_for_tensor.send())



class ToTokens(Stage):

    def __init__(self, k, blocks):
        super().__init__(k)
        self.blocks = [(w, dst, f, k.slots(2 if w > 256 else 1)) for w, dst, f in blocks]
        self.fills = [(w, dst, f, s, t) for w, dst, f, s in self.blocks for t in range(TT)]

    def by_vector(self, f, t):
        return f is None and t == 0

    def tensor(self, pe):
        k = self.k
        for i, (w, dst, f, s, t) in enumerate(self.fills):
            if i >= NB:
                before = self.fills[i - NB]
                read = k.vector_for_tensor if self.by_vector(before[2], before[4]) else k.scalar_for_tensor
                pe.wait_ge(read.sem, read.take())
            per = 4 if w > 256 else 8
            for kk in range(DC):
                if kk % per == 0 and t == 0:
                    pe.wait_ge(k.slot_landed[(s + kk // per) % RING], k.loads(s + kk // per))
                mm = k.mm(k.bank[:, i % NB, 0:w], k.h_t[:, kk, t * P:(t + 1) * P],
                          k.slot(s + kk // per)[:, (kk % per) * w:(kk % per + 1) * w],
                          start=kk == 0, stop=kk == DC - 1, last=kk == DC - 1)
            done = k.banks_for_vector if self.by_vector(f, t) else k.banks_for_scalar
            mm.then_inc(done.sem, done.send())
            if t == TT - 1:
                k.slots_through(DC // per)
        for w, dst, f, s, t in self.fills[-NB:]:
            (k.vector_for_tensor if self.by_vector(f, t) else k.scalar_for_tensor).skip(1)

    def vector(self, dve):
        k = self.k
        for i, (w, dst, f, s, t) in enumerate(self.fills):
            if self.by_vector(f, t):
                dve.wait_ge(k.banks_for_vector.sem, k.banks_for_vector.take())
                dve.tensor_copy(dst[:, t, :], k.bank[:, i % NB, 0:w]).then_inc(k.vector_for_tensor.sem, k.vector_for_tensor.send())

    def scalar(self, act):
        k = self.k
        for i, (w, dst, f, s, t) in enumerate(self.fills):
            if not self.by_vector(f, t):
                act.wait_ge(k.banks_for_scalar.sem, k.banks_for_scalar.take())
                act.activation(dst[:, t, :], k.bank[:, i % NB, 0:w], f or ACT.Copy).then_inc(k.scalar_for_tensor.sem, k.scalar_for_tensor.send())


class ToFeatureRows(Stage):

    def __init__(self, k, dst, chunks, scaled=0, scale=1.0):
        super().__init__(k)
        self.dst, self.pairs, self.scaled, self.scale = dst, chunks // 2, scaled, scale
        self.s = k.slots(self.pairs)

    def tensor(self, pe):
        k = self.k
        for j in range(self.pairs):
            if j >= NB:
                read = k.vector_for_tensor if j % 2 == 0 else k.scalar_for_tensor
                pe.wait_ge(read.sem, read.take())
            pe.wait_ge(k.slot_landed[(self.s + j) % RING], k.loads(self.s + j))
            for two in range(2):
                for kk in range(DC):
                    mm = k.mm(k.bank[:, j % NB, two * S:(two + 1) * S],
                              k.slot(self.s + j)[:, (two * DC + kk) * P:(two * DC + kk + 1) * P],
                              k.h_t[:, kk, :], start=kk == 0, stop=kk == DC - 1,
                              last=two == 1 and kk == DC - 1)
            done = k.banks_for_vector if j % 2 == 0 else k.banks_for_scalar
            mm.then_inc(done.sem, done.send())
            k.slots_through()
        for j in range(max(0, self.pairs - NB), self.pairs):
            (k.vector_for_tensor if j % 2 == 0 else k.scalar_for_tensor).skip(1)

    def piece(self, j):
        k = self.k
        return (self.dst[:, 2 * j:2 * j + 2, :], k.bank[:, j % NB, :].rearrange("p (c t) -> p c t", t=S),
                self.scale if 2 * j < self.scaled else 1.0)

    def vector(self, dve):
        k = self.k
        for j in range(0, self.pairs, 2):
            dve.wait_ge(k.banks_for_vector.sem, k.banks_for_vector.take())
            dst, src, scale = self.piece(j)
            dve.tensor_scalar(dst, src, scale, None, ALU.mult).then_inc(k.vector_for_tensor.sem, k.vector_for_tensor.send())

    def scalar(self, act):
        k = self.k
        for j in range(1, self.pairs, 2):
            act.wait_ge(k.banks_for_scalar.sem, k.banks_for_scalar.take())
            dst, src, scale = self.piece(j)
            act.activation(dst, src, ACT.Copy, scale=scale).then_inc(k.scalar_for_tensor.sem, k.scalar_for_tensor.send())


class Turn(Stage):

    def __init__(self, k, groups):
        super().__init__(k)
        self.groups = groups

    def tensor(self, pe):
        k = self.k
        for i, (sources, dst) in enumerate(self.groups):
            if i >= NB:
                read = k.vector_for_tensor if i % 2 == 0 else k.scalar_for_tensor
                pe.wait_ge(read.sem, read.take())
            for j, src in enumerate(sources):
                r, c = src.shape
                mm = pe.transpose(k.bank[0:c, i % NB, j * P:j * P + r], src, k.c("ident")[0:r, 0:r])
            done = k.banks_for_vector if i % 2 == 0 else k.banks_for_scalar
            mm.then_inc(done.sem, done.send())
        for i in range(max(0, len(self.groups) - NB), len(self.groups)):
            (k.vector_for_tensor if i % 2 == 0 else k.scalar_for_tensor).skip(1)

    def piece(self, i):
        sources, dst = self.groups[i]
        r, c = sources[0].shape
        n = len(sources)
        return dst, self.k.bank[0:c, i % NB, 0:n * P].rearrange("p (b r) -> p b r", r=P)[:, :, 0:r]

    def vector(self, dve):
        k = self.k
        for i in range(0, len(self.groups), 2):
            dve.wait_ge(k.banks_for_vector.sem, k.banks_for_vector.take())
            dst, src = self.piece(i)
            dve.tensor_copy(dst, src).then_inc(k.vector_for_tensor.sem, k.vector_for_tensor.send())

    def scalar(self, act):
        k = self.k
        for i in range(1, len(self.groups), 2):
            act.wait_ge(k.banks_for_scalar.sem, k.banks_for_scalar.take())
            dst, src = self.piece(i)
            act.activation(dst, src, ACT.Copy).then_inc(k.scalar_for_tensor.sem, k.scalar_for_tensor.send())


def moments(k, dve, pieces, stats, mv, rstd, eps):
    for i, src in enumerate(pieces):
        ins = dve.bn_stats(stats[:, 6 * i:6 * i + 6], src)
    ins.then_inc(k.dve_step, 1)
    dve.wait_ge(k.dve_step, k.step("dve"))
    n = len(pieces)
    for i in range(n):
        ins = dve.bn_aggr(mv[:, 2 * i:2 * i + 2], stats[:, 6 * i:6 * i + 6])
    ins.then_inc(k.dve_step, 1)
    dve.wait_ge(k.dve_step, k.step("dve"))
    var = mv[:, 0:2 * n].rearrange("p (t two) -> p t two", two=2)[:, :, 1]
    inverse_root(k, dve, dve.tensor_scalar(rstd, var, eps, None, ALU.add), rstd)


class Room:

    def __init__(self, k):
        self.k, self.at = k, 0

    def __call__(self, *shape):
        n = int(np.prod(shape))
        a = self.k.work[:, self.at:self.at + n]
        self.at += n
        assert self.at <= N_WORK, self.at
        if len(shape) == 2:
            return a.rearrange("p (a b) -> p a b", b=shape[1])
        if len(shape) == 3:
            return a.rearrange("p (a b c) -> p a b c", b=shape[1], c=shape[2])
        return a



class RetScores(Stage):

    def __init__(self, k, q_t, k_t, dst):
        super().__init__(k)
        self.q_t, self.k_t, self.dst = q_t, k_t, dst
        self.s = k.slots(1)

    def tensor(self, pe):
        k = self.k
        for h in range(RET_HEADS):
            for kt in range(TT):
                for c in range(2):
                    mm = k.mm(k.bank[:, h, kt * S:(kt + 1) * S], self.k_t[:, 2 * h + c, kt * P:(kt + 1) * P],
                              self.q_t[:, 2 * h + c, :], start=c == 0, stop=c == 1, last=True)
            mm.then_inc(k.banks_for_vector.sem, k.banks_for_vector.send())
        pe.wait_ge(k.vector_for_tensor.sem, k.vector_for_tensor.take())
        k.slots_through()

    def vector(self, dve):
        k = self.k
        dve.wait_ge(k.slot_landed[(self.s) % RING], k.loads(self.s))
        for h in range(RET_HEADS):
            dve.wait_ge(k.banks_for_vector.sem, k.banks_for_vector.take())
            ins = dve.tensor_tensor(self.dst[:, h, :], k.bank[:, h, :], k.slot(self.s)[:, h * 512:(h + 1) * 512],
                                    ALU.mult)
        ins.then_inc(k.vector_for_tensor.sem, k.vector_for_tensor.send())


class RetOut(Stage):

    def __init__(self, k, w, v, g, o):
        super().__init__(k)
        self.w, self.v, self.g, self.o = w, v, g, o
        self.jobs = [(t, h) for t in range(TT) for h in range(RET_HEADS)]

    def tensor(self, pe):
        k = self.k
        for i, (t, h) in enumerate(self.jobs):
            if i >= NB:
                pe.wait_ge(k.scalar_for_tensor.sem, k.scalar_for_tensor.take())
            for kt in range(t + 1):
                mm = k.mm(k.bank[:, i % NB, :], self.w[:, h, kt * S + t * P:kt * S + (t + 1) * P],
                          self.v[:, kt, h * RET_V:(h + 1) * RET_V], start=kt == 0, stop=kt == t, last=True)
            mm.then_inc(k.banks_for_scalar.sem, k.banks_for_scalar.send())
        k.scalar_for_tensor.skip(NB)

    def scalar(self, act):
        k = self.k
        for i, (t, h) in enumerate(self.jobs):
            act.wait_ge(k.banks_for_scalar.sem, k.banks_for_scalar.take())
            act.activation(self.o[:, t, h * RET_V:(h + 1) * RET_V], k.bank[:, i % NB, :],
                                            ACT.Copy).then_inc(k.scalar_for_tensor.sem, k.scalar_for_tensor.send())
        act.drain().then_inc(k.scalar_for_vector.sem, k.scalar_for_vector.send())
        take_root(k, act, k.small[:, 80:88])

    def vector(self, dve):
        k = self.k
        dve.wait_ge(k.scalar_for_vector.sem, k.scalar_for_vector.take())
        o = [self.o[:, t, h * RET_V:(h + 1) * RET_V] for t, h in self.jobs]
        moments(k, dve, o, k.small[:, 16:64], k.small[:, 64:80], k.small[:, 80:88], EPS)
        for i in range(len(o)):
            ins = dve.tensor_scalar(o[i], o[i], k.small[:, 64 + 2 * i:65 + 2 * i], k.small[:, 80 + i:81 + i],
                                    ALU.subtract, ALU.mult)
        ins.then_inc(k.dve_step, 1)
        dve.wait_ge(k.dve_step, k.step("dve"))
        for t in range(TT):
            dve.tensor_tensor(self.g[:, t, :], self.o[:, t, :], self.g[:, t, :], ALU.mult)


def ret_decay():
    g = 1.0 - 2.0 ** (-5.0 - np.arange(RET_HEADS))
    key = np.arange(P)[:, None, None, None] + P * np.arange(TT)[None, None, :, None]
    d = np.arange(S)[None, None, None, :] - key
    w = np.where(d >= 0, g[None, :, None, None] ** np.maximum(d, 0), 0.0) * RET_QK ** -0.5
    return w.reshape(P, -1).astype(np.float32)



PEER_HEADS, N_KEYS, TOP = 8, 128, 16
PAIRS = PEER_HEADS * TOP
HALF = N_KEYS // 2


class KeyScores(Stage):

    def __init__(self, k, q_t, dst):
        super().__init__(k)
        self.q_t, self.dst = q_t, dst
        self.s = k.slots(1)
        self.fills = [(t, g) for t in range(TT) for g in range(2 * PEER_HEADS // 4)]

    def tensor(self, pe):
        k = self.k
        pe.wait_ge(k.slot_landed[(self.s) % RING], k.loads(self.s))
        for i, (t, g) in enumerate(self.fills):
            if i >= NB:
                read = k.vector_for_tensor if i % 2 == 0 else k.scalar_for_tensor
                pe.wait_ge(read.sem, read.take())
            for j in range(4):
                hs = 4 * g + j
                mm = k.mm(k.bank[:, i % NB, j * P:(j + 1) * P], self.q_t[:, hs, t * P:(t + 1) * P],
                          k.slot(self.s)[:, hs * P:(hs + 1) * P], start=True, stop=True, last=True)
            done = k.banks_for_vector if i % 2 == 0 else k.banks_for_scalar
            mm.then_inc(done.sem, done.send())
        k.slots_through()
        k.vector_for_tensor.skip(NB // 2)
        k.scalar_for_tensor.skip(NB // 2)

    def vector(self, dve):
        k = self.k
        for i in range(0, len(self.fills), 2):
            t, g = self.fills[i]
            dve.wait_ge(k.banks_for_vector.sem, k.banks_for_vector.take())
            dve.tensor_copy(self.dst[:, t, g * 512:(g + 1) * 512], k.bank[:, i % NB, :]).then_inc(k.vector_for_tensor.sem, k.vector_for_tensor.send())

    def scalar(self, act):
        k = self.k
        for i in range(1, len(self.fills), 2):
            t, g = self.fills[i]
            act.wait_ge(k.banks_for_scalar.sem, k.banks_for_scalar.take())
            act.activation(self.dst[:, t, g * 512:(g + 1) * 512], k.bank[:, i % NB, :],
                                            ACT.Copy).then_inc(k.scalar_for_tensor.sem, k.scalar_for_tensor.send())


def top16(k, dve, rows, values, index):
    for r, v in zip(rows, values):
        ins = dve.max(v[:, 0:8], r)
    ins.then_inc(k.dve_step, 1)
    dve.wait_ge(k.dve_step, k.step("dve"))
    for r, v, i in zip(rows, values, index):
        ins = dve.max_index(i[:, 0:8], v[:, 0:8], r)
    ins.then_inc(k.dve_step, 1)
    dve.wait_ge(k.dve_step, k.step("dve"))
    for r, v in zip(rows, values):
        ins = dve.match_replace(r, v[:, 0:8], r, NEG)
    ins.then_inc(k.dve_step, 1)
    dve.wait_ge(k.dve_step, k.step("dve"))
    for r, v in zip(rows, values):
        ins = dve.max(v[:, 8:16], r)
    ins.then_inc(k.dve_step, 1)
    dve.wait_ge(k.dve_step, k.step("dve"))
    for r, v, i in zip(rows, values, index):
        ins = dve.max_index(i[:, 8:16], v[:, 8:16], r)
    ins.then_inc(k.dve_step, 1)
    dve.wait_ge(k.dve_step, k.step("dve"))


class Route(Stage):

    def __init__(self, k, scores, room, out):
        super().__init__(k)
        self.scores, self.out = scores, out
        nk = 2 * PEER_HEADS * TOP
        self.val, self.idx, self.idf = room(TT, nk), room(TT, nk), room(TT, nk)
        self.cand = room(TT, PEER_HEADS * TOP * TOP)
        self.hot = room(PAIRS * TOP)
        self.best, self.at, self.a, self.b = (room(TT, PAIRS) for _ in range(4))
        self.sum = room(TT * PEER_HEADS)

    def scalar(self, act):
        k = self.k
        act.wait_ge(k.vector_for_scalar.sem, k.vector_for_scalar.take())
        act.activation(self.out[:, 2, :], self.best, ACT.Exp).then_inc(k.scalar_for_vector.sem, k.scalar_for_vector.send())

    def vector(self, dve):
        k = self.k
        idx, at = self.idx.bitcast(U32), self.at.bitcast(U32)
        rows = [self.scores[:, t, i * N_KEYS:(i + 1) * N_KEYS] for t in range(TT) for i in range(2 * PEER_HEADS)]
        cut = lambda b: [b[:, t, i * TOP:(i + 1) * TOP] for t in range(TT) for i in range(2 * PEER_HEADS)]
        top16(k, dve, rows, cut(self.val), cut(idx))
        dve.tensor_copy(self.idf, idx).then_inc(k.dve_step, 1)
        dve.wait_ge(k.dve_step, k.step("dve"))
        side = lambda b, t, s: b[:, t, :].rearrange("p (h s j) -> p h s j", s=2, j=TOP)[:, :, s, :]
        full = [P, PEER_HEADS, TOP, TOP]
        for t in range(TT):
            cand = self.cand[:, t, :].rearrange("p (h a b) -> p h a b", a=TOP, b=TOP)
            ins = dve.tensor_tensor(cand, side(self.val, t, 0).unsqueeze(3).to_broadcast(full),
                                    side(self.val, t, 1).unsqueeze(2).to_broadcast(full), ALU.add)
        ins.then_inc(k.dve_step, 1)
        dve.wait_ge(k.dve_step, k.step("dve"))
        rows = [self.cand[:, t, h * 256:(h + 1) * 256] for t in range(TT) for h in range(PEER_HEADS)]
        cut = lambda b: [b[:, t, h * TOP:(h + 1) * TOP] for t in range(TT) for h in range(PEER_HEADS)]
        top16(k, dve, rows, cut(self.best), cut(at))
        a, b = self.a.bitcast(U32), self.b.bitcast(U32)
        dve.tensor_single_scalar(a, at, 4, ALU.logical_shift_right)
        dve.tensor_single_scalar(b, at, 15, ALU.bitwise_and).then_inc(k.dve_step, 1)
        dve.wait_ge(k.dve_step, k.step("dve"))
        dve.tensor_copy(self.a, a)
        dve.tensor_copy(self.b, b).then_inc(k.dve_step, 1)
        dve.wait_ge(k.dve_step, k.step("dve"))
        best = self.best.rearrange("p t (h j) -> p (t h) j", j=TOP)
        n = [P, TT * PEER_HEADS, TOP]
        dve.tensor_copy(self.sum, best[:, :, 0]).then_inc(k.dve_step, 1)
        dve.wait_ge(k.dve_step, k.step("dve"))
        dve.tensor_tensor(best, best, self.sum.unsqueeze(2).to_broadcast(n), ALU.subtract).then_inc(k.vector_for_scalar.sem, k.vector_for_scalar.send())
        hot = self.hot.rearrange("p (m j) -> p m j", j=TOP)
        hot4 = self.hot.rearrange("p (h m j) -> p h m j", m=TOP, j=TOP)
        for s, place in ((0, self.a), (1, self.b)):
            for t in range(TT):
                dve.tensor_tensor(hot, place[:, t, :].unsqueeze(2).to_broadcast([P, PAIRS, TOP]),
                                             k.c("iota")[:, 0:TOP].unsqueeze(1).to_broadcast([P, PAIRS, TOP]),
                                             ALU.is_equal).then_inc(k.dve_step, 1)
                dve.wait_ge(k.dve_step, k.step("dve"))
                dve.tensor_tensor(hot4, hot4, side(self.idf, t, s).unsqueeze(2).to_broadcast(full),
                                             ALU.mult).then_inc(k.dve_step, 1)
                dve.wait_ge(k.dve_step, k.step("dve"))
                dve.tensor_reduce(self.out[:, s, t * PAIRS:(t + 1) * PAIRS], hot, AX, ALU.add).then_inc(k.dve_step, 1)
                dve.wait_ge(k.dve_step, k.step("dve"))
        dve.wait_ge(k.scalar_for_vector.sem, k.scalar_for_vector.take())
        gate = self.out[:, 2, :].rearrange("p (m j) -> p m j", j=TOP)
        dve.tensor_reduce(self.sum, gate, AX, ALU.add).then_inc(k.dve_step, 1)
        dve.wait_ge(k.dve_step, k.step("dve"))
        dve.reciprocal(self.sum, self.sum).then_inc(k.dve_step, 1)
        dve.wait_ge(k.dve_step, k.step("dve"))
        dve.tensor_tensor(gate, gate, self.sum.unsqueeze(2).to_broadcast(n), ALU.mult)


TOKENS_AT_ONCE = BANK // HALF
HOT_RING = 2 * TOKENS_AT_ONCE


class SpreadGates(Stage):

    def __init__(self, k, half, pairs, gates, hot1, hot2):
        super().__init__(k)
        self.half, self.pairs, self.gates, self.hot1, self.hot2 = half, pairs, gates, hot1, hot2
        self.fills = S // TOKENS_AT_ONCE

    def tensor(self, pe):
        k = self.k
        for f in range(self.fills):
            if f >= NB:
                read = k.vector_for_tensor if f % 2 == 0 else k.scalar_for_tensor
                pe.wait_ge(read.sem, read.take())
            pe.wait_ge(k.gpsimd_for_tensor.sem, k.gpsimd_for_tensor.take())
            pe.wait_ge(k.gate_onehots_for_tensor.sem, k.gate_onehots_for_tensor.take())
            for j in range(TOKENS_AT_ONCE):
                r = (f * TOKENS_AT_ONCE + j) % HOT_RING
                mm = k.mm(k.bank[:, f % NB, j * HALF:(j + 1) * HALF], self.hot2[:, r, :], self.hot1[:, r, :],
                          start=True, stop=True, last=True)
            done = k.banks_for_vector if f % 2 == 0 else k.banks_for_scalar
            mm.then_inc(done.sem, done.send())
            pe.drain().then_inc(k.tensor_for_gpsimd.sem, k.tensor_for_gpsimd.send())
        (k.vector_for_tensor).skip(NB // 2)
        (k.scalar_for_tensor).skip(NB // 2)

    def gpsimd(self, pool):
        k = self.k
        for f in range(self.fills):
            if f >= 2:
                pool.wait_ge(k.tensor_for_gpsimd.sem, k.tensor_for_gpsimd.take())
            for j in range(TOKENS_AT_ONCE):
                t = f * TOKENS_AT_ONCE + j
                ins = pool.tensor_scalar(self.hot2[:, t % HOT_RING, :], k.c("iota"), self.pairs[:, 1, t:t + 1],
                                         None, ALU.is_equal)
            ins.then_inc(k.gpsimd_for_tensor.sem, k.gpsimd_for_tensor.send())
            pool.drain().then_inc(k.gpsimd_for_vector.sem, k.gpsimd_for_vector.send())
        k.tensor_for_gpsimd.skip(2)

    def vector(self, dve):
        k = self.k
        first = k.c("iota")[:, self.half * HALF:(self.half + 1) * HALF]

        def evacuate(f):
            if f % 2 == 0:
                dve.wait_ge(k.banks_for_vector.sem, k.banks_for_vector.take())
                dve.tensor_copy(*self.piece(f)).then_inc(k.vector_for_tensor.sem, k.vector_for_tensor.send())

        for f in range(self.fills):
            if f >= 2:
                evacuate(f - 2)
            dve.wait_ge(k.gpsimd_for_vector.sem, k.gpsimd_for_vector.take())
            for j in range(TOKENS_AT_ONCE):
                t = f * TOKENS_AT_ONCE + j
                ins = dve.tensor_scalar(self.hot1[:, t % HOT_RING, :], first, self.pairs[:, 0, t:t + 1],
                                        self.pairs[:, 2, t:t + 1], ALU.is_equal, ALU.mult)
            ins.then_inc(k.gate_onehots_for_tensor.sem, k.gate_onehots_for_tensor.send())
        evacuate(self.fills - 2)
        evacuate(self.fills - 1)

    def piece(self, f):
        n = TOKENS_AT_ONCE
        return (self.gates[:, :, f * n:(f + 1) * n],
                self.k.bank[:, f % NB, :].rearrange("p (t i) -> p i t", t=n))

    def scalar(self, act):
        k = self.k
        for f in range(1, self.fills, 2):
            act.wait_ge(k.banks_for_scalar.sem, k.banks_for_scalar.take())
            act.activation(*self.piece(f), ACT.Copy).then_inc(k.scalar_for_tensor.sem, k.scalar_for_tensor.send())


class Experts(Stage):

    def __init__(self, k, half, gates, act_out, gated):
        super().__init__(k)
        self.half, self.gates, self.act_out, self.gated = half, gates, act_out, gated
        self.s = k.slots(HALF)

    def tensor(self, pe):
        k = self.k

        def through_v(c):
            pe.wait_ge(k.vector_for_tensor.sem, k.vector_for_tensor.take())
            for t in range(TT):
                for h in range(2):
                    k.mm(k.acc[:, 2 * t + h, :], self.gated[:, c % 2, t * P:(t + 1) * P],
                         k.slot(self.s + c)[:, D + h * 512:D + (h + 1) * 512],
                         start=self.half == 0 and c == 0, stop=self.half == 1 and c == HALF - 1)
            k.slots_through()

        for c in range(HALF):
            pe.wait_ge(k.slot_landed[(self.s + c) % RING], k.loads(self.s + c))
            for kk in range(DC):
                mm = k.mm(k.bank[:, c % NB, 0:S], k.slot(self.s + c)[:, kk * P:(kk + 1) * P], k.h_t[:, kk, :],
                          start=kk == 0, stop=kk == DC - 1, last=kk == DC - 1)
            mm.then_inc(k.banks_for_scalar.sem, k.banks_for_scalar.send())
            if c >= 1:
                through_v(c - 1)
        through_v(HALF - 1)

    def scalar(self, act):
        k = self.k
        for c in range(HALF):
            act.wait_ge(k.banks_for_scalar.sem, k.banks_for_scalar.take())
            if c >= 2:
                act.wait_ge(k.vector_for_scalar.sem, k.vector_for_scalar.take())
            act.activation(self.act_out[:, c % 2, :], k.bank[:, c % NB, 0:S], ACT.Gelu).then_inc(k.scalar_for_vector.sem, k.scalar_for_vector.send())
        k.vector_for_scalar.skip(2)

    def vector(self, dve):
        k = self.k
        for c in range(HALF):
            dve.wait_ge(k.scalar_for_vector.sem, k.scalar_for_vector.take())
            ins = dve.tensor_tensor(self.gated[:, c % 2, :], self.act_out[:, c % 2, :], self.gates[:, c, :],
                                    ALU.mult)
            ins.then_inc(k.vector_for_tensor.sem, k.vector_for_tensor.send())
            dve.drain().then_inc(k.vector_for_scalar.sem, k.vector_for_scalar.send())



class Scores(Stage):

    def __init__(self, k, jobs, top, total, keep=None, extra_slots=0):
        super().__init__(k)
        self.jobs, self.top, self.total, self.keep = jobs, top, total, keep
        self.extra = extra_slots
        self.s = k.slots(extra_slots) if extra_slots else None

    def tensor(self, pe):
        k = self.k
        if self.extra:
            pe.wait_ge(k.slot_landed[(self.s) % RING], k.loads(self.s))
        for i, (product, n, how, p) in enumerate(self.jobs):
            if i >= NB:
                pe.wait_ge(k.vector_for_tensor.sem, k.vector_for_tensor.take())
            product(k.bank[:, i % NB, 0:n]).then_inc(k.banks_for_vector.sem, k.banks_for_vector.send())
        k.vector_for_tensor.skip(NB)
        k.slots_through(self.extra)

    def vector(self, dve):
        k = self.k
        n_jobs = len(self.jobs)
        begun = []

        def row_max(i):
            n, p = self.jobs[i][1], self.jobs[i][3]
            dve.wait_ge(k.vector_for_tensor.sem, begun[i])
            dve.tensor_reduce(self.top[:, i:i + 1], p, AX, ALU.max, negate=True).then_inc(k.vector_for_scalar.sem, k.vector_for_scalar.send())

        for i, (product, n, how, p) in enumerate(self.jobs):
            dve.wait_ge(k.banks_for_vector.sem, k.banks_for_vector.take())
            how(dve, p, k.bank[:, i % NB, 0:n]).then_inc(k.vector_for_tensor.sem, k.vector_for_tensor.send())
            begun.append(k.vector_for_tensor.sent)
            if i >= 1:
                row_max(i - 1)
        row_max(n_jobs - 1)
        dve.wait_ge(k.scalar_for_vector.sem, k.scalar_for_vector.take())
        if self.keep is not None:
            for i, (product, n, how, p) in enumerate(self.jobs):
                ins = dve.tensor_tensor(p, p, self.keep(i), ALU.mult)
        dve.reciprocal(self.total[:, 0:n_jobs], self.total[:, 0:n_jobs])

    def scalar(self, act):
        k = self.k
        for i, (product, n, how, p) in enumerate(self.jobs):
            act.wait_ge(k.vector_for_scalar.sem, k.vector_for_scalar.take())
            act.activation(p, p, ACT.Exp, bias=self.top[:, i:i + 1], accum_out=self.total[:, i:i + 1])
        act.drain().then_inc(k.scalar_for_vector.sem, k.scalar_for_vector.send())


class Values(Stage):

    def __init__(self, k, jobs, add, width=64):
        super().__init__(k)
        self.jobs, self.add, self.w = jobs, add, width
        self.per = BANK // width

    def tensor(self, pe):
        k = self.k
        for i, (p_t, v, factor, out) in enumerate(self.jobs):
            f, j = i // self.per, i % self.per
            if j == 0 and f >= NB:
                pe.wait_ge(k.vector_for_tensor.sem, k.vector_for_tensor.take())
            for a, (lhs, rhs) in enumerate(zip(p_t, v)):
                mm = k.mm(k.bank[:, f % NB, j * self.w:(j + 1) * self.w], lhs, rhs, start=a == 0,
                          stop=a == len(v) - 1, last=True)
            if j == self.per - 1:
                mm.then_inc(k.banks_for_vector.sem, k.banks_for_vector.send())
        fills = len(self.jobs) // self.per
        k.vector_for_tensor.skip(min(NB, fills))

    def vector(self, dve):
        k = self.k
        for i, (p_t, v, factor, out) in enumerate(self.jobs):
            f, j = i // self.per, i % self.per
            if j == 0:
                dve.wait_ge(k.banks_for_vector.sem, k.banks_for_vector.take())
            src = k.bank[:, f % NB, j * self.w:(j + 1) * self.w]
            if self.add:
                ins = dve.scalar_tensor_tensor(out, src, factor, out, ALU.mult, ALU.add)
            else:
                ins = dve.tensor_scalar(out, src, factor, None, ALU.mult)
            if j == self.per - 1:
                ins.then_inc(k.vector_for_tensor.sem, k.vector_for_tensor.send())


def weight_blocks(p0, p1, heads):
    return [(t, h, p0[:, h, :] if t == 0 else p1[:, h, :]) for t in range(TT) for h in range(heads)]


def turned_blocks(k, p, p_t, n):
    return Turn(k, [([p[:, i + j, :] for j in range(4)], p_t[:, i:i + 4, :]) for i in range(0, n, 4)])


def causal_attention(k, heads, q, kt, v, product_extra, how, p, p_t, top, total, factor, out, add,
                     extra_slots=0):
    jobs, value_jobs = [], []
    for t in range(TT):
        for h in range(heads):
            n = (t + 1) * P
            b = h if t == 0 else heads + 2 * h
            dst = p[:, b:b + t + 1, :].rearrange("p a b -> p (a b)")

            def product(bank, t=t, h=h, n=n):
                mm = k.mm(bank, q(h)[:, t * P:(t + 1) * P], kt(h)[:, 0:n], start=True,
                          stop=product_extra is None, last=True)
                return mm if product_extra is None else product_extra(bank, t, h, n)

            jobs.append((product, n, how(t, h, n), dst))
            value_jobs.append(([p_t[:, b + a, :] for a in range(t + 1)], [v(h, a) for a in range(t + 1)],
                               factor[:, t * heads + h:t * heads + h + 1], out[:, t, h * HD:(h + 1) * HD]))
    scores = Scores(k, jobs, top, total, extra_slots=extra_slots)
    return [scores, turned_blocks(k, p, p_t, 3 * heads), Values(k, value_jobs, add)]



CMP, STRIDE, CMP_HIDDEN = 32, 16, 256


class Compress(Stage):

    def __init__(self, k, raw, hidden, keys, values, extra):
        super().__init__(k)
        self.raw, self.hidden, self.keys, self.values, self.extra = raw, hidden, keys, values, extra
        self.sp = k.slots(1)
        self.s = k.slots(8)

    def tensor(self, pe):
        k = self.k
        extra = self.extra
        pe.wait_ge(k.vector_for_tensor.sem, k.vector_for_tensor.take())
        k.slots_through()
        for kv in range(2):
            if kv == 1:
                pe.wait_ge(k.scalar_for_tensor.sem, k.scalar_for_tensor.take())
            for l in range(CMP):
                s = self.s + 4 * kv + l // 8
                if l % 8 == 0:
                    pe.wait_ge(k.slot_landed[(s) % RING], k.loads(s))
                for hc in range(2):
                    for side in range(2):
                        base = 64 * side
                        w = k.slot(s)[base:base + 64, (l % 8) * 256 + hc * P:(l % 8) * 256 + (hc + 1) * P]
                        src = self.raw[base:base + 64, 2 * kv:2 * kv + 2, l:l + STRIDE * (N_CMP - 1) + 1:STRIDE]
                        dst = k.acc[:, 2 * hc + side, 0:2 * N_CMP].rearrange("p (c n) -> p c n", n=N_CMP)
                        k.mm(dst, w, src, start=l == 0, stop=l == CMP - 1)
                    mm = k.mm(k.bank[:, hc, 0:1], k.slot(s)[0:64, (l % 8) * 256 + hc * P:(l % 8) * 256 + (hc + 1) * P],
                              extra[0:64, CMP * kv + l:CMP * kv + l + 1], start=l == 0, stop=l == CMP - 1, last=True)
                if l == CMP - 1:
                    mm.then_inc(k.banks_for_vector.sem, k.banks_for_vector.send())
                if l % 8 == 7:
                    k.slots_through()
            pe.wait_ge(k.scalar_for_tensor.sem, k.scalar_for_tensor.take())
            if kv == 0:
                for hc in range(2):
                    mm = k.mm(k.bank[:, 2, 0:NSA_GROUPS * N_CMP], extra[:, 64 + hc * P:64 + (hc + 1) * P],
                              self.hidden[:, hc, :], start=hc == 0, stop=hc == 1, last=True)
            else:
                for g in range(NSA_GROUPS):
                    for hc in range(2):
                        mm = k.mm(k.bank[0:N_CMP, 3, g * HD:(g + 1) * HD],
                                  self.hidden[:, hc, g * N_CMP:(g + 1) * N_CMP],
                                  extra[:, 320 + hc * HD:320 + (hc + 1) * HD], start=hc == 0, stop=hc == 1, last=True)
            mm.then_inc(k.banks_for_vector.sem, k.banks_for_vector.send())

    def vector(self, dve):
        k = self.k
        bias = k.small[:, 16:18]
        dve.wait_ge(k.slot_landed[(self.sp) % RING], k.loads(self.sp))
        dve.tensor_copy(self.extra, k.slot(self.sp)[:, 0:448]).then_inc(k.vector_for_tensor.sem, k.vector_for_tensor.send())
        for kv in range(2):
            dve.wait_ge(k.banks_for_vector.sem, k.banks_for_vector.take())
            dve.tensor_copy(bias, k.bank[:, 0:2, 0]).then_inc(k.vector_for_scalar.sem, k.vector_for_scalar.send())
            dve.wait_ge(k.banks_for_vector.sem, k.banks_for_vector.take())
            if kv == 0:
                dve.tensor_copy(self.keys, k.bank[:, 2, 0:NSA_GROUPS * N_CMP]).then_inc(k.dve_step, 1)
                dve.wait_ge(k.dve_step, k.step("dve"))
            else:
                dve.tensor_copy(self.values, k.bank[0:N_CMP, 3, 0:NSA_GROUPS * HD])

    def scalar(self, act):
        k = self.k
        for kv in range(2):
            act.wait_ge(k.vector_for_scalar.sem, k.vector_for_scalar.take())
            for hc in range(2):
                for side in range(2):
                    dst = self.hidden[:, hc, :].rearrange("p (c s n) -> p c s n", s=2, n=N_CMP)[:, :, side, :]
                    ins = act.activation(dst, k.acc[:, 2 * hc + side, 0:2 * N_CMP].rearrange("p (c n) -> p c n", n=N_CMP),
                                         ACT.Gelu_apprx_tanh, bias=k.small[:, 16 + hc:17 + hc])
            ins.then_inc(k.scalar_for_tensor.sem, k.scalar_for_tensor.send())
            if kv == 0:
                act.drain().then_inc(k.scalar_for_tensor.sem, k.scalar_for_tensor.send())


class Gates(Stage):

    def __init__(self, k, factor, gates, total, branch):
        super().__init__(k)
        self.factor, self.gates, self.total, self.branch = factor, gates, total, branch

    def vector(self, dve):
        g = self.gates.rearrange("p t (h b) -> p t h b", b=3)[:, :, :, self.branch]
        for t in range(TT):
            a = slice(t * NSA_HEADS, (t + 1) * NSA_HEADS)
            dve.tensor_tensor(self.factor[:, a], g[:, t, :], self.total[:, a], ALU.mult)



FOX_HEADS = 16


class HeadNorm(Stage):

    def __init__(self, k, qk, squares):
        super().__init__(k)
        self.qk, self.squares = qk, squares
        self.s = k.slots(1)
        self.n = 2 * FOX_HEADS

    def scalar(self, act):
        take_root(self.k, act, self.k.small[:, 16:16 + TT * self.n])

    def tensor(self, pe):
        pe.wait_ge(self.k.vector_for_tensor.sem, self.k.vector_for_tensor.take())
        self.k.slots_through()

    def vector(self, dve):
        k, n = self.k, self.n
        stat = k.small[:, 16:16 + TT * n]
        for t in range(TT):
            ins = dve.tensor_tensor(self.squares[:, t, :], self.qk[:, t, :], self.qk[:, t, :], ALU.mult)
        ins.then_inc(k.dve_step, 1)
        dve.wait_ge(k.dve_step, k.step("dve"))
        dve.tensor_reduce(stat, self.squares.rearrange("p t (h d) -> p (t h) d", d=HD), AX, ALU.add).then_inc(k.dve_step, 1)
        dve.wait_ge(k.dve_step, k.step("dve"))
        inverse_root(k, dve, dve.tensor_scalar(stat, stat, 1.0 / HD, EPS, ALU.mult, ALU.add), stat)
        for t in range(TT):
            ins = dve.tensor_scalar(stat[:, t * n:t * n + n // 2], stat[:, t * n:t * n + n // 2], HD ** -0.5, None,
                                    ALU.mult)
        ins.then_inc(k.dve_step, 1)
        dve.wait_ge(k.dve_step, k.step("dve"))
        dve.wait_ge(k.slot_landed[(self.s) % RING], k.loads(self.s))
        for t in range(TT):
            heads = self.qk[:, t, :].rearrange("p (h d) -> p h d", d=HD)
            ins = dve.tensor_tensor(heads, heads, stat[:, t * n:(t + 1) * n].unsqueeze(2).to_broadcast([P, n, HD]),
                                    ALU.mult)
        ins.then_inc(k.dve_step, 1)
        dve.wait_ge(k.dve_step, k.step("dve"))
        for t in range(TT):
            ins = dve.tensor_tensor(self.qk[:, t, :], self.qk[:, t, :], k.slot(self.s)[:, 0:SLOT], ALU.mult)
        ins.then_inc(k.vector_for_tensor.sem, k.vector_for_tensor.send())


def log_sigmoid(k, act, z, b):
    act.wait_ge(k.vector_for_scalar.sem, k.vector_for_scalar.take())
    act.activation(b, z, ACT.Abs).then_inc(k.act_step, 1)
    act.wait_ge(k.act_step, k.step("act"))
    act.activation(b, b, ACT.Exp, scale=-1.0).then_inc(k.act_step, 1)
    act.wait_ge(k.act_step, k.step("act"))
    act.activation(b, b, ACT.Ln, bias=1.0).then_inc(k.scalar_for_vector.sem, k.scalar_for_vector.send())


class ForgetGates(Stage):

    def __init__(self, k, z, lf, tmp, c, c_t):
        super().__init__(k)
        self.z, self.lf, self.tmp, self.c, self.c_t = z, lf, tmp, c, c_t
        self.s = k.slots(1)

    def scalar(self, act):
        log_sigmoid(self.k, act, self.z, self.tmp)

    def vector(self, dve):
        k, H = self.k, FOX_HEADS
        dve.wait_ge(k.slot_landed[(self.s) % RING], k.loads(self.s))
        for t in range(TT):
            ins = dve.tensor_tensor(self.z[:, t, :], self.z[:, t, :], k.slot(self.s)[:, 0:H], ALU.add)
        ins.then_inc(k.vector_for_scalar.sem, k.vector_for_scalar.send())
        dve.wait_ge(k.scalar_for_vector.sem, k.scalar_for_vector.take())
        dve.scalar_tensor_tensor(self.lf, self.z, 0.0, self.tmp, ALU.min, ALU.subtract).then_inc(k.vector_for_tensor.sem, k.vector_for_tensor.send())
        dve.wait_ge(k.banks_for_vector.sem, k.banks_for_vector.take())
        dve.tensor_copy(self.c, k.bank[:, 0, 0:TT * H].rearrange("p (t h) -> p t h", t=TT))
        dve.tensor_copy(self.c_t, k.bank[0:H, 1, 0:S])

    def tensor(self, pe):
        k, H = self.k, FOX_HEADS
        pe.wait_ge(k.vector_for_tensor.sem, k.vector_for_tensor.take())
        tri = k.c("causal_t").rearrange("p (t q) -> p t q", t=TT)
        for t in range(TT):
            for a in range(t + 1):
                k.mm(k.bank[:, 0, t * H:(t + 1) * H], tri[:, a, t * P:(t + 1) * P], self.lf[:, a, :],
                     start=a == 0, stop=a == t, last=True)
        for a in range(TT):
            mm = k.mm(k.bank[0:H, 1, 0:S], self.lf[:, a, :], tri[:, a, :], start=a == 0, stop=a == TT - 1, last=True)
        mm.then_inc(k.banks_for_vector.sem, k.banks_for_vector.send())
        k.slots_through()


def pick_head():
    out = np.zeros((FOX_HEADS, FOX_HEADS, P), np.float32)
    for h in range(FOX_HEADS):
        out[h, h] = -1.0
    return out.reshape(FOX_HEADS, -1)


class Keep(Stage):

    def __init__(self, k, dst):
        super().__init__(k)
        self.dst = dst
        self.n = -(-dst.shape[1] // SLOT)
        self.s = k.slots(self.n)

    def vector(self, dve):
        k = self.k
        for j in range(self.n):
            dve.wait_ge(k.slot_landed[(self.s + j) % RING], k.loads(self.s + j))
            end = min((j + 1) * SLOT, self.dst.shape[1])
            dve.tensor_copy(self.dst[:, j * SLOT:end], k.slot(self.s + j)[:, 0:end - j * SLOT]).then_inc(k.vector_for_tensor.sem, k.vector_for_tensor.send())

    def tensor(self, pe):
        k = self.k
        for j in range(self.n):
            pe.wait_ge(k.vector_for_tensor.sem, k.vector_for_tensor.take())
        k.slots_through(self.n)



CONV, TAPS, PAD = 512, 31, 30
GLA_HEADS, GLA_DV = 4, 128
SUB = 16
N_SUB = S // SUB
CLAMP = 70.0


class Convolve(Stage):

    def __init__(self, k, feat, u, y, w, b):
        super().__init__(k)
        self.feat, self.u, self.y, self.w, self.b = feat, u, y, w, b

    def scalar(self, act):
        gate = self.feat[:, 4:8, :]
        act.activation(gate, gate, ACT.Sigmoid).then_inc(self.k.scalar_for_vector.sem, self.k.scalar_for_vector.send())

    def vector(self, dve):
        k = self.k
        dve.memset(self.u[:, :, 0:PAD], 0.0)
        dve.wait_ge(k.scalar_for_vector.sem, k.scalar_for_vector.take())
        dve.tensor_tensor(self.u[:, :, PAD:], self.feat[:, 0:4, :], self.feat[:, 4:8, :], ALU.mult).then_inc(k.dve_step, 1)
        dve.wait_ge(k.dve_step, k.step("dve"))
        n = CONV // P
        for tap in range(TAPS):
            for c in range(n):
                src, w = self.u[:, c, tap:tap + S], self.w[:, c * TAPS + tap:c * TAPS + tap + 1]
                if tap == 0:
                    ins = dve.tensor_scalar(self.y[:, c, :], src, w, self.b[:, c:c + 1], ALU.mult, ALU.add)
                else:
                    dve.wait_ge(k.dve_step, k.steps["dve"] - n + 1)
                    ins = dve.scalar_tensor_tensor(self.y[:, c, :], src, w, self.y[:, c, :], ALU.mult, ALU.add)
                ins.then_inc(k.dve_step, 1)
                k.steps["dve"] += 1


class ConvNorm(Stage):

    def __init__(self, k, y, out, g, b):
        super().__init__(k)
        self.y, self.out, self.g, self.b = y, out, g, b

    def scalar(self, act):
        k = self.k
        take_root(k, act, k.small[:, 80:82])
        act.wait_ge(k.vector_for_scalar.sem, k.vector_for_scalar.take())
        for t in range(TT):
            act.activation(self.out[:, t, :], self.y[:, t, :], ACT.Silu)

    def vector(self, dve):
        k = self.k
        layer_norm(k, dve, self.y, self.g, self.b)
        dve.drain().then_inc(k.vector_for_scalar.sem, k.vector_for_scalar.send())


def layer_norm(k, dve, y, g, b):
    moments(k, dve, [y[:, t, :] for t in range(TT)], k.small[:, 16:28], k.small[:, 64:68], k.small[:, 80:82], EPS)
    for t in range(TT):
        ins = dve.tensor_scalar(y[:, t, :], y[:, t, :], k.small[:, 64 + 2 * t:65 + 2 * t],
                                k.small[:, 80 + t:81 + t], ALU.subtract, ALU.mult)
    ins.then_inc(k.dve_step, 1)
    dve.wait_ge(k.dve_step, k.step("dve"))
    for op, row in ((ALU.mult, g), (ALU.add, b)):
        for t in range(TT):
            ins = dve.tensor_tensor(y[:, t, :], y[:, t, :], row, op)
        ins.then_inc(k.dve_step, 1)
        dve.wait_ge(k.dve_step, k.step("dve"))


class GlaDecays(Stage):

    def __init__(self, k, w_low, w2, bias, low, z, tmp, b_t):
        super().__init__(k)
        self.w_low, self.w2, self.bias, self.low, self.z, self.tmp, self.b_t = w_low, w2, bias, low, z, tmp, b_t

    def tensor(self, pe):
        k = self.k
        for kk in range(DC):
            mm = k.mm(k.bank[0:16, 0, 0:S], self.w_low[:, kk * 16:(kk + 1) * 16], k.h_t[:, kk, :], start=kk == 0,
                      stop=kk == DC - 1, last=True)
        mm.then_inc(k.banks_for_vector.sem, k.banks_for_vector.send())
        pe.wait_ge(k.vector_for_tensor.sem, k.vector_for_tensor.take())
        for t in range(TT):
            mm = k.mm(k.bank[:, 1, t * S:(t + 1) * S], self.low[:, t * P:(t + 1) * P], self.w2, start=True,
                      stop=True, last=True)
        mm.then_inc(k.banks_for_vector.sem, k.banks_for_vector.send())
        pe.wait_ge(k.vector_for_tensor.sem, k.vector_for_tensor.take())
        tri = k.c("causal_t").rearrange("p (t q) -> p t q", t=TT)
        for hp in range(2):
            for a in range(TT):
                mm = k.mm(k.bank[:, 2, hp * S:(hp + 1) * S], self.z[:, a, hp * P:(hp + 1) * P], tri[:, a, :],
                          start=a == 0, stop=a == TT - 1, last=True)
        mm.then_inc(k.banks_for_vector.sem, k.banks_for_vector.send())

    def scalar(self, act):
        log_sigmoid(self.k, act, self.z, self.tmp)

    def vector(self, dve):
        k = self.k
        dve.wait_ge(k.banks_for_vector.sem, k.banks_for_vector.take())
        dve.tensor_copy(self.low, k.bank[0:16, 0, 0:S]).then_inc(k.vector_for_tensor.sem, k.vector_for_tensor.send())
        dve.wait_ge(k.banks_for_vector.sem, k.banks_for_vector.take())
        for t in range(TT):
            ins = dve.tensor_tensor(self.z[:, t, :], k.bank[:, 1, t * S:(t + 1) * S], self.bias, ALU.add)
        ins.then_inc(k.vector_for_scalar.sem, k.vector_for_scalar.send())
        dve.wait_ge(k.scalar_for_vector.sem, k.scalar_for_vector.take())
        dve.scalar_tensor_tensor(self.z, self.z, 0.0, self.tmp, ALU.min, ALU.subtract).then_inc(k.dve_step, 1)
        dve.wait_ge(k.dve_step, k.step("dve"))
        dve.tensor_scalar(self.z, self.z, 1.0 / 16.0, None, ALU.mult).then_inc(k.vector_for_tensor.sem, k.vector_for_tensor.send())
        dve.wait_ge(k.banks_for_vector.sem, k.banks_for_vector.take())
        dve.tensor_copy(self.b_t, k.bank[:, 2, :].rearrange("p (a b) -> p a b", a=2))


class GlaScale(Stage):

    def __init__(self, k, q_t, k_t, b_t, ref, q_s, k_a, k_b):
        super().__init__(k)
        self.q_t, self.k_t, self.b_t, self.ref, self.q_s, self.k_a, self.k_b = q_t, k_t, b_t, ref, q_s, k_a, k_b

    def scalar(self, act):
        k = self.k
        act.wait_ge(k.vector_for_scalar.sem, k.vector_for_scalar.take())
        act.activation(self.q_s, self.q_s, ACT.Exp).then_inc(k.scalar_for_vector.sem, k.scalar_for_vector.send())
        for hp in range(2):
            for dst in (self.k_a, self.k_b):
                act.wait_ge(k.vector_for_scalar.sem, k.vector_for_scalar.take())
                act.activation(dst[:, hp], dst[:, hp], ACT.Exp).then_inc(k.scalar_for_vector.sem, k.scalar_for_vector.send())

    def vector(self, dve):
        k = self.k
        dve.memset(self.ref[:, :, 0:1], 0.0)
        dve.tensor_copy(self.ref[:, :, 1:N_SUB], self.b_t[:, :, SUB - 1:S - 1:SUB]).then_inc(k.dve_step, 1)
        dve.wait_ge(k.dve_step, k.step("dve"))
        cut = lambda b: b.rearrange("p a (n i) -> p a n i", i=SUB)
        dve.tensor_tensor(cut(self.q_s), cut(self.b_t),
                                            self.ref.unsqueeze(3).to_broadcast([P, 2, N_SUB, SUB]), ALU.subtract).then_inc(k.vector_for_scalar.sem, k.vector_for_scalar.send())
        parts = [(hp, dst, kt) for hp in range(2) for dst, kt in ((self.k_a, 0), (self.k_b, 1))]
        for hp, dst, kt in parts:
            blocks = slice(kt * N_SUB // 2, N_SUB)
            n = [P, N_SUB - kt * N_SUB // 2, P]
            dve.tensor_tensor(dst[:, hp], self.ref[:, hp, blocks].unsqueeze(2).to_broadcast(n),
                                         self.b_t[:, hp, kt * P:(kt + 1) * P].unsqueeze(1).to_broadcast(n),
                                         ALU.subtract).then_inc(k.dve_step, 1)
            dve.wait_ge(k.dve_step, k.step("dve"))
            dve.tensor_scalar(dst[:, hp], dst[:, hp], CLAMP, None, ALU.min).then_inc(k.vector_for_scalar.sem, k.vector_for_scalar.send())
        dve.wait_ge(k.scalar_for_vector.sem, k.scalar_for_vector.take())
        dve.scalar_tensor_tensor(self.q_s, self.q_t, HD ** -0.5, self.q_s, ALU.mult, ALU.mult)
        for hp, dst, kt in parts:
            n = [P, N_SUB - kt * N_SUB // 2, P]
            dve.wait_ge(k.scalar_for_vector.sem, k.scalar_for_vector.take())
            dve.tensor_tensor(dst[:, hp], dst[:, hp], self.k_t[:, hp, kt * P:(kt + 1) * P].unsqueeze(1).to_broadcast(n),
                              ALU.mult)


class GlaAttend(Stage):

    def __init__(self, k, q_s, k_a, k_b, w, v, o):
        super().__init__(k)
        self.q_s, self.k_a, self.k_b, self.w, self.v, self.o = q_s, k_a, k_b, w, v, o

    def tensor(self, pe):
        k = self.k
        for h in range(GLA_HEADS):
            base, hp = 64 * (h % 2), h // 2
            for b in range(N_SUB):
                for kt in range(1 + b // (N_SUB // 2)):
                    key = self.k_a[base:base + 64, hp, b, :] if kt == 0 else self.k_b[base:base + 64, hp, b - N_SUB // 2, :]
                    mm = k.mm(k.bank[:, h, kt * S + b * SUB:kt * S + (b + 1) * SUB], key,
                              self.q_s[base:base + 64, hp, b * SUB:(b + 1) * SUB], start=True, stop=True, last=True)
            mm.then_inc(k.banks_for_vector.sem, k.banks_for_vector.send())
        for t in range(TT):
            for h in range(GLA_HEADS):
                if t == 0:
                    pe.wait_ge(k.vector_for_tensor.sem, k.vector_for_tensor.take())
                for a in range(t + 1):
                    mm = k.mm(k.acc[:, t, h * GLA_DV:(h + 1) * GLA_DV], self.w[:, h, a, t * P:(t + 1) * P],
                              self.v[:, a, h * GLA_DV:(h + 1) * GLA_DV], start=a == 0, stop=a == t, last=True)
            mm.then_inc(k.banks_for_scalar.sem, k.banks_for_scalar.send())

    def vector(self, dve):
        k = self.k
        tri = k.c("causal_t").rearrange("p (t q) -> p t q", t=TT)
        for h in range(GLA_HEADS):
            dve.wait_ge(k.banks_for_vector.sem, k.banks_for_vector.take())
            bank = k.bank[:, h, :].rearrange("p (a q) -> p a q", a=TT)
            dve.tensor_tensor(self.w[:, h, 0, :], bank[:, 0, :], tri[:, 0, :], ALU.mult)
            dve.tensor_tensor(self.w[:, h, 1, P:], bank[:, 1, P:], tri[:, 1, P:], ALU.mult).then_inc(k.vector_for_tensor.sem, k.vector_for_tensor.send())

    def scalar(self, act):
        k = self.k
        for t in range(TT):
            act.wait_ge(k.banks_for_scalar.sem, k.banks_for_scalar.take())
            act.activation(self.o[:, t, :], k.acc[:, t, :], ACT.Copy)


class HeadRms(Stage):

    def __init__(self, k, src, out, n, gain, other, squares):
        super().__init__(k)
        self.src, self.out, self.n, self.gain, self.other, self.squares = src, out, n, gain, other, squares
        self.groups = src[0].shape[1] // n

    def scalar(self, act):
        take_root(self.k, act, self.k.small[:, 16:16 + TT * self.groups])

    def vector(self, dve):
        k, G, n = self.k, self.groups, self.n
        stat = k.small[:, 16:16 + TT * G]
        for t in range(TT):
            ins = dve.tensor_tensor(self.squares[t], self.src[t], self.src[t], ALU.mult)
        ins.then_inc(k.dve_step, 1)
        dve.wait_ge(k.dve_step, k.step("dve"))
        for t in range(TT):
            ins = dve.tensor_reduce(stat[:, t * G:(t + 1) * G], self.squares[t].rearrange("p (g n) -> p g n", n=n),
                                    AX, ALU.add)
        ins.then_inc(k.dve_step, 1)
        dve.wait_ge(k.dve_step, k.step("dve"))
        inverse_root(k, dve, dve.tensor_scalar(stat, stat, 1.0 / n, EPS, ALU.mult, ALU.add), stat)
        for t in range(TT):
            for g in range(G):
                a = slice(g * n, (g + 1) * n)
                ins = dve.scalar_tensor_tensor(self.out[t][:, a], self.src[t][:, a], stat[:, t * G + g:t * G + g + 1],
                                               self.gain[:, a], ALU.mult, ALU.mult)
        ins.then_inc(k.dve_step, 1)
        dve.wait_ge(k.dve_step, k.step("dve"))
        if self.other is not None:
            for t in range(TT):
                dve.tensor_tensor(self.out[t], self.out[t], self.other[:, t, :], ALU.mult)



ROPE_HEADS = 8


class Rope(Stage):

    def __init__(self, k, qk, tmp):
        super().__init__(k)
        self.qk, self.tmp = qk, tmp

    def vector(self, dve):
        k, n, half = self.k, 2 * ROPE_HEADS, HD // 2
        shape = [P, n, half]
        for t in range(TT):
            x = self.qk[:, t, :].rearrange("p (h s d) -> p h s d", s=2, d=half)
            cos = k.c("cos")[:, t * half:(t + 1) * half].unsqueeze(1).to_broadcast(shape)
            sin = k.c("sin")[:, t * half:(t + 1) * half].unsqueeze(1).to_broadcast(shape)
            a, b = (self.tmp[:, t, i * n * half:(i + 1) * n * half].rearrange("p (h d) -> p h d", d=half)
                    for i in range(2))
            dve.tensor_tensor(a, x[:, :, 1, :], sin, ALU.mult)
            dve.tensor_tensor(b, x[:, :, 0, :], sin, ALU.mult).then_inc(k.dve_step, 1)
            dve.wait_ge(k.dve_step, k.step("dve"))
            dve.tensor_tensor(x[:, :, 0, :], x[:, :, 0, :], cos, ALU.mult)
            dve.tensor_tensor(x[:, :, 1, :], x[:, :, 1, :], cos, ALU.mult).then_inc(k.dve_step, 1)
            dve.wait_ge(k.dve_step, k.step("dve"))
            dve.tensor_tensor(x[:, :, 0, :], x[:, :, 0, :], a, ALU.subtract)
            dve.tensor_tensor(x[:, :, 1, :], x[:, :, 1, :], b, ALU.add)


class Spatial(Stage):

    def __init__(self, k, u, v, w, b, g, beta, out):
        super().__init__(k)
        self.u, self.v, self.w, self.b, self.g, self.beta, self.out = u, v, w, b, g, beta, out

    def scalar(self, act):
        take_root(self.k, act, self.k.small[:, 80:82])

    def vector(self, dve):
        k = self.k
        layer_norm(k, dve, self.v, self.g, self.beta)
        dve.tensor_tensor(self.w, self.w, k.c("causal_t")[:, 0:P].unsqueeze(1).to_broadcast(
            [P, ROPE_HEADS, P]), ALU.mult).then_inc(k.vector_for_tensor.sem, k.vector_for_tensor.send())
        for t in range(TT):
            dve.wait_ge(k.banks_for_vector.sem, k.banks_for_vector.take())
            for h in range(ROPE_HEADS):
                a = slice(h * HD, (h + 1) * HD)
                dve.scalar_tensor_tensor(self.out[:, t, a], k.bank[:, t, a], self.b[:, h:h + 1], self.u[:, t, a],
                                         ALU.add, ALU.mult)

    def tensor(self, pe):
        k = self.k
        pe.wait_ge(k.vector_for_tensor.sem, k.vector_for_tensor.take())
        for t in range(TT):
            for h in range(ROPE_HEADS):
                mm = k.mm(k.bank[:, t, h * HD:(h + 1) * HD], self.w[:, h, :], self.v[:, t, h * HD:(h + 1) * HD],
                          start=True, stop=True, last=True)
            mm.then_inc(k.banks_for_vector.sem, k.banks_for_vector.send())



def rows(*vectors):
    v = np.concatenate([np.asarray(a, np.float32).ravel() for a in vectors])
    n = -(-v.size // SLOT)
    out = np.zeros((n, P, SLOT), np.float32)
    for i in range(n):
        piece = v[i * SLOT:(i + 1) * SLOT]
        out[i, :, :piece.size] = piece[None, :]
    return out


def params(*blocks):
    out = np.zeros((1, P, SLOT), np.float32)
    at = 0
    for b in blocks:
        out[0, :b.shape[0], at:at + b.shape[1]] = b
        at += b.shape[1]
    return out


def by_columns(w):
    K, N = w.shape
    if N <= 256:
        return params(w.reshape(DC, P, N).transpose(1, 0, 2).reshape(P, DC * N))
    a = w.reshape(K // (4 * P), 4, P, N // 512, 512)
    return a.transpose(3, 0, 2, 1, 4).reshape(-1, P, SLOT)


def by_features(w):
    K, N = w.shape
    a = w.reshape(DC, P, N // (2 * P), 2, P)
    return a.transpose(2, 1, 3, 0, 4).reshape(-1, P, SLOT)


def gated_pair(w, n):
    a = w.reshape(DC, P, 2, n // P, P)
    return a.transpose(3, 1, 2, 0, 4).reshape(-1, P, SLOT)


def by_rows(w):
    K, N = w.shape
    return w.reshape(K // (2 * P), 2, P, N).transpose(0, 2, 1, 3).reshape(-1, P, SLOT)


def columns(v):
    return np.asarray(v).reshape(-1, P).T



def modulated(w, b, part):
    cols = slice(part * 3 * D, (part + 1) * 3 * D)
    return [by_columns(w[:, cols]), rows(b[cols])]


def first_ffn(k, i, j, I=None):
    if I is not None:
        return modulated(I["ada_w"][i], I["ada_b"][i], 2 * j) + [
            gated_pair(I["ffn_w_in"][i, j], D_FF), by_rows(I["ffn_w_out"][i, j]),
            rows(I["ln_g"][i, 2 * j], I["ln_b"][i, 2 * j])]
    f = [Modulation(k, 0.5, True), Pre(k, False, True), ToFeatures(k, k.h_tok, k.h_t, DC), FfnIn(k)]
    return f + [OutProj(k, f[-1].hidden, FC), Post(k, True, True)]


def retention(k, I=None):
    n_qk, n_v = RET_HEADS * RET_QK, RET_HEADS * RET_V
    if I is not None:
        w = I["ret_w_in"][0]
        return modulated(I["ada_w"][0], I["ada_b"][0], 1) + [
            by_features(w[:, :2 * n_qk]), by_columns(w[:, 2 * n_qk:]), params(ret_decay()),
            by_rows(I["ret_w_out"][0]), rows(I["ln_g"][0, 1], I["ln_b"][0, 1])]
    room = Room(k)
    qk = room(2 * DC, S)
    v, g, w = room(TT, n_v), room(TT, n_v), room(RET_HEADS, 2 * S)
    o = room(TT, n_v)
    out = [Modulation(k, 1.0, True), Pre(k, False, True), ToFeatures(k, k.h_tok, k.h_t, DC),
           ToFeatureRows(k, qk, 2 * DC),
           ToTokens(k, [(512, v[:, :, b * 512:(b + 1) * 512], None) for b in range(n_v // 512)]
                    + [(512, g[:, :, b * 512:(b + 1) * 512], ACT.Silu) for b in range(n_v // 512)]),
           RetScores(k, qk[:, 0:DC, :], qk[:, DC:, :], w), RetOut(k, w, v, g, o),
           ToFeatures(k, g, qk, n_v // P)]
    return out + [OutProj(k, qk, n_v // P), Post(k, True, True)]


def peer(k, layer, I=None):
    if I is not None:
        keys = I["peer_keys_2"][layer].reshape(2 * PEER_HEADS, N_KEYS, P)
        u, v = I["peer_u_2"][layer], I["peer_v_2"][layer]
        n = u.shape[0] // P
        experts = np.concatenate([u.reshape(n, P, DC, P).transpose(0, 3, 2, 1).reshape(n, P, D),
                                  v.reshape(n, P, D)], axis=2)
        return [rows(I["ffn_norm_2"][layer]), by_features(I["peer_wq_2"][layer]),
                params(keys.transpose(2, 0, 1).reshape(P, -1)), experts]
    room = Room(k)
    gates = room(HALF, S)
    pairs, hot1, hot2 = room(3, S), room(HOT_RING, HALF), room(HOT_RING, P)
    act_out, gated = room(2, S), room(2, S)
    early = Room(k)
    q_t, scores = early(2 * PEER_HEADS, S), early(TT, 2 * PEER_HEADS * N_KEYS)
    found = hot2.rearrange("p a b -> p (a b)")[:, 0:3 * TT * PAIRS].rearrange("p (a b) -> p a b", a=3)
    blocks = [(found[:, a, t * PAIRS:(t + 1) * PAIRS], pairs[:, a, t * P:(t + 1) * P])
              for a in range(3) for t in range(TT)]
    out = [Pre(k, True, False), ToFeatures(k, k.h_tok, k.h_t, DC), ToFeatureRows(k, q_t, 2 * PEER_HEADS),
           KeyScores(k, q_t, scores), Route(k, scores, early, found),
           Turn(k, [([src], dst.unsqueeze(1)) for src, dst in blocks])]
    for half in range(2):
        out += [SpreadGates(k, half, pairs, gates, hot1, hot2), Experts(k, half, gates, act_out, gated)]
    return out + [Post(k, False, False)]


def fox(k, I=None):
    if I is not None:
        w = I["od_w_in_2"][0]
        gains = np.concatenate([np.tile(I["od_q_norm_g_2"][0], FOX_HEADS), np.tile(I["od_k_norm_g_2"][0], FOX_HEADS)])
        return [rows(I["od_norm_mix_2"][0]), by_columns(w[:, :3 * D]), by_columns(w[:, 3 * D:]), rows(gains),
                rows(I["od_fgate_b_2"][0]), params(pick_head()), by_rows(I["od_w_out_2"][0])]
    room = Room(k)
    qk, v, qk_t = room(TT, 2 * D), room(TT, D), room(2 * DC, S)
    p = room(3 * FOX_HEADS, P)
    z, lf, tmp = (room(TT, FOX_HEADS) for _ in range(3))
    c, c_t = room(TT, FOX_HEADS), room(S)
    top, total = room(TT * FOX_HEADS), room(TT * FOX_HEADS)
    p_t = room(3 * FOX_HEADS, P)
    squares = p_t.rearrange("p a b -> p (a b)")[:, 0:4 * D].rearrange("p (t n) -> p t n", t=TT)
    mask = k.c("mask").rearrange("p (t q) -> p t q", t=TT)
    norm, gates = HeadNorm, ForgetGates
    out = [Pre(k, True, False), ToFeatures(k, k.h_tok, k.h_t, DC),
           ToTokens(k, [(512, qk[:, :, b * 512:(b + 1) * 512], None) for b in range(4)]
                    + [(512, v[:, :, b * 512:(b + 1) * 512], None) for b in range(2)]
                    + [(FOX_HEADS, z, None)]),
           HeadNorm(k, qk, squares), ForgetGates(k, z, lf, tmp, c, c_t[0:FOX_HEADS, :]),
           ToFeatures(k, qk, qk_t, 2 * DC)]
    where = [0]
    side = lambda first: lambda h: qk_t[64 * (h % 2):64 * (h % 2) + 64, first + h // 2, :]

    def minus_key(bank, t, h, n):
        return k.mm(bank, k.slot(where[0])[0:FOX_HEADS, h * P:(h + 1) * P], c_t[0:FOX_HEADS, 0:n], start=False,
                    stop=True, last=True)

    def how(t, h, n):
        return lambda dve, dst, bank: dve.scalar_tensor_tensor(dst, bank, c[:, t, h:h + 1], mask[:, t, 0:n],
                                                               ALU.add, ALU.add)

    att = causal_attention(k, FOX_HEADS, side(0), side(DC), lambda h, a: v[:, a, h * HD:(h + 1) * HD],
                           minus_key, how, p, p_t, top, total, total, k.h_tok, False, extra_slots=1)
    where[0] = att[0].s
    return out + att + [ToFeatures(k, k.h_tok, k.h_t, DC), OutProj(k, k.h_t, DC), Post(k, False, False)]


def nsa(k, I=None):
    kv = NSA_GROUPS * HD
    if I is not None:
        w = I["nsa_w_in"][0]
        part = [w[:, D + j * kv:D + (j + 1) * kv] for j in range(6)]
        twice = lambda a: np.repeat(a.reshape(D, NSA_GROUPS, 1, HD), 2, axis=2).reshape(D, 2 * kv)
        first = lambda a: np.tile(a.reshape(4, 8, HD, CMP_HIDDEN).transpose(0, 2, 1, 3).reshape(4, HD, SLOT), (1, 2, 1))
        pe = [np.tile(I[n][0].T, (2, 1)) for n in ("nsa_pe_k", "nsa_pe_v")]
        second = lambda a, n: np.tile(a.reshape(2, P, 1, HD), (1, 1, n, 1)).transpose(1, 0, 2, 3).reshape(P, -1)
        return modulated(I["ada_w"][1], I["ada_b"][1], 1) + [
            by_features(np.concatenate([w[:, :D], part[0], part[1], twice(part[2]), twice(part[4])], axis=1)),
            by_columns(np.concatenate([part[3], part[5]], axis=1)), by_columns(w[:, D + 6 * kv:]),
            params(pe[0], pe[1], second(I["nsa_ck_w2"][0], 2), second(I["nsa_cv_w2"][0], 1)),
            first(I["nsa_ck_w1"][0]), first(I["nsa_cv_w1"][0]), by_rows(I["nsa_w_out"][0]),
            rows(I["ln_g"][1, 1], I["ln_b"][1, 1])]
    room = Room(k)
    H = NSA_HEADS
    feat, v, gates = room(20, S), room(TT, 2 * kv), room(TT, 3 * H)
    p, p_t = room(3 * H, P), room(3 * H, P)
    hidden, ck, cv = room(2, NSA_GROUPS * N_CMP), room(NSA_GROUPS * N_CMP), room(kv)
    top, total, factor = room(TT * H), room(TT * H), room(TT * H)
    q = lambda h: feat[64 * (h % 2):64 * (h % 2) + 64, h // 2, :]
    slope = lambda h: float(2.0 ** (-8.0 * (h + 1) / H))
    dist = k.c("dist").rearrange("p (t q) -> p t q", t=TT)
    cmp_dist = k.c("cmp_dist").rearrange("p (t q) -> p t q", t=TT)
    cmp_mask = k.c("cmp_mask").rearrange("p (t q) -> p t q", t=TT)

    def alibi(d):
        return lambda t, h, n: lambda dve, dst, bank: dve.scalar_tensor_tensor(
            dst, d[:, t, 0:n], -slope(h), bank, ALU.mult, ALU.add)

    out = [Modulation(k, 1.0, True), Pre(k, False, True), ToFeatures(k, k.h_tok, k.h_t, DC),
           ToFeatureRows(k, feat, 20, scaled=DC, scale=HD ** -0.5),
           ToTokens(k, [(2 * kv, v, None), (3 * H, gates, ACT.Sigmoid)]),
           Compress(k, feat[:, DC:DC + 4, :], hidden, ck, cv[0:N_CMP, :], room(448))]
    jobs = [(t, h) for t in range(TT) for h in range(H)]

    def cmp_product(t, h):
        g, base = h // 4, 64 * (h % 2)
        return lambda bank: k.mm(bank, q(h)[:, t * P:(t + 1) * P], ck[base:base + 64, g * N_CMP:(g + 1) * N_CMP],
                                 start=True, stop=True, last=True)

    small = p[:, 0:4, :].rearrange("p a b -> p (a b)")[:, 0:2 * H * N_CMP].rearrange("p (j n) -> p j n", n=N_CMP)
    out.append(Scores(k, [(cmp_product(t, h), N_CMP, alibi(cmp_dist)(t, h, N_CMP), small[:, i, :])
                          for i, (t, h) in enumerate(jobs)], top, total, keep=lambda i: cmp_mask[:, jobs[i][0], :]))
    out.append(Gates(k, factor, gates, total, 0))
    out.append(Turn(k, [([small[:, i + j, :] for j in range(4)], p_t[0:N_CMP, i:i + 4, :]) for i in range(0, 2 * H, 4)]))
    out.append(Values(k, [([p_t[0:N_CMP, i, :]], [cv[0:N_CMP, h // 4 * HD:(h // 4 + 1) * HD]], factor[:, i:i + 1],
                           k.h_tok[:, t, h * HD:(h + 1) * HD]) for i, (t, h) in enumerate(jobs)], False))
    for branch in (1, 2):
        first = DC + 4 + 4 * (branch - 1)
        kt = lambda h, first=first: feat[64 * (h % 2):64 * (h % 2) + 64, first + h // 4, :]
        val = lambda h, a, b=branch: v[:, a, (b - 1) * kv + h // 4 * HD:(b - 1) * kv + (h // 4 + 1) * HD]
        att = causal_attention(k, H, q, kt, val, None, alibi(dist), p, p_t, top, total, factor, k.h_tok, True)
        out += [att[0], Gates(k, factor, gates, total, branch), att[1], att[2]]
    return out + [ToFeatures(k, k.h_tok, k.h_t, DC), OutProj(k, k.h_t, DC), Post(k, True, True)]


def even(k, I=None):
    cuts = np.cumsum([CONV, CONV, 256, 256, 512, 512])
    if I is not None:
        w = I["ev_w_in_2"][0]
        taps = I["ev_conv_w_2"][0].reshape(TAPS, CONV // P, P).transpose(2, 1, 0).reshape(P, -1)
        return [rows(I["ev_norm_mix_2"][0]),
                params(taps, columns(I["ev_conv_b_2"][0]), I["ev_gate_w2_2"][0], by_columns(w[:, cuts[5]:])[0, :, 0:P]),
                rows(I["ev_gate_b_2"][0], np.tile(I["ev_gla_norm_g_2"][0], GLA_HEADS), I["ev_conv_ln_g_2"][0],
                     I["ev_conv_ln_b_2"][0]),
                by_features(w[:, :cuts[3]]), by_columns(w[:, cuts[3]:cuts[5]]), by_rows(I["ev_w_out_2"][0])]
    room = Room(k)
    n_tap = CONV // P * TAPS
    extra, norms = room(n_tap + 4 + S + P), room(S + 3 * 512)
    feat, v, r = room(12, S), room(TT, 512), room(TT, 512)
    u, y, y_tok = room(4, PAD + S), room(4, S), room(TT, 512)
    low, z, b_t, ref, q_s = room(S)[0:16, :], room(TT, S), room(2, S), room(2, N_SUB), room(2, S)
    k_a, k_b = room(2, N_SUB * P), room(2, N_SUB // 2 * P)
    k_a, k_b = (b.rearrange("p a (n s) -> p a n s", s=P) for b in (k_a, k_b))
    w, o = room(GLA_HEADS, TT * S), room(TT, 512)
    w = w.rearrange("p h (a q) -> p h a q", a=TT)
    tmp = o.rearrange("p a b -> p (a b)")[:, 0:TT * S].rearrange("p (a b) -> p a b", a=TT)
    second = [k.h_tok[:, t, 512:] for t in range(TT)]
    return [Pre(k, True, False), ToFeatures(k, k.h_tok, k.h_t, DC), Keep(k, extra), Keep(k, norms),
            ToFeatureRows(k, feat, 12),
            ToTokens(k, [(512, v, None), (512, r, ACT.Silu)]),
            Convolve(k, feat, u, y, extra, extra[:, n_tap:n_tap + 4]),
            Turn(k, [([y[:, c, t * P:(t + 1) * P] for c in range(4)],
                      y_tok[:, t, :].rearrange("p (c q) -> p c q", q=P)) for t in range(TT)]),
            ConvNorm(k, y_tok, k.h_tok[:, :, 0:512], norms[:, S + 512:S + 1024], norms[:, S + 1024:]),
            GlaDecays(k, extra[:, n_tap + 4 + S:], extra[0:16, n_tap + 4:n_tap + 4 + S], norms[:, 0:S], low, z, tmp,
                      b_t),
            GlaScale(k, feat[:, 8:10, :], feat[:, 10:12, :], b_t, ref, q_s, k_a, k_b),
            GlaAttend(k, q_s, k_a, k_b, w, v, o),
            HeadRms(k, [o[:, t, :] for t in range(TT)], second, GLA_DV, norms[:, S:S + 512], r,
                    [y[:, 2 * t:2 * t + 2, :].rearrange("p a b -> p (a b)") for t in range(TT)]),
            ToFeatures(k, k.h_tok, k.h_t, DC), OutProj(k, k.h_t, DC), Post(k, False, False)]


def third_ffn(k, j, I=None):
    if I is not None:
        n = j + 1 if j == 0 else 2
        return modulated(I["w_ada_3"][0], I["b_ada_3"][0], 2 * j) + [
            rows(I[f"norm_ffn{n}_3"][0]), gated_pair(I[f"w_ffn{n}_gu_3"][0], D_FF),
            by_rows(I[f"w_ffn{n}_down_3"][0])]
    f = [Modulation(k, 0.5, False), Pre(k, True, True), ToFeatures(k, k.h_tok, k.h_t, DC), FfnIn(k)]
    return f + [OutProj(k, f[-1].hidden, FC), Post(k, False, True)]


def third_mix(k, I=None):
    H = ROPE_HEADS
    if I is not None:
        return modulated(I["w_ada_3"][0], I["b_ada_3"][0], 1) + [
            rows(I["norm_mix_3"][0]), by_columns(I["w_in_3"][0]),
            params(I["gmlp_w_s_3"][0].transpose(2, 0, 1).reshape(P, -1), I["gmlp_b_s_3"][0].T),
            rows(I["gmlp_ln_g_3"][0], I["gmlp_ln_b_3"][0], I["g_attn_out_3"][0], I["g_gmlp_out_3"][0]),
            by_rows(I["w_out_3"][0])]
    room = Room(k)
    qk, v, gu, gv = room(TT, D), room(TT, 512), room(TT, 512), room(TT, 512)
    extra, norms = room(D + H), room(SLOT)
    tmp, qk_t = room(TT, D), room(DC, S)
    p, p_t = room(3 * H, P), room(3 * H, P)
    top, total = room(TT * H), room(TT * H)
    mask = k.c("mask").rearrange("p (t q) -> p t q", t=TT)
    side = lambda first: lambda h: qk_t[64 * (h % 2):64 * (h % 2) + 64, first + h // 2, :]

    def how(t, h, n):
        return lambda dve, dst, bank: dve.scalar_tensor_tensor(dst, bank, HD ** -0.5, mask[:, t, 0:n], ALU.mult,
                                                               ALU.add)

    att = causal_attention(k, H, side(0), side(4), lambda h, a: v[:, a, h * HD:(h + 1) * HD], None, how, p, p_t,
                           top, total, total, k.h_tok, False)
    halves = [[k.h_tok[:, t, a * 512:(a + 1) * 512] for t in range(TT)] for a in range(2)]
    squares = [tmp[:, t, 0:512] for t in range(TT)]
    return [Modulation(k, 1.0, False), Pre(k, True, True), ToFeatures(k, k.h_tok, k.h_t, DC),
            ToTokens(k, [(512, qk[:, :, 0:512], None), (512, qk[:, :, 512:], None), (512, v, None),
                         (512, gu, ACT.Gelu_apprx_tanh), (512, gv, ACT.Gelu_apprx_tanh)]),
            Keep(k, extra), Keep(k, norms), Rope(k, qk, tmp), ToFeatures(k, qk, qk_t, DC)] + att + [
            Spatial(k, gu, gv, extra[:, 0:D].rearrange("p (h t) -> p h t", t=P), extra[:, D:], norms[:, 0:512],
                    norms[:, 512:1024], k.h_tok[:, :, 512:]),
            HeadRms(k, halves[0], halves[0], 512, norms[:, 1024:1536], None, squares),
            HeadRms(k, halves[1], halves[1], 512, norms[:, 1536:], None, squares),
            ToFeatures(k, k.h_tok, k.h_t, DC), OutProj(k, k.h_t, DC), Post(k, False, True)]


def final_norm(k, I=None):
    if I is not None:
        return [rows(I["norm_final_3"])]
    return [Pre(k, True, False, dst=k.x)]


def silu_c(k, name, I=None):
    if I is not None:
        return [params(columns(I[name][0]))]
    return [Silu_c(k, name)]


def layers(only=None):
    out = [("c0", silu_c, ("c",)), ("a0", first_ffn, (0, 0)), ("m0", retention, ()), ("b0", first_ffn, (0, 1)),
           ("a1", first_ffn, (1, 0)), ("m1", nsa, ()), ("b1", first_ffn, (1, 1)),
           ("ev", even, ()), ("p0", peer, (0,)), ("od", fox, ()), ("p1", peer, (1,)),
           ("c3", silu_c, ("c_3",)), ("t1", third_ffn, (0,)), ("t2", third_mix, ()), ("t3", third_ffn, (1,)),
           ("fin", final_norm, ())]
    return [x for x in out if only is None or x[0] in only]


def program(nc, x, const, stream, out, only=None):
    with ExitStack() as ctx:
        k = Chip(ctx, nc)
        stages = [s for _, f, a in layers(only) for s in f(k, *a)]
        total = k.n_slots
        assert total == stream.shape[0], (total, stream.shape)
        block = ctx.enter_context(nc.Block())

        @block.sync
        def _(sp):
            for s in range(total):
                if s >= RING:
                    sp.wait_ge(k.slots_used, s - RING + 1)
                sp.dma_start(k.slot(s), stream[s]).then_inc(k.slot_landed[s % RING], 16)

        def run(eng, name):
            eng.wait_ge(k.loaded, 32)
            for i, s in enumerate(stages):
                parts = {"tensor": s.tensor, "vector": s.vector, "scalar": s.scalar, "gpsimd": s.gpsimd}
                parts[name](eng)
                k.phase_end(eng, i)

        @block.tensor
        def _(pe):
            run(pe, "tensor")

        @block.vector
        def _(dve):
            run(dve, "vector")

        @block.gpsimd
        def _(pool):
            run(pool, "gpsimd")

        @block.scalar
        def _(act):
            act.dma_start(k.x[:, :, :], x.rearrange("b (t p) d -> p (b t) d", p=P)).then_inc(k.loaded, 16)
            act.dma_start(k.const[:, :], const).then_inc(k.loaded, 16)
            run(act, "scalar")
            act.dma_start(out.rearrange("b (t p) d -> p (b t) d", p=P), k.x[:, :, :]).then_inc(k.stored, 16)
            act.wait_ge(k.stored, 16)

        for g in k.signals:
            assert g.sent == g.seen, (g.name, g.sent, g.seen)


def stream_of(inputs, only=None):
    return np.concatenate([b for _, f, a in layers(only) for b in f(None, *a, I=inputs)])


def kernel(**inputs):
    import concourse.bacc as bacc
    from concourse.bass_utils import run_bass_kernel_spmd

    I = {n: np.asarray(v) for n, v in inputs.items()}
    arrays = {"x": I["x"], "const": np.concatenate(list(CONSTS.values()), axis=1), "stream": stream_of(I)}
    nc = bacc.Bacc("TRN2", target_bir_lowering=False, num_devices=1)
    args = [nc.dram_tensor(n, a.shape, F32, kind="ExternalInput").ap() for n, a in arrays.items()]
    out = nc.dram_tensor("out", (1, S, D), F32, kind="ExternalOutput").ap()
    program(nc, *args, out)
    r = run_bass_kernel_spmd(nc, [arrays], core_ids=[0])
    return r.results[0]["out"]
```

```python
from contextlib import ExitStack

import numpy as np

import concourse.bass as bass
from concourse import mybir

F32 = mybir.dt.float32
F32R = mybir.dt.float32r
U32 = mybir.dt.uint32
ALU = mybir.AluOpType
ACT = mybir.ActivationFunctionType
AX = mybir.AxisListType.X

P = 128
S = 256
TT = S // P
D = 1024
DC = D // P
D_FF = 2816
FC = D_FF // P
DEPTH = 2
SLOT = 2048
RING = 4
HALF_SLOT = SLOT // 2
BANK = 512
NB = 4
LN_EPS = 1e-5
EPS = 1e-6
NEG = -1e30
DN_ALPHA = (2 * DEPTH) ** 0.25


class Signal:

    def __init__(self, ctx, nc, name):
        self.name, self.sem = name, ctx.enter_context(nc.semaphore(name))
        self.sent = self.seen = 0

    def send(self):
        self.sent += 1
        return 1

    def take(self, n=1):
        self.seen += n
        return self.seen

    def skip(self, n):
        self.seen += n


class Chip:

    def __init__(self, ctx, nc):
        self.ctx, self.nc = ctx, nc

        def sb(name, shape, dt=F32):
            return ctx.enter_context(nc.sbuf_tensor(name, shape, dt))

        self.x = sb("x_tok", [P, TT, D])
        self.h_tok = sb("h_tok", [P, TT, D])
        self.h_t = sb("h_feat", [P, DC, S])
        self.mod = sb("mod_rows", [P, 3, D])
        self.c_bc = sb("c_rep", [P, DC, P])
        self.ring = sb("weight_ring", [P, RING, SLOT])
        self.w_hi = sb("weights_high", [P, 2, HALF_SLOT], F32R)
        self.w_lo = sb("weights_low", [P, 2, HALF_SLOT], F32R)
        self.h_hi = sb("h_high", [P, DC, S], F32R)
        self.h_lo = sb("h_low", [P, DC, S], F32R)
        self.g_hi = sb("hidden_high", [P, 2, S], F32R)
        self.g_lo = sb("hidden_low", [P, 2, S], F32R)
        self.const = sb("constants", [P, N_CONST])
        self.small = sb("small", [P, 256])
        self.work = sb("work", [P, N_WORK])
        self.acc = ctx.enter_context(nc.psum_tensor("acc", [P, 4, BANK], F32))
        self.bank = ctx.enter_context(nc.psum_tensor("bank", [P, NB, BANK], F32))

        self.banks_for_scalar = Signal(ctx, nc, "banks_for_scalar")
        self.banks_for_vector = Signal(ctx, nc, "banks_for_vector")
        self.scalar_for_tensor = Signal(ctx, nc, "scalar_for_tensor")
        self.vector_for_tensor = Signal(ctx, nc, "vector_for_tensor")
        self.scalar_for_vector = Signal(ctx, nc, "scalar_for_vector")
        self.vector_for_scalar = Signal(ctx, nc, "vector_for_scalar")
        self.gpsimd_for_vector = Signal(ctx, nc, "gpsimd_for_vector")
        self.gpsimd_for_tensor = Signal(ctx, nc, "gpsimd_for_tensor")
        self.tensor_for_gpsimd = Signal(ctx, nc, "tensor_for_gpsimd")
        self.gate_onehots_for_tensor = Signal(ctx, nc, "gate_onehots_for_tensor")
        self.signals = [self.banks_for_scalar,
                        self.banks_for_vector,
                        self.scalar_for_tensor,
                        self.vector_for_tensor,
                        self.scalar_for_vector,
                        self.vector_for_scalar,
                        self.gpsimd_for_vector,
                        self.gpsimd_for_tensor,
                        self.tensor_for_gpsimd,
                        self.gate_onehots_for_tensor]
        self.dve_step = ctx.enter_context(nc.semaphore("dve_step"))
        self.act_step = ctx.enter_context(nc.semaphore("act_step"))
        self.pool_step = ctx.enter_context(nc.semaphore("pool_step"))
        self.steps = {"dve": 0, "act": 0, "pool": 0}
        self.phase_done = ctx.enter_context(nc.semaphore("phase_done"))
        self.slot_landed = [ctx.enter_context(nc.semaphore(f"slot_landed{i}")) for i in range(RING)]
        self.highs_ready = ctx.enter_context(nc.semaphore("highs_ready"))
        self.lows_ready = ctx.enter_context(nc.semaphore("lows_ready"))
        self.halves_used = ctx.enter_context(nc.semaphore("halves_used"))
        self.slots_used = ctx.enter_context(nc.semaphore("slots_used"))
        self.couples_made = ctx.enter_context(nc.semaphore("couples_made"))
        self.loaded = ctx.enter_context(nc.semaphore("inputs_loaded"))
        self.stored = ctx.enter_context(nc.semaphore("output_stored"))
        self.n_slots = 0
        self.pending = 0
        self.gate_fills = 0
        self.last = self.merged = None
        self.n_halves = self.pending_halves = 0

    def c(self, name):
        a, n = CONST_AT[name]
        return self.const[:, a:a + n]

    def slots(self, n):
        a = self.n_slots
        self.n_slots += n
        return a

    def slot(self, s):
        return self.ring[:, s % RING, :]

    def loads(self, s):
        return 16 * (s // RING + 1)

    def mm(self, out, lhs, rhs, start, stop, last=False):
        ins = self.nc.tensor.matmul(out, lhs, rhs, start=start, stop=stop)
        if self.pending_halves and not last:
            ins.then_inc(self.halves_used, self.pending_halves)
            self.pending_halves = 0
        elif self.pending and not last:
            ins.then_inc(self.slots_used, self.pending)
            self.pending = 0
        return ins

    def slots_through(self, n=1):
        self.pending += n

    def phase_end(self, eng, index):
        if eng is self.nc.tensor and self.pending:
            eng.drain().then_inc(self.slots_used, self.pending)
            self.pending = 0
        if eng is self.nc.tensor and self.pending_halves:
            eng.drain().then_inc(self.halves_used, self.pending_halves)
            self.pending_halves = 0
        eng.drain().then_inc(self.phase_done, 1)
        eng.wait_ge(self.phase_done, 4 * (index + 1))

    def step(self, engine):
        self.steps[engine] += 1
        return self.steps[engine]


class Stage:
    def __init__(self, k):
        self.k = k

    def tensor(self, pe):
        pass

    def vector(self, dve):
        pass

    def scalar(self, act):
        pass

    def gpsimd(self, pool):
        pass



RET_HEADS = 4
RET_QK = D // RET_HEADS
RET_V = 2 * RET_QK
N_CMP = (S - 32) // 16 + 1
NSA_HEADS, NSA_GROUPS, HD = 16, 4, 64


def constants():
    p = np.arange(P)
    q = np.arange(S)
    tok = p[:, None, None] + P * np.arange(TT)[None, :, None]
    out = {}
    out["ident"] = np.eye(P)
    out["causal_t"] = (tok <= q[None, None, :]).reshape(P, -1)
    out["mask"] = np.where(tok >= q[None, None, :], 0.0, NEG).reshape(P, -1)
    out["dist"] = np.where(tok >= q[None, None, :], tok - q[None, None, :], 1e32).reshape(P, -1)
    out["iota"] = np.broadcast_to(np.arange(P), (P, P))
    end = np.arange(N_CMP) * 16 + 31
    d = tok - end[None, None, :]
    out["cmp_dist"] = np.where(d >= 0, d, 1e32).reshape(P, -1)
    out["cmp_mask"] = (d >= 0).reshape(P, -1)
    inv = (10000.0 ** (-np.arange(32, dtype=np.float32) / 32)).astype(np.float32)
    ang = tok.astype(np.float32) * inv[None, None, :]
    out["cos"] = np.cos(ang).reshape(P, -1)
    out["sin"] = np.sin(ang).reshape(P, -1)
    return {k: np.ascontiguousarray(v, dtype=np.float32) for k, v in out.items()}


CONSTS = constants()
CONST_AT, N_CONST = {}, 0
for _n, _v in CONSTS.items():
    CONST_AT[_n] = (N_CONST, _v.shape[1])
    N_CONST += _v.shape[1]
N_WORK = 23300



class Silu_c(Stage):

    def __init__(self, k, which):
        super().__init__(k)
        self.s = k.slots(1)
        self.which = which

    def scalar(self, act):
        k = self.k
        act.wait_ge(k.slot_landed[(self.s) % RING], k.loads(self.s))
        cs = k.small[:, 0:DC]
        act.activation(cs, k.slot(self.s)[:, 0:DC], ACT.Silu).then_inc(k.act_step, 1)
        act.wait_ge(k.act_step, k.step("act"))
        for j in range(DC):
            ins = act.activation(k.c_bc[:, j, :], k.c("ident"), ACT.Identity, bias=cs[:, j:j + 1], scale=0.0)
        ins.then_inc(k.scalar_for_tensor.sem, k.scalar_for_tensor.send())

    def tensor(self, pe):
        k = self.k
        pe.wait_ge(k.scalar_for_tensor.sem, k.scalar_for_tensor.take())
        pe.sem_inc(k.slots_used, 1)



class Modulation(Stage):

    def __init__(self, k, gate_scale, gate_one, beside=None):
        super().__init__(k)
        self.gate_scale, self.gate_one, self.beside = gate_scale, gate_one, beside
        self.other_slots = 0 if beside is None else beside.own_slots
        self.s = k.slots(12)
        self.sb = k.slots(2)

    def tensor(self, pe):
        k = self.k
        for b in range(6):
            if b >= NB:
                pe.wait_ge(k.scalar_for_tensor.sem, k.scalar_for_tensor.take())
            for kk in range(DC):
                s = self.s + 2 * b + kk // 4
                if kk % 4 == 0:
                    pe.wait_ge(k.slot_landed[s % RING], k.loads(s))
                if self.other_slots and b == 0 and kk == 4:
                    pe.wait_ge(k.vector_for_tensor.sem, k.vector_for_tensor.take())
                    k.slots_through(self.other_slots + 1)
                mm = k.mm(k.bank[:, b % NB, :], k.c_bc[:, kk, :],
                          k.slot(s)[:, (kk % 4) * 512:(kk % 4 + 1) * 512],
                          start=kk == 0, stop=kk == DC - 1, last=kk == DC - 1)
                if kk % 4 == 3:
                    if not self.other_slots or b > 0 or kk > 4:
                        k.slots_through()
            mm.then_inc(k.banks_for_scalar.sem, k.banks_for_scalar.send())
        k.scalar_for_tensor.skip(NB)
        pe.wait_ge(k.vector_for_tensor.sem, k.vector_for_tensor.take())
        k.slots_through(2)

    def scalar(self, act):
        k = self.k
        for b in range(6):
            if b == 1 and self.beside is not None:
                self.beside.scalar_beside(act)
            act.wait_ge(k.banks_for_scalar.sem, k.banks_for_scalar.take())
            act.activation(k.mod[:, b // 2, b % 2 * 512:(b % 2 + 1) * 512], k.bank[:, b % NB, :], ACT.Copy).then_inc(
                k.scalar_for_tensor.sem, k.scalar_for_tensor.send())
        act.drain().then_inc(k.scalar_for_vector.sem, k.scalar_for_vector.send())

    def vector(self, dve):
        k = self.k
        if self.beside is not None:
            self.beside.vector(dve)
        dve.wait_ge(k.slot_landed[self.sb % RING], k.loads(self.sb))
        dve.wait_ge(k.slot_landed[(self.sb + 1) % RING], k.loads(self.sb + 1))
        dve.wait_ge(k.scalar_for_vector.sem, k.scalar_for_vector.take())
        dve.tensor_tensor(k.mod[:, 0, :], k.mod[:, 0, :], k.slot(self.sb)[:, 0:D], ALU.add)
        dve.scalar_tensor_tensor(k.mod[:, 1, :], k.mod[:, 1, :], 1.0, k.slot(self.sb)[:, D:2 * D], ALU.add, ALU.add)
        dve.scalar_tensor_tensor(k.mod[:, 2, :], k.mod[:, 2, :], 1.0 if self.gate_one else 0.0,
                                 k.slot(self.sb + 1)[:, 0:D], ALU.add, ALU.add).then_inc(k.dve_step, 1)
        dve.wait_ge(k.dve_step, k.step("dve"))
        dve.tensor_scalar(k.mod[:, 2, :], k.mod[:, 2, :], self.gate_scale, None, ALU.mult).then_inc(
            k.vector_for_tensor.sem, k.vector_for_tensor.send())


def rms_rows(k, dve, src_tiles, n, eps, stat):
    for t, src in enumerate(src_tiles):
        ins = dve.scalar_tensor_tensor(k.h_tok[:, t, 0:n], src, 1.0, src, ALU.mult, ALU.mult,
                                       accum_out=stat[:, t:t + 1])
    ins.then_inc(k.dve_step, 1)
    dve.wait_ge(k.dve_step, k.step("dve"))
    T = len(src_tiles)
    inverse_root(k, dve, dve.tensor_scalar(stat[:, 0:T], stat[:, 0:T], 1.0 / n, eps, ALU.mult, ALU.add),
                 stat[:, 0:T])


def inverse_root(k, dve, ins, stat):
    ins.then_inc(k.vector_for_scalar.sem, k.vector_for_scalar.send())
    dve.wait_ge(k.scalar_for_vector.sem, k.scalar_for_vector.take())
    dve.reciprocal(stat, stat).then_inc(k.dve_step, 1)
    dve.wait_ge(k.dve_step, k.step("dve"))


def take_root(k, act, stat):
    act.wait_ge(k.vector_for_scalar.sem, k.vector_for_scalar.take())
    act.activation(stat, stat, ACT.Sqrt).then_inc(k.scalar_for_vector.sem, k.scalar_for_vector.send())


class Pre(Stage):

    def __init__(self, k, norm, modulated, dst=None):
        super().__init__(k)
        self.norm, self.modulated = norm, modulated
        self.s = k.slots(1) if norm else None
        self.dst = dst

    def tensor(self, pe):
        if self.norm:
            pe.wait_ge(self.k.vector_for_tensor.sem, self.k.vector_for_tensor.take())
            self.k.slots_through()

    def scalar(self, act):
        if self.norm:
            take_root(self.k, act, self.k.small[:, 16:18])

    def vector(self, dve):
        k = self.k
        src, dst = k.x, k.h_tok if self.dst is None else self.dst
        if self.norm:
            stat = k.small[:, 16:18]
            rms_rows(k, dve, [k.x[:, t, :] for t in range(TT)], D, EPS, stat)
            dve.wait_ge(k.slot_landed[(self.s) % RING], k.loads(self.s))
            for t in range(TT):
                ins = dve.scalar_tensor_tensor(dst[:, t, :], k.x[:, t, :], stat[:, t:t + 1],
                                               k.slot(self.s)[:, 0:D], ALU.mult, ALU.mult)
            ins.then_inc(k.vector_for_tensor.sem, k.vector_for_tensor.send())
            src = dst
        if self.modulated:
            if self.norm:
                dve.wait_ge(k.vector_for_tensor.sem, k.vector_for_tensor.sent)
            for t in range(TT):
                ins = dve.tensor_tensor(dst[:, t, :], src[:, t, :], k.mod[:, 1, :], ALU.mult)
            ins.then_inc(k.dve_step, 1)
            dve.wait_ge(k.dve_step, k.step("dve"))
            for t in range(TT):
                dve.tensor_tensor(dst[:, t, :], dst[:, t, :], k.mod[:, 0, :], ALU.add)


class ToFeatures(Stage):

    def __init__(self, k, src, dst, chunks):
        super().__init__(k)
        self.src, self.dst, self.chunks = src, dst, chunks
        self.steps = [(t, c, min(4, chunks - c)) for c in range(0, chunks, 4) for t in range(TT)]

    def tensor(self, pe):
        k = self.k
        for i, (t, c, n) in enumerate(self.steps):
            if i >= NB:
                read = k.vector_for_tensor if i % 2 == 0 else k.scalar_for_tensor
                pe.wait_ge(read.sem, read.take())
            for j in range(n):
                mm = pe.transpose(k.bank[:, i % NB, j * P:(j + 1) * P],
                                  self.src[:, t, (c + j) * P:(c + j + 1) * P], k.c("ident"))
            done = k.banks_for_vector if i % 2 == 0 else k.banks_for_scalar
            mm.then_inc(done.sem, done.send())
        for i in range(max(0, len(self.steps) - NB), len(self.steps)):
            (k.vector_for_tensor if i % 2 == 0 else k.scalar_for_tensor).skip(1)

    def evacuate(self, eng, parity):
        k = self.k
        taken, sent = (k.banks_for_vector, k.vector_for_tensor) if parity == 0 else (k.banks_for_scalar, k.scalar_for_tensor)
        for i, (t, c, n) in enumerate(self.steps):
            if i % 2 != parity:
                continue
            eng.wait_ge(taken.sem, taken.take())
            dst = self.dst[:, c:c + n, t * P:(t + 1) * P]
            src = k.bank[:, i % NB, 0:n * P].rearrange("p (c q) -> p c q", q=P)
            ins = eng.tensor_copy(dst, src) if parity == 0 else eng.activation(dst, src, ACT.Copy)
            ins.then_inc(sent.sem, sent.send())

    def vector(self, dve):
        self.evacuate(dve, 0)

    def scalar(self, act):
        self.evacuate(act, 1)


class SplitInput(Stage):

    def __init__(self, k, src=None):
        super().__init__(k)
        self.src = k.h_t if src is None else src

    def scalar(self, act):
        k = self.k
        for c in range(0, DC, 2):
            act.activation(k.h_hi[:, c:c + 2, :], self.src[:, c:c + 2, :], ACT.Copy).then_inc(
                k.scalar_for_vector.sem, k.scalar_for_vector.send())

    def vector(self, dve):
        k = self.k
        for c in range(0, DC, 2):
            dve.wait_ge(k.scalar_for_vector.sem, k.scalar_for_vector.take())
            dve.tensor_tensor(k.h_lo[:, c:c + 2, :], self.src[:, c:c + 2, :], k.h_hi[:, c:c + 2, :].bitcast(F32),
                              ALU.subtract)


class SplitWeights(Stage):

    QUARTER = HALF_SLOT // 2

    def take_halves(self, n):
        assert n % 2 == 0
        self.n, self.s, self.base = n, self.k.slots(n // 2), self.k.n_halves
        self.k.n_halves += n

    def raw(self, g, q):
        a = (g % 2) * HALF_SLOT + q * self.QUARTER
        return self.k.slot(self.s + g // 2)[:, a:a + self.QUARTER]

    def tensor(self, pe):
        k = self.k
        for g in range(self.n):
            b = (self.base + g) % 2
            pe.wait_ge(k.lows_ready, self.base + g + 1)
            if g % 2 == 1:
                k.slots_through()
            self.products(pe, g, k.w_hi[:, b, :], k.w_lo[:, b, :])
            k.pending_halves += 1
        self.tensor_end()

    def tensor_end(self):
        pass

    def scalar_after(self, act, g):
        pass

    def vector_after(self, dve, g):
        pass

    def scalar(self, act):
        k = self.k
        for g in range(self.n + 2):
            b = (self.base + g) % 2
            if g < self.n:
                act.wait_ge(k.slot_landed[(self.s + g // 2) % RING], k.loads(self.s + g // 2))
                if self.base + g >= 2:
                    act.wait_ge(k.halves_used, self.base + g - 1)
                for q in range(2):
                    act.activation(k.w_hi[:, b, q * self.QUARTER:(q + 1) * self.QUARTER], self.raw(g, q),
                                   ACT.Copy).then_inc(k.highs_ready, 1)
            if g >= 2:
                self.scalar_after(act, g - 2)

    def vector(self, dve):
        k = self.k
        for g in range(self.n + 2):
            b = (self.base + g) % 2
            if g < self.n:
                for q in range(2):
                    w = slice(q * self.QUARTER, (q + 1) * self.QUARTER)
                    dve.wait_ge(k.highs_ready, 2 * (self.base + g) + q + 1)
                    ins = dve.tensor_tensor(k.w_lo[:, b, w], self.raw(g, q), k.w_hi[:, b, w].bitcast(F32),
                                            ALU.subtract)
                ins.then_inc(k.lows_ready, 1)
            if g >= 2:
                self.vector_after(dve, g - 2)


class TwoLayers(SplitWeights):

    def __init__(self, k, chunks, parts, func, gates, first, final, act_out, product):
        super().__init__(k)
        self.chunks, self.parts, self.func, self.gates = chunks, parts, func, gates
        self.first, self.final, self.act_out, self.product = first, final, act_out, product
        self.halves = []
        for c in range(chunks + 1):
            if c < chunks:
                self.halves += [("in", c, part) for part in range(parts)]
            if c >= 1:
                self.halves.append(("out", c - 1, 0))
        self.take_halves(len(self.halves))
        self.hidden_at = {g: c for g, (kind, c, part) in enumerate(self.halves)
                          if kind == "in" and part == parts - 1}

    def products(self, pe, g, hi, lo):
        k = self.k
        for kind, c, part in self.halves[g:g + 1]:
            if kind == "in":
                out = k.bank[:, c % NB, part * S:(part + 1) * S]
                for kk in range(DC):
                    w = slice(kk * P, (kk + 1) * P)
                    for i, (a, x) in enumerate(((hi, k.h_hi), (hi, k.h_lo), (lo, k.h_hi))):
                        mm = k.mm(out, a[:, w], x[:, kk, :], start=kk == 0 and i == 0, stop=kk == DC - 1 and i == 2,
                                  last=kk == DC - 1 and i == 2)
                if part == self.parts - 1:
                    mm.then_inc(k.banks_for_scalar.sem, k.banks_for_scalar.send())
            else:
                pe.wait_ge(k.vector_for_tensor.sem, k.vector_for_tensor.take())
                for t in range(TT):
                    x_hi, x_lo = (x[:, c % 2, t * P:(t + 1) * P] for x in (k.g_hi, k.g_lo))
                    for h in range(2):
                        w = slice(h * 512, (h + 1) * 512)
                        for i, (x, a) in enumerate(((x_hi, hi), (x_hi, lo), (x_lo, hi))):
                            k.mm(k.acc[:, 2 * t + h, :], x, a[:, w], start=self.first and c == 0 and i == 0,
                                 stop=self.final and c == self.chunks - 1 and i == 2)

    def tensor_end(self):
        pass

    def scalar_after(self, act, g):
        k = self.k
        if g in self.hidden_at:
            c = self.hidden_at[g]
            act.wait_ge(k.banks_for_scalar.sem, k.banks_for_scalar.take())
            if c >= 2:
                act.wait_ge(k.vector_for_scalar.sem, k.vector_for_scalar.take())
            act.activation(self.act_out[:, c % 2, :], k.bank[:, c % NB, 0:S], self.func).then_inc(
                k.scalar_for_vector.sem, k.scalar_for_vector.send())
            if c == self.chunks - 1:
                k.vector_for_scalar.skip(2)

    def vector_after(self, dve, g):
        k = self.k
        if g in self.hidden_at:
            c = self.hidden_at[g]
            dve.wait_ge(k.scalar_for_vector.sem, k.scalar_for_vector.take())
            other = k.bank[:, c % NB, S:2 * S] if self.gates is None else self.gates[:, c, :]
            dve.tensor_tensor(self.product, self.act_out[:, c % 2, :], other, ALU.mult).then_inc(
                k.vector_for_scalar.sem, k.vector_for_scalar.send())
            dve.wait_ge(k.vector_for_scalar.sem, k.vector_for_scalar.sent)
            dve.tensor_copy(k.g_hi[:, c % 2, :], self.product).then_inc(k.dve_step, 1)
            dve.wait_ge(k.dve_step, k.step("dve"))
            dve.tensor_tensor(k.g_lo[:, c % 2, :], self.product, k.g_hi[:, c % 2, :].bitcast(F32),
                              ALU.subtract).then_inc(k.vector_for_tensor.sem, k.vector_for_tensor.send())
            dve.wait_ge(k.vector_for_tensor.sem, k.vector_for_tensor.sent)


class OutProj(SplitWeights):

    def __init__(self, k, first=True, final=True):
        super().__init__(k)
        self.first, self.final = first, final
        self.take_halves(DC)

    def products(self, pe, c, hi, lo):
        k = self.k
        for t in range(TT):
            y_hi, y_lo = (y[:, c, t * P:(t + 1) * P] for y in (k.h_hi, k.h_lo))
            for h in range(2):
                w = slice(h * 512, (h + 1) * 512)
                for i, (y, a) in enumerate(((y_hi, hi), (y_hi, lo), (y_lo, hi))):
                    k.mm(k.acc[:, 2 * t + h, :], y, a[:, w], start=self.first and c == 0 and i == 0,
                         stop=self.final and c == DC - 1 and i == 2)


class Post(Stage):

    def __init__(self, k, norm, gated):
        super().__init__(k)
        self.norm, self.gated = norm, gated
        self.s = k.slots(1) if norm else None
        self.own_slots = 1 if norm else 0
        self.rows = k.work[:, 0:SLOT]
        self.accompanied = False

    def scalar_beside(self, act):
        k = self.k
        if self.gated:
            act.wait_ge(k.vector_for_scalar.sem, k.vector_for_scalar.take())
        self.scalar(act)

    def tensor(self, pe):
        if self.norm:
            pe.wait_ge(self.k.vector_for_tensor.sem, self.k.vector_for_tensor.take())
            self.k.slots_through()

    def scalar(self, act):
        if self.norm:
            take_root(self.k, act, self.k.small[:, 44:46])

    def vector(self, dve):
        k = self.k
        if self.norm:
            dve.wait_ge(k.slot_landed[self.s % RING], k.loads(self.s))
            dve.tensor_copy(self.rows, k.slot(self.s)[:, 0:SLOT]).then_inc(
                k.vector_for_tensor.sem, k.vector_for_tensor.send())
            dve.wait_ge(k.vector_for_tensor.sem, k.vector_for_tensor.sent)
        y = k.acc[:, :, :].rearrange("p (t h) n -> p t (h n)", t=TT)
        for t in range(TT):
            if self.gated:
                ins = dve.tensor_tensor(k.h_tok[:, t, :], y[:, t, :], k.mod[:, 2, :], ALU.mult)
        if self.gated:
            ins.then_inc(k.dve_step, 1)
            dve.wait_ge(k.dve_step, k.step("dve"))
            if self.accompanied:
                dve.tensor_copy(k.small[:, 46:47], k.h_tok[:, 0, 0:1]).then_inc(
                    k.vector_for_scalar.sem, k.vector_for_scalar.send())
        for t in range(TT):
            add = k.h_tok[:, t, :] if self.gated else y[:, t, :]
            ins = dve.scalar_tensor_tensor(k.x[:, t, :], k.x[:, t, :], DN_ALPHA if self.norm else 1.0, add,
                                           ALU.mult, ALU.add)
        ins.then_inc(k.dve_step, 1)
        dve.wait_ge(k.dve_step, k.step("dve"))
        if not self.norm:
            return
        stats, mv = k.small[:, 16:40].rearrange("p (t c s) -> p t c s", t=TT, c=2), k.small[:, 40:44]
        for t in range(TT):
            for c in range(2):
                ins = dve.bn_stats(stats[:, t, c, :], k.x[:, t, c * 512:(c + 1) * 512])
        ins.then_inc(k.dve_step, 1)
        dve.wait_ge(k.dve_step, k.step("dve"))
        for t in range(TT):
            ins = dve.bn_aggr(mv[:, 2 * t:2 * t + 2], k.small[:, 16 + 12 * t:28 + 12 * t])
        ins.then_inc(k.dve_step, 1)
        dve.wait_ge(k.dve_step, k.step("dve"))
        rstd = k.small[:, 44:46]
        var = mv.rearrange("p (t two) -> p t two", two=2)[:, :, 1]
        inverse_root(k, dve, dve.tensor_scalar(rstd, var, LN_EPS, None, ALU.add), rstd)
        for t in range(TT):
            ins = dve.tensor_scalar(k.x[:, t, :], k.x[:, t, :], mv[:, 2 * t:2 * t + 1], rstd[:, t:t + 1],
                                    ALU.subtract, ALU.mult)
        ins.then_inc(k.dve_step, 1)
        dve.wait_ge(k.dve_step, k.step("dve"))
        for t in range(TT):
            ins = dve.tensor_tensor(k.x[:, t, :], k.x[:, t, :], self.rows[:, 0:D], ALU.mult)
        ins.then_inc(k.dve_step, 1)
        dve.wait_ge(k.dve_step, k.step("dve"))
        for t in range(TT):
            dve.tensor_tensor(k.x[:, t, :], k.x[:, t, :], self.rows[:, D:2 * D], ALU.add)



class ToTokensNarrow(Stage):

    def __init__(self, k, blocks):
        super().__init__(k)
        self.blocks = [(w, dst, f, k.slots(2 if w > 256 else 1)) for w, dst, f in blocks]
        self.fills = [(w, dst, f, s, t) for w, dst, f, s in self.blocks for t in range(TT)]

    def by_vector(self, f, t):
        return f is None and t == 0

    def tensor(self, pe):
        k = self.k
        for i, (w, dst, f, s, t) in enumerate(self.fills):
            if i >= NB:
                before = self.fills[i - NB]
                read = k.vector_for_tensor if self.by_vector(before[2], before[4]) else k.scalar_for_tensor
                pe.wait_ge(read.sem, read.take())
            per = 4 if w > 256 else 8
            for kk in range(DC):
                if kk % per == 0 and t == 0:
                    pe.wait_ge(k.slot_landed[(s + kk // per) % RING], k.loads(s + kk // per))
                mm = k.mm(k.bank[:, i % NB, 0:w], k.h_t[:, kk, t * P:(t + 1) * P],
                          k.slot(s + kk // per)[:, (kk % per) * w:(kk % per + 1) * w],
                          start=kk == 0, stop=kk == DC - 1, last=kk == DC - 1)
            done = k.banks_for_vector if self.by_vector(f, t) else k.banks_for_scalar
            mm.then_inc(done.sem, done.send())
            if t == TT - 1:
                k.slots_through(DC // per)
        for w, dst, f, s, t in self.fills[-NB:]:
            (k.vector_for_tensor if self.by_vector(f, t) else k.scalar_for_tensor).skip(1)

    def vector(self, dve):
        k = self.k
        for i, (w, dst, f, s, t) in enumerate(self.fills):
            if self.by_vector(f, t):
                dve.wait_ge(k.banks_for_vector.sem, k.banks_for_vector.take())
                dve.tensor_copy(dst[:, t, :], k.bank[:, i % NB, 0:w]).then_inc(k.vector_for_tensor.sem, k.vector_for_tensor.send())

    def scalar(self, act):
        k = self.k
        for i, (w, dst, f, s, t) in enumerate(self.fills):
            if not self.by_vector(f, t):
                act.wait_ge(k.banks_for_scalar.sem, k.banks_for_scalar.take())
                act.activation(dst[:, t, :], k.bank[:, i % NB, 0:w], f or ACT.Copy).then_inc(k.scalar_for_tensor.sem, k.scalar_for_tensor.send())


class ToTokens(SplitWeights):

    def __init__(self, k, blocks):
        super().__init__(k)
        self.blocks = blocks
        self.take_halves(4 * len(blocks))

    def by_vector(self, b, t):
        return self.blocks[b][1] is None and t == 0

    def products(self, pe, g, hi, lo):
        k = self.k
        b, piece = g // 4, g % 4
        for t in range(TT):
            bank = (TT * b + t) % NB
            if piece == 0 and b >= NB // TT:
                read = k.vector_for_tensor if self.by_vector(b - NB // TT, t) else k.scalar_for_tensor
                pe.wait_ge(read.sem, read.take())
            for j in range(2):
                kk = 2 * piece + j
                x_hi, x_lo = (x[:, kk, t * P:(t + 1) * P] for x in (k.h_hi, k.h_lo))
                w = slice(j * 512, (j + 1) * 512)
                for i, (x, a) in enumerate(((x_hi, hi), (x_hi, lo), (x_lo, hi))):
                    end = kk == DC - 1 and i == 2
                    mm = k.mm(k.bank[:, bank, :], x, a[:, w], start=kk == 0 and i == 0, stop=end, last=end)
            if piece == 3:
                done = k.banks_for_vector if self.by_vector(b, t) else k.banks_for_scalar
                mm.then_inc(done.sem, done.send())

    def tensor_end(self):
        k = self.k
        for b in range(max(0, len(self.blocks) - NB // TT), len(self.blocks)):
            for t in range(TT):
                (k.vector_for_tensor if self.by_vector(b, t) else k.scalar_for_tensor).skip(1)

    def vector_after(self, dve, g):
        k = self.k
        b = g // 4
        if g % 4 == 3 and self.by_vector(b, 0):
            dve.wait_ge(k.banks_for_vector.sem, k.banks_for_vector.take())
            dve.tensor_copy(self.blocks[b][0][:, 0, :], k.bank[:, TT * b % NB, :]).then_inc(
                k.vector_for_tensor.sem, k.vector_for_tensor.send())

    def scalar_after(self, act, g):
        k = self.k
        b = g // 4
        for t in range(TT):
            if g % 4 == 3 and not self.by_vector(b, t):
                act.wait_ge(k.banks_for_scalar.sem, k.banks_for_scalar.take())
                act.activation(self.blocks[b][0][:, t, :], k.bank[:, (TT * b + t) % NB, :],
                               self.blocks[b][1] or ACT.Copy).then_inc(
                    k.scalar_for_tensor.sem, k.scalar_for_tensor.send())


class ToFeatureRows(SplitWeights):

    def __init__(self, k, dst, chunks, scaled=0, scale=1.0):
        super().__init__(k)
        self.dst, self.pairs, self.scaled, self.scale = dst, chunks // 2, scaled, scale
        self.take_halves(chunks)

    def products(self, pe, g, hi, lo):
        k = self.k
        j, two = g // 2, g % 2
        if two == 0 and j >= NB:
            read = k.vector_for_tensor if j % 2 == 0 else k.scalar_for_tensor
            pe.wait_ge(read.sem, read.take())
        for kk in range(DC):
            w = slice(kk * P, (kk + 1) * P)
            for i, (a, x) in enumerate(((hi, k.h_hi), (hi, k.h_lo), (lo, k.h_hi))):
                end = kk == DC - 1 and i == 2
                mm = k.mm(k.bank[:, j % NB, two * S:(two + 1) * S], a[:, w], x[:, kk, :],
                          start=kk == 0 and i == 0, stop=end, last=end and two == 1)
        if two == 1:
            done = k.banks_for_vector if j % 2 == 0 else k.banks_for_scalar
            mm.then_inc(done.sem, done.send())

    def tensor_end(self):
        k = self.k
        for j in range(max(0, self.pairs - NB), self.pairs):
            (k.vector_for_tensor if j % 2 == 0 else k.scalar_for_tensor).skip(1)

    def piece(self, j):
        k = self.k
        return (self.dst[:, 2 * j:2 * j + 2, :], k.bank[:, j % NB, :].rearrange("p (c t) -> p c t", t=S),
                self.scale if 2 * j < self.scaled else 1.0)

    def vector_after(self, dve, g):
        k = self.k
        if g % 4 == 1:
            dve.wait_ge(k.banks_for_vector.sem, k.banks_for_vector.take())
            dst, src, scale = self.piece(g // 2)
            dve.tensor_scalar(dst, src, scale, None, ALU.mult).then_inc(
                k.vector_for_tensor.sem, k.vector_for_tensor.send())

    def scalar_after(self, act, g):
        k = self.k
        if g % 4 == 3:
            act.wait_ge(k.banks_for_scalar.sem, k.banks_for_scalar.take())
            dst, src, scale = self.piece(g // 2)
            act.activation(dst, src, ACT.Copy, scale=scale).then_inc(
                k.scalar_for_tensor.sem, k.scalar_for_tensor.send())


class Turn(Stage):

    def __init__(self, k, groups):
        super().__init__(k)
        self.groups = groups

    def tensor(self, pe):
        k = self.k
        for i, (sources, dst) in enumerate(self.groups):
            if i >= NB:
                read = k.vector_for_tensor if i % 2 == 0 else k.scalar_for_tensor
                pe.wait_ge(read.sem, read.take())
            for j, src in enumerate(sources):
                r, c = src.shape
                mm = pe.transpose(k.bank[0:c, i % NB, j * P:j * P + r], src, k.c("ident")[0:r, 0:r])
            done = k.banks_for_vector if i % 2 == 0 else k.banks_for_scalar
            mm.then_inc(done.sem, done.send())
        for i in range(max(0, len(self.groups) - NB), len(self.groups)):
            (k.vector_for_tensor if i % 2 == 0 else k.scalar_for_tensor).skip(1)

    def piece(self, i):
        sources, dst = self.groups[i]
        r, c = sources[0].shape
        n = len(sources)
        return dst, self.k.bank[0:c, i % NB, 0:n * P].rearrange("p (b r) -> p b r", r=P)[:, :, 0:r]

    def vector(self, dve):
        k = self.k
        for i in range(0, len(self.groups), 2):
            dve.wait_ge(k.banks_for_vector.sem, k.banks_for_vector.take())
            dst, src = self.piece(i)
            dve.tensor_copy(dst, src).then_inc(k.vector_for_tensor.sem, k.vector_for_tensor.send())

    def scalar(self, act):
        k = self.k
        for i in range(1, len(self.groups), 2):
            act.wait_ge(k.banks_for_scalar.sem, k.banks_for_scalar.take())
            dst, src = self.piece(i)
            act.activation(dst, src, ACT.Copy).then_inc(k.scalar_for_tensor.sem, k.scalar_for_tensor.send())


def moments(k, dve, pieces, stats, mv, rstd, eps):
    for i, src in enumerate(pieces):
        ins = dve.bn_stats(stats[:, 6 * i:6 * i + 6], src)
    ins.then_inc(k.dve_step, 1)
    dve.wait_ge(k.dve_step, k.step("dve"))
    n = len(pieces)
    for i in range(n):
        ins = dve.bn_aggr(mv[:, 2 * i:2 * i + 2], stats[:, 6 * i:6 * i + 6])
    ins.then_inc(k.dve_step, 1)
    dve.wait_ge(k.dve_step, k.step("dve"))
    var = mv[:, 0:2 * n].rearrange("p (t two) -> p t two", two=2)[:, :, 1]
    inverse_root(k, dve, dve.tensor_scalar(rstd, var, eps, None, ALU.add), rstd)


class Room:

    def __init__(self, k):
        self.k, self.at = k, 0

    def __call__(self, *shape):
        n = int(np.prod(shape))
        a = self.k.work[:, self.at:self.at + n]
        self.at += n
        assert self.at <= N_WORK, self.at
        if len(shape) == 2:
            return a.rearrange("p (a b) -> p a b", b=shape[1])
        if len(shape) == 3:
            return a.rearrange("p (a b c) -> p a b c", b=shape[1], c=shape[2])
        return a



class RetScores(Stage):

    def __init__(self, k, q_t, k_t, dst):
        super().__init__(k)
        self.q_t, self.k_t, self.dst = q_t, k_t, dst
        self.s = k.slots(1)

    def tensor(self, pe):
        k = self.k
        for h in range(RET_HEADS):
            for kt in range(TT):
                for c in range(2):
                    mm = k.mm(k.bank[:, h, kt * S:(kt + 1) * S], self.k_t[:, 2 * h + c, kt * P:(kt + 1) * P],
                              self.q_t[:, 2 * h + c, :], start=c == 0, stop=c == 1, last=True)
            mm.then_inc(k.banks_for_vector.sem, k.banks_for_vector.send())
        pe.wait_ge(k.vector_for_tensor.sem, k.vector_for_tensor.take())
        k.slots_through()

    def vector(self, dve):
        k = self.k
        dve.wait_ge(k.slot_landed[(self.s) % RING], k.loads(self.s))
        for h in range(RET_HEADS):
            dve.wait_ge(k.banks_for_vector.sem, k.banks_for_vector.take())
            ins = dve.tensor_tensor(self.dst[:, h, :], k.bank[:, h, :], k.slot(self.s)[:, h * 512:(h + 1) * 512],
                                    ALU.mult)
        ins.then_inc(k.vector_for_tensor.sem, k.vector_for_tensor.send())


class RetOut(Stage):

    def __init__(self, k, w, v, g, o):
        super().__init__(k)
        self.w, self.v, self.g, self.o = w, v, g, o
        self.jobs = [(t, h) for t in range(TT) for h in range(RET_HEADS)]

    def tensor(self, pe):
        k = self.k
        for i, (t, h) in enumerate(self.jobs):
            if i >= NB:
                pe.wait_ge(k.scalar_for_tensor.sem, k.scalar_for_tensor.take())
            for kt in range(t + 1):
                mm = k.mm(k.bank[:, i % NB, :], self.w[:, h, kt * S + t * P:kt * S + (t + 1) * P],
                          self.v[:, kt, h * RET_V:(h + 1) * RET_V], start=kt == 0, stop=kt == t, last=True)
            mm.then_inc(k.banks_for_scalar.sem, k.banks_for_scalar.send())
        k.scalar_for_tensor.skip(NB)

    def scalar(self, act):
        k = self.k
        for i, (t, h) in enumerate(self.jobs):
            act.wait_ge(k.banks_for_scalar.sem, k.banks_for_scalar.take())
            act.activation(self.o[:, t, h * RET_V:(h + 1) * RET_V], k.bank[:, i % NB, :],
                                            ACT.Copy).then_inc(k.scalar_for_tensor.sem, k.scalar_for_tensor.send())
        act.drain().then_inc(k.scalar_for_vector.sem, k.scalar_for_vector.send())
        take_root(k, act, k.small[:, 80:88])

    def vector(self, dve):
        k = self.k
        dve.wait_ge(k.scalar_for_vector.sem, k.scalar_for_vector.take())
        o = [self.o[:, t, h * RET_V:(h + 1) * RET_V] for t, h in self.jobs]
        moments(k, dve, o, k.small[:, 16:64], k.small[:, 64:80], k.small[:, 80:88], EPS)
        for i in range(len(o)):
            ins = dve.tensor_scalar(o[i], o[i], k.small[:, 64 + 2 * i:65 + 2 * i], k.small[:, 80 + i:81 + i],
                                    ALU.subtract, ALU.mult)
        ins.then_inc(k.dve_step, 1)
        dve.wait_ge(k.dve_step, k.step("dve"))
        for t in range(TT):
            dve.tensor_tensor(self.g[:, t, :], self.o[:, t, :], self.g[:, t, :], ALU.mult)


def ret_decay():
    g = 1.0 - 2.0 ** (-5.0 - np.arange(RET_HEADS))
    key = np.arange(P)[:, None, None, None] + P * np.arange(TT)[None, None, :, None]
    d = np.arange(S)[None, None, None, :] - key
    w = np.where(d >= 0, g[None, :, None, None] ** np.maximum(d, 0), 0.0) * RET_QK ** -0.5
    return w.reshape(P, -1).astype(np.float32)



PEER_HEADS, N_KEYS, TOP = 8, 128, 16
PAIRS = PEER_HEADS * TOP
HALF = N_KEYS // 2


class KeyScores(Stage):

    def __init__(self, k, q_t, dst):
        super().__init__(k)
        self.q_t, self.dst = q_t, dst
        self.s = k.slots(1)
        self.fills = [(t, g) for t in range(TT) for g in range(2 * PEER_HEADS // 4)]

    def tensor(self, pe):
        k = self.k
        pe.wait_ge(k.slot_landed[(self.s) % RING], k.loads(self.s))
        for i, (t, g) in enumerate(self.fills):
            if i >= NB:
                read = k.vector_for_tensor if i % 2 == 0 else k.scalar_for_tensor
                pe.wait_ge(read.sem, read.take())
            for j in range(4):
                hs = 4 * g + j
                mm = k.mm(k.bank[:, i % NB, j * P:(j + 1) * P], self.q_t[:, hs, t * P:(t + 1) * P],
                          k.slot(self.s)[:, hs * P:(hs + 1) * P], start=True, stop=True, last=True)
            done = k.banks_for_vector if i % 2 == 0 else k.banks_for_scalar
            mm.then_inc(done.sem, done.send())
        k.slots_through()
        k.vector_for_tensor.skip(NB // 2)
        k.scalar_for_tensor.skip(NB // 2)

    def vector(self, dve):
        k = self.k
        for i in range(0, len(self.fills), 2):
            t, g = self.fills[i]
            dve.wait_ge(k.banks_for_vector.sem, k.banks_for_vector.take())
            dve.tensor_copy(self.dst[:, t, g * 512:(g + 1) * 512], k.bank[:, i % NB, :]).then_inc(k.vector_for_tensor.sem, k.vector_for_tensor.send())

    def scalar(self, act):
        k = self.k
        for i in range(1, len(self.fills), 2):
            t, g = self.fills[i]
            act.wait_ge(k.banks_for_scalar.sem, k.banks_for_scalar.take())
            act.activation(self.dst[:, t, g * 512:(g + 1) * 512], k.bank[:, i % NB, :],
                                            ACT.Copy).then_inc(k.scalar_for_tensor.sem, k.scalar_for_tensor.send())


def top16(k, dve, rows, values, index):
    for r, v in zip(rows, values):
        ins = dve.max(v[:, 0:8], r)
    ins.then_inc(k.dve_step, 1)
    dve.wait_ge(k.dve_step, k.step("dve"))
    for r, v, i in zip(rows, values, index):
        ins = dve.max_index(i[:, 0:8], v[:, 0:8], r)
    ins.then_inc(k.dve_step, 1)
    dve.wait_ge(k.dve_step, k.step("dve"))
    for r, v in zip(rows, values):
        ins = dve.match_replace(r, v[:, 0:8], r, NEG)
    ins.then_inc(k.dve_step, 1)
    dve.wait_ge(k.dve_step, k.step("dve"))
    for r, v in zip(rows, values):
        ins = dve.max(v[:, 8:16], r)
    ins.then_inc(k.dve_step, 1)
    dve.wait_ge(k.dve_step, k.step("dve"))
    for r, v, i in zip(rows, values, index):
        ins = dve.max_index(i[:, 8:16], v[:, 8:16], r)
    ins.then_inc(k.dve_step, 1)
    dve.wait_ge(k.dve_step, k.step("dve"))


class Route(Stage):

    def __init__(self, k, scores, room, out):
        super().__init__(k)
        self.scores, self.out = scores, out
        nk = 2 * PEER_HEADS * TOP
        self.val, self.idx, self.idf = room(TT, nk), room(TT, nk), room(TT, nk)
        self.cand = room(TT, PEER_HEADS * TOP * TOP)
        self.hot = room(PAIRS * TOP)
        self.best, self.at, self.a, self.b = (room(TT, PAIRS) for _ in range(4))
        self.sum = room(TT * PEER_HEADS)

    def scalar(self, act):
        k = self.k
        act.wait_ge(k.vector_for_scalar.sem, k.vector_for_scalar.take())
        act.activation(self.out[:, 2, :], self.best, ACT.Exp).then_inc(k.scalar_for_vector.sem, k.scalar_for_vector.send())

    def vector(self, dve):
        k = self.k
        idx, at = self.idx.bitcast(U32), self.at.bitcast(U32)
        rows = [self.scores[:, t, i * N_KEYS:(i + 1) * N_KEYS] for t in range(TT) for i in range(2 * PEER_HEADS)]
        cut = lambda b: [b[:, t, i * TOP:(i + 1) * TOP] for t in range(TT) for i in range(2 * PEER_HEADS)]
        top16(k, dve, rows, cut(self.val), cut(idx))
        dve.tensor_copy(self.idf, idx).then_inc(k.dve_step, 1)
        dve.wait_ge(k.dve_step, k.step("dve"))
        side = lambda b, t, s: b[:, t, :].rearrange("p (h s j) -> p h s j", s=2, j=TOP)[:, :, s, :]
        full = [P, PEER_HEADS, TOP, TOP]
        for t in range(TT):
            cand = self.cand[:, t, :].rearrange("p (h a b) -> p h a b", a=TOP, b=TOP)
            ins = dve.tensor_tensor(cand, side(self.val, t, 0).unsqueeze(3).to_broadcast(full),
                                    side(self.val, t, 1).unsqueeze(2).to_broadcast(full), ALU.add)
        ins.then_inc(k.dve_step, 1)
        dve.wait_ge(k.dve_step, k.step("dve"))
        rows = [self.cand[:, t, h * 256:(h + 1) * 256] for t in range(TT) for h in range(PEER_HEADS)]
        cut = lambda b: [b[:, t, h * TOP:(h + 1) * TOP] for t in range(TT) for h in range(PEER_HEADS)]
        top16(k, dve, rows, cut(self.best), cut(at))
        a, b = self.a.bitcast(U32), self.b.bitcast(U32)
        dve.tensor_single_scalar(a, at, 4, ALU.logical_shift_right)
        dve.tensor_single_scalar(b, at, 15, ALU.bitwise_and).then_inc(k.dve_step, 1)
        dve.wait_ge(k.dve_step, k.step("dve"))
        dve.tensor_copy(self.a, a)
        dve.tensor_copy(self.b, b).then_inc(k.dve_step, 1)
        dve.wait_ge(k.dve_step, k.step("dve"))
        best = self.best.rearrange("p t (h j) -> p (t h) j", j=TOP)
        n = [P, TT * PEER_HEADS, TOP]
        dve.tensor_copy(self.sum, best[:, :, 0]).then_inc(k.dve_step, 1)
        dve.wait_ge(k.dve_step, k.step("dve"))
        dve.tensor_tensor(best, best, self.sum.unsqueeze(2).to_broadcast(n), ALU.subtract).then_inc(k.vector_for_scalar.sem, k.vector_for_scalar.send())
        hot = self.hot.rearrange("p (m j) -> p m j", j=TOP)
        hot4 = self.hot.rearrange("p (h m j) -> p h m j", m=TOP, j=TOP)
        for s, place in ((0, self.a), (1, self.b)):
            for t in range(TT):
                dve.tensor_tensor(hot, place[:, t, :].unsqueeze(2).to_broadcast([P, PAIRS, TOP]),
                                             k.c("iota")[:, 0:TOP].unsqueeze(1).to_broadcast([P, PAIRS, TOP]),
                                             ALU.is_equal).then_inc(k.dve_step, 1)
                dve.wait_ge(k.dve_step, k.step("dve"))
                dve.tensor_tensor(hot4, hot4, side(self.idf, t, s).unsqueeze(2).to_broadcast(full),
                                             ALU.mult).then_inc(k.dve_step, 1)
                dve.wait_ge(k.dve_step, k.step("dve"))
                dve.tensor_reduce(self.out[:, s, t * PAIRS:(t + 1) * PAIRS], hot, AX, ALU.add).then_inc(k.dve_step, 1)
                dve.wait_ge(k.dve_step, k.step("dve"))
        dve.wait_ge(k.scalar_for_vector.sem, k.scalar_for_vector.take())
        gate = self.out[:, 2, :].rearrange("p (m j) -> p m j", j=TOP)
        dve.tensor_reduce(self.sum, gate, AX, ALU.add).then_inc(k.dve_step, 1)
        dve.wait_ge(k.dve_step, k.step("dve"))
        dve.reciprocal(self.sum, self.sum).then_inc(k.dve_step, 1)
        dve.wait_ge(k.dve_step, k.step("dve"))
        dve.tensor_tensor(gate, gate, self.sum.unsqueeze(2).to_broadcast(n), ALU.mult)


TOKENS_AT_ONCE = BANK // HALF
POOL_TOKENS = 2
HOT_RING = 2 * TOKENS_AT_ONCE


class SpreadGates(Stage):

    def __init__(self, k, half, pairs, gates, hot1, hot2):
        super().__init__(k)
        self.half, self.pairs, self.gates, self.hot1, self.hot2 = half, pairs, gates, hot1, hot2
        self.fills = S // TOKENS_AT_ONCE
        self.before = k.gate_fills
        k.gate_fills += self.fills

    def tensor(self, pe):
        k = self.k
        for f in range(self.fills):
            if f >= NB:
                read = k.vector_for_tensor if f % 2 == 0 else k.scalar_for_tensor
                pe.wait_ge(read.sem, read.take())
            pe.wait_ge(k.gpsimd_for_tensor.sem, k.gpsimd_for_tensor.take())
            pe.wait_ge(k.gate_onehots_for_tensor.sem, k.gate_onehots_for_tensor.take())
            for j in range(TOKENS_AT_ONCE):
                r = (f * TOKENS_AT_ONCE + j) % HOT_RING
                mm = k.mm(k.bank[:, f % NB, j * HALF:(j + 1) * HALF], self.hot2[:, r, :], self.hot1[:, r, :],
                          start=True, stop=True, last=True)
            done = k.banks_for_vector if f % 2 == 0 else k.banks_for_scalar
            mm.then_inc(done.sem, done.send())
            pe.drain().then_inc(k.tensor_for_gpsimd.sem, k.tensor_for_gpsimd.send())
        (k.vector_for_tensor).skip(NB // 2)
        (k.scalar_for_tensor).skip(NB // 2)

    def gpsimd(self, pool):
        k = self.k
        for f in range(self.fills):
            if f >= 2:
                pool.wait_ge(k.tensor_for_gpsimd.sem, k.tensor_for_gpsimd.take())
            for j in range(POOL_TOKENS):
                t = f * TOKENS_AT_ONCE + j
                ins = pool.tensor_scalar(self.hot2[:, t % HOT_RING, :], k.c("iota"), self.pairs[:, 1, t:t + 1],
                                         None, ALU.is_equal)
            ins.then_inc(k.gpsimd_for_tensor.sem, k.gpsimd_for_tensor.send())
        k.tensor_for_gpsimd.skip(2)

    def vector(self, dve):
        k = self.k
        first = k.c("iota")[:, self.half * HALF:(self.half + 1) * HALF]

        def evacuate(f):
            if f % 2 == 0:
                dve.wait_ge(k.banks_for_vector.sem, k.banks_for_vector.take())
                dve.tensor_copy(*self.piece(f)).then_inc(k.vector_for_tensor.sem, k.vector_for_tensor.send())

        for f in range(self.fills):
            if f >= 2:
                evacuate(f - 2)
            if f >= 2:
                dve.wait_ge(k.tensor_for_gpsimd.sem, self.before + f - 1)
            for j in range(POOL_TOKENS, TOKENS_AT_ONCE):
                t = f * TOKENS_AT_ONCE + j
                dve.tensor_scalar(self.hot2[:, t % HOT_RING, :], k.c("iota"), self.pairs[:, 1, t:t + 1], None,
                                  ALU.is_equal)
            for j in range(TOKENS_AT_ONCE):
                t = f * TOKENS_AT_ONCE + j
                ins = dve.tensor_scalar(self.hot1[:, t % HOT_RING, :], first, self.pairs[:, 0, t:t + 1],
                                        self.pairs[:, 2, t:t + 1], ALU.is_equal, ALU.mult)
            ins.then_inc(k.gate_onehots_for_tensor.sem, k.gate_onehots_for_tensor.send())
        evacuate(self.fills - 2)
        evacuate(self.fills - 1)

    def piece(self, f):
        n = TOKENS_AT_ONCE
        return (self.gates[:, :, f * n:(f + 1) * n],
                self.k.bank[:, f % NB, :].rearrange("p (t i) -> p i t", t=n))

    def scalar(self, act):
        k = self.k
        for f in range(1, self.fills, 2):
            act.wait_ge(k.banks_for_scalar.sem, k.banks_for_scalar.take())
            act.activation(*self.piece(f), ACT.Copy).then_inc(k.scalar_for_tensor.sem, k.scalar_for_tensor.send())



class Scores(Stage):

    def __init__(self, k, jobs, top, total, keep=None, extra_slots=0):
        super().__init__(k)
        self.jobs, self.top, self.total, self.keep = jobs, top, total, keep
        self.extra = extra_slots
        self.s = k.slots(extra_slots) if extra_slots else None

    def tensor(self, pe):
        k = self.k
        if self.extra:
            pe.wait_ge(k.slot_landed[(self.s) % RING], k.loads(self.s))
        for i, (product, n, how, p) in enumerate(self.jobs):
            if i >= NB:
                pe.wait_ge(k.vector_for_tensor.sem, k.vector_for_tensor.take())
            product(k.bank[:, i % NB, 0:n]).then_inc(k.banks_for_vector.sem, k.banks_for_vector.send())
        k.vector_for_tensor.skip(NB)
        k.slots_through(self.extra)

    def vector(self, dve):
        k = self.k
        n_jobs = len(self.jobs)
        begun = []

        def row_max(i):
            n, p = self.jobs[i][1], self.jobs[i][3]
            dve.wait_ge(k.vector_for_tensor.sem, begun[i])
            dve.tensor_reduce(self.top[:, i:i + 1], p, AX, ALU.max, negate=True).then_inc(k.vector_for_scalar.sem, k.vector_for_scalar.send())

        for i, (product, n, how, p) in enumerate(self.jobs):
            dve.wait_ge(k.banks_for_vector.sem, k.banks_for_vector.take())
            how(dve, p, k.bank[:, i % NB, 0:n]).then_inc(k.vector_for_tensor.sem, k.vector_for_tensor.send())
            begun.append(k.vector_for_tensor.sent)
            if i >= 1:
                row_max(i - 1)
        row_max(n_jobs - 1)
        dve.wait_ge(k.scalar_for_vector.sem, k.scalar_for_vector.take())
        if self.keep is not None:
            for i, (product, n, how, p) in enumerate(self.jobs):
                ins = dve.tensor_tensor(p, p, self.keep(i), ALU.mult)
        dve.reciprocal(self.total[:, 0:n_jobs], self.total[:, 0:n_jobs])

    def scalar(self, act):
        k = self.k
        for i, (product, n, how, p) in enumerate(self.jobs):
            act.wait_ge(k.vector_for_scalar.sem, k.vector_for_scalar.take())
            act.activation(p, p, ACT.Exp, bias=self.top[:, i:i + 1], accum_out=self.total[:, i:i + 1])
        act.drain().then_inc(k.scalar_for_vector.sem, k.scalar_for_vector.send())


class Values(Stage):

    def __init__(self, k, jobs, add, width=64):
        super().__init__(k)
        self.jobs, self.add, self.w = jobs, add, width
        self.per = BANK // width

    def tensor(self, pe):
        k = self.k
        for i, (p_t, v, factor, out) in enumerate(self.jobs):
            f, j = i // self.per, i % self.per
            if j == 0 and f >= NB:
                pe.wait_ge(k.vector_for_tensor.sem, k.vector_for_tensor.take())
            for a, (lhs, rhs) in enumerate(zip(p_t, v)):
                mm = k.mm(k.bank[:, f % NB, j * self.w:(j + 1) * self.w], lhs, rhs, start=a == 0,
                          stop=a == len(v) - 1, last=True)
            if j == self.per - 1:
                mm.then_inc(k.banks_for_vector.sem, k.banks_for_vector.send())
        fills = len(self.jobs) // self.per
        k.vector_for_tensor.skip(min(NB, fills))

    def vector(self, dve):
        k = self.k
        for i, (p_t, v, factor, out) in enumerate(self.jobs):
            f, j = i // self.per, i % self.per
            if j == 0:
                dve.wait_ge(k.banks_for_vector.sem, k.banks_for_vector.take())
            src = k.bank[:, f % NB, j * self.w:(j + 1) * self.w]
            if self.add:
                ins = dve.scalar_tensor_tensor(out, src, factor, out, ALU.mult, ALU.add)
            else:
                ins = dve.tensor_scalar(out, src, factor, None, ALU.mult)
            if j == self.per - 1:
                ins.then_inc(k.vector_for_tensor.sem, k.vector_for_tensor.send())


def weight_blocks(p0, p1, heads):
    return [(t, h, p0[:, h, :] if t == 0 else p1[:, h, :]) for t in range(TT) for h in range(heads)]


def turned_blocks(k, p, p_t, n):
    return Turn(k, [([p[:, i + j, :] for j in range(4)], p_t[:, i:i + 4, :]) for i in range(0, n, 4)])


def causal_attention(k, heads, q, kt, v, product_extra, how, p, p_t, top, total, factor, out, add,
                     extra_slots=0):
    jobs, value_jobs = [], []
    for t in range(TT):
        for h in range(heads):
            n = (t + 1) * P
            b = h if t == 0 else heads + 2 * h
            dst = p[:, b:b + t + 1, :].rearrange("p a b -> p (a b)")

            def product(bank, t=t, h=h, n=n):
                mm = k.mm(bank, q(h)[:, t * P:(t + 1) * P], kt(h)[:, 0:n], start=True,
                          stop=product_extra is None, last=True)
                return mm if product_extra is None else product_extra(bank, t, h, n)

            jobs.append((product, n, how(t, h, n), dst))
            value_jobs.append(([p_t[:, b + a, :] for a in range(t + 1)], [v(h, a) for a in range(t + 1)],
                               factor[:, t * heads + h:t * heads + h + 1], out[:, t, h * HD:(h + 1) * HD]))
    scores = Scores(k, jobs, top, total, extra_slots=extra_slots)
    return [scores, turned_blocks(k, p, p_t, 3 * heads), Values(k, value_jobs, add)]



CMP, STRIDE, CMP_HIDDEN = 32, 16, 256


class Compress(Stage):

    def __init__(self, k, raw, couples, hidden, keys, values, extra):
        super().__init__(k)
        self.raw, self.hidden, self.keys, self.values, self.extra = raw, hidden, keys, values, extra
        self.couples = couples
        self.sp = k.slots(1)
        self.s = k.slots(2 * CMP // 16)

    def tensor(self, pe):
        k = self.k
        extra, blocks = self.extra, NSA_GROUPS * N_CMP
        pe.wait_ge(k.vector_for_tensor.sem, k.vector_for_tensor.take())
        k.slots_through()
        pe.wait_ge(k.couples_made, 16 * 4)
        for kv in range(2):
            if kv == 1:
                pe.wait_ge(k.scalar_for_tensor.sem, k.scalar_for_tensor.take())
            for m in range(CMP // 2):
                s = self.s + 2 * kv + m // 8
                if m % 8 == 0:
                    pe.wait_ge(k.slot_landed[s % RING], k.loads(s))
                tokens = self.couples[:, NSA_GROUPS * kv:NSA_GROUPS * (kv + 1),
                                      2 * m:2 * m + STRIDE * (N_CMP - 1) + 1:STRIDE]
                for hc in range(2):
                    w = k.slot(s)[:, (m % 8) * CMP_HIDDEN + hc * P:(m % 8) * CMP_HIDDEN + (hc + 1) * P]
                    dst = k.acc[:, hc, 0:blocks].rearrange("p (g n) -> p g n", n=N_CMP)
                    k.mm(dst, w, tokens, start=m == 0, stop=m == CMP // 2 - 1)
                    at = CMP // 2 * kv + m
                    mm = k.mm(k.bank[:, hc, 0:1], w, extra[:, at:at + 1], start=m == 0, stop=m == CMP // 2 - 1,
                              last=True)
                if m == CMP // 2 - 1:
                    mm.then_inc(k.banks_for_vector.sem, k.banks_for_vector.send())
                if m % 8 == 7:
                    k.slots_through()
            pe.wait_ge(k.scalar_for_tensor.sem, k.scalar_for_tensor.take())
            if kv == 0:
                for hc in range(2):
                    mm = k.mm(k.bank[:, 2, 0:NSA_GROUPS * N_CMP], extra[:, CMP + hc * P:CMP + (hc + 1) * P],
                              self.hidden[:, hc, :], start=hc == 0, stop=hc == 1, last=True)
            else:
                for g in range(NSA_GROUPS):
                    for hc in range(2):
                        mm = k.mm(k.bank[0:N_CMP, 3, g * HD:(g + 1) * HD],
                                  self.hidden[:, hc, g * N_CMP:(g + 1) * N_CMP],
                                  extra[:, CMP + 2 * P + hc * HD:CMP + 2 * P + (hc + 1) * HD], start=hc == 0, stop=hc == 1, last=True)
            mm.then_inc(k.banks_for_vector.sem, k.banks_for_vector.send())

    def vector(self, dve):
        k = self.k
        bias = k.small[:, 16:18]
        dve.wait_ge(k.slot_landed[(self.sp) % RING], k.loads(self.sp))
        dve.tensor_copy(self.extra, k.slot(self.sp)[:, 0:CMP + 2 * P + 2 * HD]).then_inc(k.vector_for_tensor.sem, k.vector_for_tensor.send())
        for kv in range(2):
            dve.wait_ge(k.banks_for_vector.sem, k.banks_for_vector.take())
            dve.tensor_copy(bias, k.bank[:, 0:2, 0]).then_inc(k.vector_for_scalar.sem, k.vector_for_scalar.send())
            dve.wait_ge(k.banks_for_vector.sem, k.banks_for_vector.take())
            if kv == 0:
                dve.tensor_copy(self.keys, k.bank[:, 2, 0:NSA_GROUPS * N_CMP]).then_inc(k.dve_step, 1)
                dve.wait_ge(k.dve_step, k.step("dve"))
            else:
                dve.tensor_copy(self.values, k.bank[0:N_CMP, 3, 0:NSA_GROUPS * HD])

    def scalar(self, act):
        k = self.k
        couples = self.couples.rearrange("p (c s) t -> p c s t", s=2)
        for side in range(2):
            raw = self.raw[64 * side:64 * side + 64, :, :]
            act.dma_start(couples[0:64, :, side, :], raw).then_inc(k.couples_made, 16)
            act.dma_start(couples[64:P, :, side, 0:S - 1], raw[:, :, 1:S]).then_inc(k.couples_made, 16)
        for kv in range(2):
            act.wait_ge(k.vector_for_scalar.sem, k.vector_for_scalar.take())
            for hc in range(2):
                ins = act.activation(self.hidden[:, hc, :], k.acc[:, hc, 0:NSA_GROUPS * N_CMP],
                                     ACT.Gelu_apprx_tanh, bias=k.small[:, 16 + hc:17 + hc])
            ins.then_inc(k.scalar_for_tensor.sem, k.scalar_for_tensor.send())
            if kv == 0:
                act.drain().then_inc(k.scalar_for_tensor.sem, k.scalar_for_tensor.send())


class Gates(Stage):

    def __init__(self, k, factor, gates, total, branch):
        super().__init__(k)
        self.factor, self.gates, self.total, self.branch = factor, gates, total, branch

    def vector(self, dve):
        g = self.gates.rearrange("p t (h b) -> p t h b", b=3)[:, :, :, self.branch]
        for t in range(TT):
            a = slice(t * NSA_HEADS, (t + 1) * NSA_HEADS)
            dve.tensor_tensor(self.factor[:, a], g[:, t, :], self.total[:, a], ALU.mult)



FOX_HEADS = 16


class HeadNorm(Stage):

    def __init__(self, k, qk, squares):
        super().__init__(k)
        self.qk, self.squares = qk, squares
        self.s = k.slots(1)
        self.n = 2 * FOX_HEADS

    def scalar(self, act):
        take_root(self.k, act, self.k.small[:, 16:16 + TT * self.n])

    def tensor(self, pe):
        pe.wait_ge(self.k.vector_for_tensor.sem, self.k.vector_for_tensor.take())
        self.k.slots_through()

    def vector(self, dve):
        k, n = self.k, self.n
        stat = k.small[:, 16:16 + TT * n]
        for t in range(TT):
            ins = dve.tensor_tensor(self.squares[:, t, :], self.qk[:, t, :], self.qk[:, t, :], ALU.mult)
        ins.then_inc(k.dve_step, 1)
        dve.wait_ge(k.dve_step, k.step("dve"))
        dve.tensor_reduce(stat, self.squares.rearrange("p t (h d) -> p (t h) d", d=HD), AX, ALU.add).then_inc(k.dve_step, 1)
        dve.wait_ge(k.dve_step, k.step("dve"))
        inverse_root(k, dve, dve.tensor_scalar(stat, stat, 1.0 / HD, EPS, ALU.mult, ALU.add), stat)
        for t in range(TT):
            ins = dve.tensor_scalar(stat[:, t * n:t * n + n // 2], stat[:, t * n:t * n + n // 2], HD ** -0.5, None,
                                    ALU.mult)
        ins.then_inc(k.dve_step, 1)
        dve.wait_ge(k.dve_step, k.step("dve"))
        dve.wait_ge(k.slot_landed[(self.s) % RING], k.loads(self.s))
        for t in range(TT):
            heads = self.qk[:, t, :].rearrange("p (h d) -> p h d", d=HD)
            ins = dve.tensor_tensor(heads, heads, stat[:, t * n:(t + 1) * n].unsqueeze(2).to_broadcast([P, n, HD]),
                                    ALU.mult)
        ins.then_inc(k.dve_step, 1)
        dve.wait_ge(k.dve_step, k.step("dve"))
        for t in range(TT):
            ins = dve.tensor_tensor(self.qk[:, t, :], self.qk[:, t, :], k.slot(self.s)[:, 0:SLOT], ALU.mult)
        ins.then_inc(k.vector_for_tensor.sem, k.vector_for_tensor.send())


def log_sigmoid(k, act, z, b):
    act.wait_ge(k.vector_for_scalar.sem, k.vector_for_scalar.take())
    act.activation(b, z, ACT.Abs).then_inc(k.act_step, 1)
    act.wait_ge(k.act_step, k.step("act"))
    act.activation(b, b, ACT.Exp, scale=-1.0).then_inc(k.act_step, 1)
    act.wait_ge(k.act_step, k.step("act"))
    act.activation(b, b, ACT.Ln, bias=1.0).then_inc(k.scalar_for_vector.sem, k.scalar_for_vector.send())


class ForgetGates(Stage):

    def __init__(self, k, z, lf, tmp, c, c_t):
        super().__init__(k)
        self.z, self.lf, self.tmp, self.c, self.c_t = z, lf, tmp, c, c_t
        self.s = k.slots(1)

    def scalar(self, act):
        log_sigmoid(self.k, act, self.z, self.tmp)

    def vector(self, dve):
        k, H = self.k, FOX_HEADS
        dve.wait_ge(k.slot_landed[(self.s) % RING], k.loads(self.s))
        for t in range(TT):
            ins = dve.tensor_tensor(self.z[:, t, :], self.z[:, t, :], k.slot(self.s)[:, 0:H], ALU.add)
        ins.then_inc(k.vector_for_scalar.sem, k.vector_for_scalar.send())
        dve.wait_ge(k.scalar_for_vector.sem, k.scalar_for_vector.take())
        dve.scalar_tensor_tensor(self.lf, self.z, 0.0, self.tmp, ALU.min, ALU.subtract).then_inc(k.vector_for_tensor.sem, k.vector_for_tensor.send())
        dve.wait_ge(k.banks_for_vector.sem, k.banks_for_vector.take())
        dve.tensor_copy(self.c, k.bank[:, 0, 0:TT * H].rearrange("p (t h) -> p t h", t=TT))
        dve.tensor_copy(self.c_t, k.bank[0:H, 1, 0:S])

    def tensor(self, pe):
        k, H = self.k, FOX_HEADS
        pe.wait_ge(k.vector_for_tensor.sem, k.vector_for_tensor.take())
        tri = k.c("causal_t").rearrange("p (t q) -> p t q", t=TT)
        for t in range(TT):
            for a in range(t + 1):
                k.mm(k.bank[:, 0, t * H:(t + 1) * H], tri[:, a, t * P:(t + 1) * P], self.lf[:, a, :],
                     start=a == 0, stop=a == t, last=True)
        for a in range(TT):
            mm = k.mm(k.bank[0:H, 1, 0:S], self.lf[:, a, :], tri[:, a, :], start=a == 0, stop=a == TT - 1, last=True)
        mm.then_inc(k.banks_for_vector.sem, k.banks_for_vector.send())
        k.slots_through()


def pick_head():
    out = np.zeros((FOX_HEADS, FOX_HEADS, P), np.float32)
    for h in range(FOX_HEADS):
        out[h, h] = -1.0
    return out.reshape(FOX_HEADS, -1)


class Keep(Stage):

    def __init__(self, k, dst):
        super().__init__(k)
        self.dst = dst
        self.n = -(-dst.shape[1] // SLOT)
        self.s = k.slots(self.n)

    def vector(self, dve):
        k = self.k
        for j in range(self.n):
            dve.wait_ge(k.slot_landed[(self.s + j) % RING], k.loads(self.s + j))
            end = min((j + 1) * SLOT, self.dst.shape[1])
            dve.tensor_copy(self.dst[:, j * SLOT:end], k.slot(self.s + j)[:, 0:end - j * SLOT]).then_inc(k.vector_for_tensor.sem, k.vector_for_tensor.send())

    def tensor(self, pe):
        k = self.k
        for j in range(self.n):
            pe.wait_ge(k.vector_for_tensor.sem, k.vector_for_tensor.take())
        k.slots_through(self.n)



CONV, TAPS, PAD = 512, 31, 30
GLA_HEADS, GLA_DV = 4, 128
SUB = 16
N_SUB = S // SUB
CLAMP = 70.0


class Convolve(Stage):

    def __init__(self, k, feat, u, y, w, b):
        super().__init__(k)
        self.feat, self.u, self.y, self.w, self.b = feat, u, y, w, b
        self.own_slots = 0

    def scalar_beside(self, act):
        self.scalar(act)

    def scalar(self, act):
        gate = self.feat[:, 4:8, :]
        act.activation(gate, gate, ACT.Sigmoid).then_inc(self.k.scalar_for_vector.sem, self.k.scalar_for_vector.send())

    def vector(self, dve):
        k = self.k
        dve.memset(self.u[:, :, 0:PAD], 0.0)
        dve.wait_ge(k.scalar_for_vector.sem, k.scalar_for_vector.take())
        dve.tensor_tensor(self.u[:, :, PAD:], self.feat[:, 0:4, :], self.feat[:, 4:8, :], ALU.mult).then_inc(k.dve_step, 1)
        dve.wait_ge(k.dve_step, k.step("dve"))
        n = CONV // P
        for tap in range(TAPS):
            for c in range(n):
                src, w = self.u[:, c, tap:tap + S], self.w[:, c * TAPS + tap:c * TAPS + tap + 1]
                if tap == 0:
                    ins = dve.tensor_scalar(self.y[:, c, :], src, w, self.b[:, c:c + 1], ALU.mult, ALU.add)
                else:
                    dve.wait_ge(k.dve_step, k.steps["dve"] - n + 1)
                    ins = dve.scalar_tensor_tensor(self.y[:, c, :], src, w, self.y[:, c, :], ALU.mult, ALU.add)
                ins.then_inc(k.dve_step, 1)
                k.steps["dve"] += 1


class ConvNorm(Stage):

    def __init__(self, k, y, out, g, b):
        super().__init__(k)
        self.y, self.out, self.g, self.b = y, out, g, b

    def scalar(self, act):
        k = self.k
        take_root(k, act, k.small[:, 80:82])
        act.wait_ge(k.vector_for_scalar.sem, k.vector_for_scalar.take())
        for t in range(TT):
            act.activation(self.out[:, t, :], self.y[:, t, :], ACT.Silu)

    def vector(self, dve):
        k = self.k
        layer_norm(k, dve, self.y, self.g, self.b)
        dve.drain().then_inc(k.vector_for_scalar.sem, k.vector_for_scalar.send())


def layer_norm(k, dve, y, g, b):
    moments(k, dve, [y[:, t, :] for t in range(TT)], k.small[:, 16:28], k.small[:, 64:68], k.small[:, 80:82], EPS)
    for t in range(TT):
        ins = dve.tensor_scalar(y[:, t, :], y[:, t, :], k.small[:, 64 + 2 * t:65 + 2 * t],
                                k.small[:, 80 + t:81 + t], ALU.subtract, ALU.mult)
    ins.then_inc(k.dve_step, 1)
    dve.wait_ge(k.dve_step, k.step("dve"))
    for op, row in ((ALU.mult, g), (ALU.add, b)):
        for t in range(TT):
            ins = dve.tensor_tensor(y[:, t, :], y[:, t, :], row, op)
        ins.then_inc(k.dve_step, 1)
        dve.wait_ge(k.dve_step, k.step("dve"))


class GlaDecays(Stage):

    def __init__(self, k, w_low, w2, bias, low, z, tmp, b_t):
        super().__init__(k)
        self.w_low, self.w2, self.bias, self.low, self.z, self.tmp, self.b_t = w_low, w2, bias, low, z, tmp, b_t

    def tensor(self, pe):
        k = self.k
        for kk in range(DC):
            mm = k.mm(k.bank[0:16, 0, 0:S], self.w_low[:, kk * 16:(kk + 1) * 16], k.h_t[:, kk, :], start=kk == 0,
                      stop=kk == DC - 1, last=True)
        mm.then_inc(k.banks_for_vector.sem, k.banks_for_vector.send())
        pe.wait_ge(k.vector_for_tensor.sem, k.vector_for_tensor.take())
        for t in range(TT):
            mm = k.mm(k.bank[:, 1, t * S:(t + 1) * S], self.low[:, t * P:(t + 1) * P], self.w2, start=True,
                      stop=True, last=True)
        mm.then_inc(k.banks_for_vector.sem, k.banks_for_vector.send())
        pe.wait_ge(k.vector_for_tensor.sem, k.vector_for_tensor.take())
        tri = k.c("causal_t").rearrange("p (t q) -> p t q", t=TT)
        for hp in range(2):
            for a in range(TT):
                mm = k.mm(k.bank[:, 2, hp * S:(hp + 1) * S], self.z[:, a, hp * P:(hp + 1) * P], tri[:, a, :],
                          start=a == 0, stop=a == TT - 1, last=True)
        mm.then_inc(k.banks_for_vector.sem, k.banks_for_vector.send())

    def scalar(self, act):
        log_sigmoid(self.k, act, self.z, self.tmp)

    def vector(self, dve):
        k = self.k
        dve.wait_ge(k.banks_for_vector.sem, k.banks_for_vector.take())
        dve.tensor_copy(self.low, k.bank[0:16, 0, 0:S]).then_inc(k.vector_for_tensor.sem, k.vector_for_tensor.send())
        dve.wait_ge(k.banks_for_vector.sem, k.banks_for_vector.take())
        for t in range(TT):
            ins = dve.tensor_tensor(self.z[:, t, :], k.bank[:, 1, t * S:(t + 1) * S], self.bias, ALU.add)
        ins.then_inc(k.vector_for_scalar.sem, k.vector_for_scalar.send())
        dve.wait_ge(k.scalar_for_vector.sem, k.scalar_for_vector.take())
        dve.scalar_tensor_tensor(self.z, self.z, 0.0, self.tmp, ALU.min, ALU.subtract).then_inc(k.dve_step, 1)
        dve.wait_ge(k.dve_step, k.step("dve"))
        dve.tensor_scalar(self.z, self.z, 1.0 / 16.0, None, ALU.mult).then_inc(k.vector_for_tensor.sem, k.vector_for_tensor.send())
        dve.wait_ge(k.banks_for_vector.sem, k.banks_for_vector.take())
        dve.tensor_copy(self.b_t, k.bank[:, 2, :].rearrange("p (a b) -> p a b", a=2))


class GlaScale(Stage):

    def __init__(self, k, q_t, k_t, b_t, ref, q_s, k_a, k_b):
        super().__init__(k)
        self.q_t, self.k_t, self.b_t, self.ref, self.q_s, self.k_a, self.k_b = q_t, k_t, b_t, ref, q_s, k_a, k_b

    def scalar(self, act):
        k = self.k
        act.wait_ge(k.vector_for_scalar.sem, k.vector_for_scalar.take())
        act.activation(self.q_s, self.q_s, ACT.Exp).then_inc(k.scalar_for_vector.sem, k.scalar_for_vector.send())
        for hp in range(2):
            for dst in (self.k_a, self.k_b):
                act.wait_ge(k.vector_for_scalar.sem, k.vector_for_scalar.take())
                act.activation(dst[:, hp], dst[:, hp], ACT.Exp).then_inc(k.scalar_for_vector.sem, k.scalar_for_vector.send())

    def vector(self, dve):
        k = self.k
        dve.memset(self.ref[:, :, 0:1], 0.0)
        dve.tensor_copy(self.ref[:, :, 1:N_SUB], self.b_t[:, :, SUB - 1:S - 1:SUB]).then_inc(k.dve_step, 1)
        dve.wait_ge(k.dve_step, k.step("dve"))
        cut = lambda b: b.rearrange("p a (n i) -> p a n i", i=SUB)
        dve.tensor_tensor(cut(self.q_s), cut(self.b_t),
                                            self.ref.unsqueeze(3).to_broadcast([P, 2, N_SUB, SUB]), ALU.subtract).then_inc(k.vector_for_scalar.sem, k.vector_for_scalar.send())
        parts = [(hp, dst, kt) for hp in range(2) for dst, kt in ((self.k_a, 0), (self.k_b, 1))]
        for hp, dst, kt in parts:
            blocks = slice(kt * N_SUB // 2, N_SUB)
            n = [P, N_SUB - kt * N_SUB // 2, P]
            dve.tensor_tensor(dst[:, hp], self.ref[:, hp, blocks].unsqueeze(2).to_broadcast(n),
                                         self.b_t[:, hp, kt * P:(kt + 1) * P].unsqueeze(1).to_broadcast(n),
                                         ALU.subtract).then_inc(k.dve_step, 1)
            dve.wait_ge(k.dve_step, k.step("dve"))
            dve.tensor_scalar(dst[:, hp], dst[:, hp], CLAMP, None, ALU.min).then_inc(k.vector_for_scalar.sem, k.vector_for_scalar.send())
        dve.wait_ge(k.scalar_for_vector.sem, k.scalar_for_vector.take())
        dve.scalar_tensor_tensor(self.q_s, self.q_t, HD ** -0.5, self.q_s, ALU.mult, ALU.mult)
        for hp, dst, kt in parts:
            n = [P, N_SUB - kt * N_SUB // 2, P]
            dve.wait_ge(k.scalar_for_vector.sem, k.scalar_for_vector.take())
            dve.tensor_tensor(dst[:, hp], dst[:, hp], self.k_t[:, hp, kt * P:(kt + 1) * P].unsqueeze(1).to_broadcast(n),
                              ALU.mult)


class GlaAttend(Stage):

    def __init__(self, k, q_s, k_a, k_b, w, v, o):
        super().__init__(k)
        self.q_s, self.k_a, self.k_b, self.w, self.v, self.o = q_s, k_a, k_b, w, v, o

    def tensor(self, pe):
        k = self.k
        for h in range(GLA_HEADS):
            base, hp = 64 * (h % 2), h // 2
            for b in range(N_SUB):
                for kt in range(1 + b // (N_SUB // 2)):
                    key = self.k_a[base:base + 64, hp, b, :] if kt == 0 else self.k_b[base:base + 64, hp, b - N_SUB // 2, :]
                    mm = k.mm(k.bank[:, h, kt * S + b * SUB:kt * S + (b + 1) * SUB], key,
                              self.q_s[base:base + 64, hp, b * SUB:(b + 1) * SUB], start=True, stop=True, last=True)
            mm.then_inc(k.banks_for_vector.sem, k.banks_for_vector.send())
        for t in range(TT):
            for h in range(GLA_HEADS):
                if t == 0:
                    pe.wait_ge(k.vector_for_tensor.sem, k.vector_for_tensor.take())
                for a in range(t + 1):
                    mm = k.mm(k.acc[:, t, h * GLA_DV:(h + 1) * GLA_DV], self.w[:, h, a, t * P:(t + 1) * P],
                              self.v[:, a, h * GLA_DV:(h + 1) * GLA_DV], start=a == 0, stop=a == t, last=True)
            mm.then_inc(k.banks_for_scalar.sem, k.banks_for_scalar.send())

    def vector(self, dve):
        k = self.k
        tri = k.c("causal_t").rearrange("p (t q) -> p t q", t=TT)
        for h in range(GLA_HEADS):
            dve.wait_ge(k.banks_for_vector.sem, k.banks_for_vector.take())
            bank = k.bank[:, h, :].rearrange("p (a q) -> p a q", a=TT)
            dve.tensor_tensor(self.w[:, h, 0, :], bank[:, 0, :], tri[:, 0, :], ALU.mult)
            dve.tensor_tensor(self.w[:, h, 1, P:], bank[:, 1, P:], tri[:, 1, P:], ALU.mult).then_inc(k.vector_for_tensor.sem, k.vector_for_tensor.send())

    def scalar(self, act):
        k = self.k
        for t in range(TT):
            act.wait_ge(k.banks_for_scalar.sem, k.banks_for_scalar.take())
            act.activation(self.o[:, t, :], k.acc[:, t, :], ACT.Copy)


class HeadRms(Stage):

    def __init__(self, k, src, out, n, gain, other, squares):
        super().__init__(k)
        self.src, self.out, self.n, self.gain, self.other, self.squares = src, out, n, gain, other, squares
        self.groups = src[0].shape[1] // n

    def scalar(self, act):
        take_root(self.k, act, self.k.small[:, 16:16 + TT * self.groups])

    def vector(self, dve):
        k, G, n = self.k, self.groups, self.n
        stat = k.small[:, 16:16 + TT * G]
        for t in range(TT):
            ins = dve.tensor_tensor(self.squares[t], self.src[t], self.src[t], ALU.mult)
        ins.then_inc(k.dve_step, 1)
        dve.wait_ge(k.dve_step, k.step("dve"))
        for t in range(TT):
            ins = dve.tensor_reduce(stat[:, t * G:(t + 1) * G], self.squares[t].rearrange("p (g n) -> p g n", n=n),
                                    AX, ALU.add)
        ins.then_inc(k.dve_step, 1)
        dve.wait_ge(k.dve_step, k.step("dve"))
        inverse_root(k, dve, dve.tensor_scalar(stat, stat, 1.0 / n, EPS, ALU.mult, ALU.add), stat)
        for t in range(TT):
            for g in range(G):
                a = slice(g * n, (g + 1) * n)
                ins = dve.scalar_tensor_tensor(self.out[t][:, a], self.src[t][:, a], stat[:, t * G + g:t * G + g + 1],
                                               self.gain[:, a], ALU.mult, ALU.mult)
        ins.then_inc(k.dve_step, 1)
        dve.wait_ge(k.dve_step, k.step("dve"))
        if self.other is not None:
            for t in range(TT):
                dve.tensor_tensor(self.out[t], self.out[t], self.other[:, t, :], ALU.mult)



ROPE_HEADS = 8


class Rope(Stage):

    def __init__(self, k, qk, tmp):
        super().__init__(k)
        self.qk, self.tmp = qk, tmp

    def vector(self, dve):
        k, n, half = self.k, 2 * ROPE_HEADS, HD // 2
        shape = [P, n, half]
        for t in range(TT):
            x = self.qk[:, t, :].rearrange("p (h s d) -> p h s d", s=2, d=half)
            cos = k.c("cos")[:, t * half:(t + 1) * half].unsqueeze(1).to_broadcast(shape)
            sin = k.c("sin")[:, t * half:(t + 1) * half].unsqueeze(1).to_broadcast(shape)
            a, b = (self.tmp[:, t, i * n * half:(i + 1) * n * half].rearrange("p (h d) -> p h d", d=half)
                    for i in range(2))
            dve.tensor_tensor(a, x[:, :, 1, :], sin, ALU.mult)
            dve.tensor_tensor(b, x[:, :, 0, :], sin, ALU.mult).then_inc(k.dve_step, 1)
            dve.wait_ge(k.dve_step, k.step("dve"))
            dve.tensor_tensor(x[:, :, 0, :], x[:, :, 0, :], cos, ALU.mult)
            dve.tensor_tensor(x[:, :, 1, :], x[:, :, 1, :], cos, ALU.mult).then_inc(k.dve_step, 1)
            dve.wait_ge(k.dve_step, k.step("dve"))
            dve.tensor_tensor(x[:, :, 0, :], x[:, :, 0, :], a, ALU.subtract)
            dve.tensor_tensor(x[:, :, 1, :], x[:, :, 1, :], b, ALU.add)


class Spatial(Stage):

    def __init__(self, k, u, v, w, b, g, beta, out):
        super().__init__(k)
        self.u, self.v, self.w, self.b, self.g, self.beta, self.out = u, v, w, b, g, beta, out

    def scalar(self, act):
        take_root(self.k, act, self.k.small[:, 80:82])

    def vector(self, dve):
        k = self.k
        layer_norm(k, dve, self.v, self.g, self.beta)
        dve.tensor_tensor(self.w, self.w, k.c("causal_t")[:, 0:P].unsqueeze(1).to_broadcast(
            [P, ROPE_HEADS, P]), ALU.mult).then_inc(k.vector_for_tensor.sem, k.vector_for_tensor.send())
        for t in range(TT):
            dve.wait_ge(k.banks_for_vector.sem, k.banks_for_vector.take())
            for h in range(ROPE_HEADS):
                a = slice(h * HD, (h + 1) * HD)
                dve.scalar_tensor_tensor(self.out[:, t, a], k.bank[:, t, a], self.b[:, h:h + 1], self.u[:, t, a],
                                         ALU.add, ALU.mult)

    def tensor(self, pe):
        k = self.k
        pe.wait_ge(k.vector_for_tensor.sem, k.vector_for_tensor.take())
        for t in range(TT):
            for h in range(ROPE_HEADS):
                mm = k.mm(k.bank[:, t, h * HD:(h + 1) * HD], self.w[:, h, :], self.v[:, t, h * HD:(h + 1) * HD],
                          start=True, stop=True, last=True)
            mm.then_inc(k.banks_for_vector.sem, k.banks_for_vector.send())



def rows(*vectors):
    v = np.concatenate([np.asarray(a, np.float32).ravel() for a in vectors])
    n = -(-v.size // SLOT)
    out = np.zeros((n, P, SLOT), np.float32)
    for i in range(n):
        piece = v[i * SLOT:(i + 1) * SLOT]
        out[i, :, :piece.size] = piece[None, :]
    return out


def params(*blocks):
    out = np.zeros((1, P, SLOT), np.float32)
    at = 0
    for b in blocks:
        out[0, :b.shape[0], at:at + b.shape[1]] = b
        at += b.shape[1]
    return out


def by_columns(w):
    K, N = w.shape
    if N <= 256:
        return params(w.reshape(DC, P, N).transpose(1, 0, 2).reshape(P, DC * N))
    a = w.reshape(K // (4 * P), 4, P, N // 512, 512)
    return a.transpose(3, 0, 2, 1, 4).reshape(-1, P, SLOT)


def by_features(w):
    K, N = w.shape
    a = w.reshape(DC, P, N // (2 * P), 2, P)
    return a.transpose(2, 1, 3, 0, 4).reshape(-1, P, SLOT)


def in_halves(halves):
    n = len(halves)
    return np.stack(halves).reshape(n // 2, 2, P, HALF_SLOT).transpose(0, 2, 1, 3).reshape(-1, P, SLOT)


def two_layers(w_in, w_out, chunks, parts):
    halves = []
    for c in range(chunks + 1):
        if c < chunks:
            halves += [w_in[c, part] for part in range(parts)]
        if c >= 1:
            halves.append(w_out[c - 1])
    return in_halves(halves)


def ffn_halves(w_in, w_out):
    a = w_in.reshape(DC, P, 2, FC, P).transpose(3, 2, 1, 0, 4).reshape(FC, 2, P, HALF_SLOT)
    return two_layers(a, w_out.reshape(FC, P, D), FC, 2)


def gated_pair(w, n):
    a = w.reshape(DC, P, 2, n // P, P)
    return a.transpose(3, 1, 2, 0, 4).reshape(-1, P, SLOT)


def by_rows(w):
    K, N = w.shape
    return w.reshape(K // (2 * P), 2, P, N).transpose(0, 2, 1, 3).reshape(-1, P, SLOT)


def columns(v):
    return np.asarray(v).reshape(-1, P).T



def modulated(w, b, part):
    cols = slice(part * 3 * D, (part + 1) * 3 * D)
    return [by_columns(w[:, cols]), rows(b[cols])]


def modulation(k, gate_scale, gate_one):
    beside = k.last if isinstance(k.last, Post) else None
    if beside is not None:
        beside.accompanied = beside.gated
    made = Modulation(k, gate_scale, gate_one, beside)
    k.merged = made if beside is not None else None
    return made


def ffn_layers(k):
    room = Room(k)
    return TwoLayers(k, FC, 2, ACT.Silu, None, True, True, room(2, S), room(S))


def first_ffn(k, i, j, I=None):
    if I is not None:
        return modulated(I["ada_w"][i], I["ada_b"][i], 2 * j) + [
            ffn_halves(I["ffn_w_in"][i, j], I["ffn_w_out"][i, j]),
            rows(I["ln_g"][i, 2 * j], I["ln_b"][i, 2 * j])]
    f = [modulation(k, 0.5, True), Pre(k, False, True), ToFeatures(k, k.h_tok, k.h_t, DC), SplitInput(k),
         ffn_layers(k)]
    return f + [Post(k, True, True)]


def retention(k, I=None):
    n_qk, n_v = RET_HEADS * RET_QK, RET_HEADS * RET_V
    if I is not None:
        w = I["ret_w_in"][0]
        return modulated(I["ada_w"][0], I["ada_b"][0], 1) + [
            by_features(w[:, :2 * n_qk]), by_columns(w[:, 2 * n_qk:]), params(ret_decay()),
            by_rows(I["ret_w_out"][0]), rows(I["ln_g"][0, 1], I["ln_b"][0, 1])]
    room = Room(k)
    qk = room(2 * DC, S)
    v, g, w = room(TT, n_v), room(TT, n_v), room(RET_HEADS, 2 * S)
    o = room(TT, n_v)
    out = [modulation(k, 1.0, True), Pre(k, False, True), ToFeatures(k, k.h_tok, k.h_t, DC), SplitInput(k),
           ToFeatureRows(k, qk, 2 * DC),
           ToTokens(k, [(v[:, :, b * 512:(b + 1) * 512], None) for b in range(n_v // 512)]
                    + [(g[:, :, b * 512:(b + 1) * 512], ACT.Silu) for b in range(n_v // 512)]),
           RetScores(k, qk[:, 0:DC, :], qk[:, DC:, :], w), RetOut(k, w, v, g, o),
           ToFeatures(k, g, qk, n_v // P)]
    return out + [SplitInput(k, qk[:, 0:DC, :]), OutProj(k, True, False), SplitInput(k, qk[:, DC:, :]),
                  OutProj(k, False, True), Post(k, True, True)]


def peer(k, layer, I=None):
    if I is not None:
        keys = I["peer_keys_2"][layer].reshape(2 * PEER_HEADS, N_KEYS, P)
        u, v = I["peer_u_2"][layer], I["peer_v_2"][layer]
        n = u.shape[0] // P
        u = u.reshape(n, 1, P, DC, P).transpose(0, 1, 4, 3, 2).reshape(n, 1, P, D)
        v = v.reshape(n, P, D)
        experts = [two_layers(u[a:a + HALF], v[a:a + HALF], HALF, 1) for a in (0, HALF)]
        return [rows(I["ffn_norm_2"][layer]), by_features(I["peer_wq_2"][layer]),
                params(keys.transpose(2, 0, 1).reshape(P, -1))] + experts
    room = Room(k)
    gates = room(HALF, S)
    pairs, hot1, hot2 = room(3, S), room(HOT_RING, HALF), room(HOT_RING, P)
    act_out, product = room(2, S), room(S)
    early = Room(k)
    q_t, scores = early(2 * PEER_HEADS, S), early(TT, 2 * PEER_HEADS * N_KEYS)
    found = hot2.rearrange("p a b -> p (a b)")[:, 0:3 * TT * PAIRS].rearrange("p (a b) -> p a b", a=3)
    blocks = [(found[:, a, t * PAIRS:(t + 1) * PAIRS], pairs[:, a, t * P:(t + 1) * P])
              for a in range(3) for t in range(TT)]
    out = [Pre(k, True, False), ToFeatures(k, k.h_tok, k.h_t, DC), SplitInput(k), ToFeatureRows(k, q_t, 2 * PEER_HEADS),
           KeyScores(k, q_t, scores), Route(k, scores, early, found),
           Turn(k, [([src], dst.unsqueeze(1)) for src, dst in blocks])]
    for half in range(2):
        out += [SpreadGates(k, half, pairs, gates, hot1, hot2), 
                TwoLayers(k, HALF, 1, ACT.Gelu, gates, half == 0, half == 1, act_out, product)]
    return out + [Post(k, False, False)]


def fox(k, I=None):
    if I is not None:
        w = I["od_w_in_2"][0]
        gains = np.concatenate([np.tile(I["od_q_norm_g_2"][0], FOX_HEADS), np.tile(I["od_k_norm_g_2"][0], FOX_HEADS)])
        return [rows(I["od_norm_mix_2"][0]), by_columns(w[:, :3 * D]), by_columns(w[:, 3 * D:]), rows(gains),
                rows(I["od_fgate_b_2"][0]), params(pick_head()), by_rows(I["od_w_out_2"][0])]
    room = Room(k)
    qk, v, qk_t = room(TT, 2 * D), room(TT, D), room(2 * DC, S)
    p = room(3 * FOX_HEADS, P)
    z, lf, tmp = (room(TT, FOX_HEADS) for _ in range(3))
    c, c_t = room(TT, FOX_HEADS), room(S)
    top, total = room(TT * FOX_HEADS), room(TT * FOX_HEADS)
    p_t = room(3 * FOX_HEADS, P)
    squares = p_t.rearrange("p a b -> p (a b)")[:, 0:4 * D].rearrange("p (t n) -> p t n", t=TT)
    mask = k.c("mask").rearrange("p (t q) -> p t q", t=TT)
    norm, gates = HeadNorm, ForgetGates
    out = [Pre(k, True, False), ToFeatures(k, k.h_tok, k.h_t, DC), SplitInput(k),
           ToTokens(k, [(qk[:, :, b * 512:(b + 1) * 512], None) for b in range(4)]
                    + [(v[:, :, b * 512:(b + 1) * 512], None) for b in range(2)]),
           ToTokensNarrow(k, [(FOX_HEADS, z, None)]),
           HeadNorm(k, qk, squares), ForgetGates(k, z, lf, tmp, c, c_t[0:FOX_HEADS, :]),
           ToFeatures(k, qk, qk_t, 2 * DC)]
    where = [0]
    side = lambda first: lambda h: qk_t[64 * (h % 2):64 * (h % 2) + 64, first + h // 2, :]

    def minus_key(bank, t, h, n):
        return k.mm(bank, k.slot(where[0])[0:FOX_HEADS, h * P:(h + 1) * P], c_t[0:FOX_HEADS, 0:n], start=False,
                    stop=True, last=True)

    def how(t, h, n):
        return lambda dve, dst, bank: dve.scalar_tensor_tensor(dst, bank, c[:, t, h:h + 1], mask[:, t, 0:n],
                                                               ALU.add, ALU.add)

    att = causal_attention(k, FOX_HEADS, side(0), side(DC), lambda h, a: v[:, a, h * HD:(h + 1) * HD],
                           minus_key, how, p, p_t, top, total, total, k.h_tok, False, extra_slots=1)
    where[0] = att[0].s
    return out + att + [ToFeatures(k, k.h_tok, k.h_t, DC), SplitInput(k), OutProj(k), Post(k, False, False)]


def nsa(k, I=None):
    kv = NSA_GROUPS * HD
    if I is not None:
        w = I["nsa_w_in"][0]
        part = [w[:, D + j * kv:D + (j + 1) * kv] for j in range(6)]
        twice = lambda a: np.repeat(a.reshape(D, NSA_GROUPS, 1, HD), 2, axis=2).reshape(D, 2 * kv)
        first = lambda a: a.reshape(2, 8, P, CMP_HIDDEN).transpose(0, 2, 1, 3).reshape(2, P, SLOT)
        pe = [I[n][0].reshape(CMP // 2, P).T for n in ("nsa_pe_k", "nsa_pe_v")]
        second = lambda a, n: np.tile(a.reshape(2, P, 1, HD), (1, 1, n, 1)).transpose(1, 0, 2, 3).reshape(P, -1)
        return modulated(I["ada_w"][1], I["ada_b"][1], 1) + [
            by_features(np.concatenate([w[:, :D], part[0], part[1], twice(part[2]), twice(part[4])], axis=1)),
            by_columns(np.concatenate([part[3], part[5]], axis=1)), by_columns(w[:, D + 6 * kv:]),
            params(pe[0], pe[1], second(I["nsa_ck_w2"][0], 2), second(I["nsa_cv_w2"][0], 1)),
            first(I["nsa_ck_w1"][0]), first(I["nsa_cv_w1"][0]), by_rows(I["nsa_w_out"][0]),
            rows(I["ln_g"][1, 1], I["ln_b"][1, 1])]
    room = Room(k)
    H = NSA_HEADS
    feat, v, gates = room(20, S), room(TT, 2 * kv), room(TT, 3 * H)
    p, p_t = room(3 * H, P), room(3 * H, P)
    couples = p.rearrange("p a b -> p (a b)")[:, 0:2 * NSA_GROUPS * S].rearrange("p (g t) -> p g t", t=S)
    hidden, ck, cv = room(2, NSA_GROUPS * N_CMP), room(NSA_GROUPS * N_CMP), room(kv)
    top, total, factor = room(TT * H), room(TT * H), room(TT * H)
    q = lambda h: feat[64 * (h % 2):64 * (h % 2) + 64, h // 2, :]
    slope = lambda h: float(2.0 ** (-8.0 * (h + 1) / H))
    dist = k.c("dist").rearrange("p (t q) -> p t q", t=TT)
    cmp_dist = k.c("cmp_dist").rearrange("p (t q) -> p t q", t=TT)
    cmp_mask = k.c("cmp_mask").rearrange("p (t q) -> p t q", t=TT)

    def alibi(d):
        return lambda t, h, n: lambda dve, dst, bank: dve.scalar_tensor_tensor(
            dst, d[:, t, 0:n], -slope(h), bank, ALU.mult, ALU.add)

    out = [modulation(k, 1.0, True), Pre(k, False, True), ToFeatures(k, k.h_tok, k.h_t, DC), SplitInput(k),
           ToFeatureRows(k, feat, 20, scaled=DC, scale=HD ** -0.5),
           ToTokens(k, [(v, None)]), ToTokensNarrow(k, [(3 * H, gates, ACT.Sigmoid)]),
           Compress(k, feat[:, DC:DC + 4, :], couples, hidden, ck, cv[0:N_CMP, :], room(CMP + 2 * P + 2 * HD))]
    jobs = [(t, h) for t in range(TT) for h in range(H)]

    def cmp_product(t, h):
        g, base = h // 4, 64 * (h % 2)
        return lambda bank: k.mm(bank, q(h)[:, t * P:(t + 1) * P], ck[base:base + 64, g * N_CMP:(g + 1) * N_CMP],
                                 start=True, stop=True, last=True)

    small = p[:, 0:4, :].rearrange("p a b -> p (a b)")[:, 0:2 * H * N_CMP].rearrange("p (j n) -> p j n", n=N_CMP)
    out.append(Scores(k, [(cmp_product(t, h), N_CMP, alibi(cmp_dist)(t, h, N_CMP), small[:, i, :])
                          for i, (t, h) in enumerate(jobs)], top, total, keep=lambda i: cmp_mask[:, jobs[i][0], :]))
    out.append(Gates(k, factor, gates, total, 0))
    out.append(Turn(k, [([small[:, i + j, :] for j in range(4)], p_t[0:N_CMP, i:i + 4, :]) for i in range(0, 2 * H, 4)]))
    out.append(Values(k, [([p_t[0:N_CMP, i, :]], [cv[0:N_CMP, h // 4 * HD:(h // 4 + 1) * HD]], factor[:, i:i + 1],
                           k.h_tok[:, t, h * HD:(h + 1) * HD]) for i, (t, h) in enumerate(jobs)], False))
    for branch in (1, 2):
        first = DC + 4 + 4 * (branch - 1)
        kt = lambda h, first=first: feat[64 * (h % 2):64 * (h % 2) + 64, first + h // 4, :]
        val = lambda h, a, b=branch: v[:, a, (b - 1) * kv + h // 4 * HD:(b - 1) * kv + (h // 4 + 1) * HD]
        att = causal_attention(k, H, q, kt, val, None, alibi(dist), p, p_t, top, total, factor, k.h_tok, True)
        out += [att[0], Gates(k, factor, gates, total, branch), att[1], att[2]]
    return out + [ToFeatures(k, k.h_tok, k.h_t, DC), SplitInput(k), OutProj(k), Post(k, True, True)]


def even(k, I=None):
    cuts = np.cumsum([CONV, CONV, 256, 256, 512, 512])
    if I is not None:
        w = I["ev_w_in_2"][0]
        taps = I["ev_conv_w_2"][0].reshape(TAPS, CONV // P, P).transpose(2, 1, 0).reshape(P, -1)
        return [rows(I["ev_norm_mix_2"][0]),
                params(taps, columns(I["ev_conv_b_2"][0]), I["ev_gate_w2_2"][0], by_columns(w[:, cuts[5]:])[0, :, 0:P]),
                rows(I["ev_gate_b_2"][0], np.tile(I["ev_gla_norm_g_2"][0], GLA_HEADS), I["ev_conv_ln_g_2"][0],
                     I["ev_conv_ln_b_2"][0]),
                by_features(w[:, :cuts[3]]), by_columns(w[:, cuts[3]:cuts[5]])] + modulated(I["w_ada_3"][0], I["b_ada_3"][0], 0) + [
                by_rows(I["ev_w_out_2"][0])]
    room = Room(k)
    n_tap = CONV // P * TAPS
    extra, norms = room(n_tap + 4 + S + P), room(S + 3 * 512)
    feat, v, r = room(12, S), room(TT, 512), room(TT, 512)
    u, y, y_tok = room(4, PAD + S), room(4, S), room(TT, 512)
    low, z, b_t, ref, q_s = room(S)[0:16, :], room(TT, S), room(2, S), room(2, N_SUB), room(2, S)
    k_a, k_b = room(2, N_SUB * P), room(2, N_SUB // 2 * P)
    k_a, k_b = (b.rearrange("p a (n s) -> p a n s", s=P) for b in (k_a, k_b))
    w, o = room(GLA_HEADS, TT * S), room(TT, 512)
    w = w.rearrange("p h (a q) -> p h a q", a=TT)
    tmp = o.rearrange("p a b -> p (a b)")[:, 0:TT * S].rearrange("p (a b) -> p a b", a=TT)
    second = [k.h_tok[:, t, 512:] for t in range(TT)]
    return [Pre(k, True, False), ToFeatures(k, k.h_tok, k.h_t, DC), SplitInput(k), Keep(k, extra), Keep(k, norms),
            ToFeatureRows(k, feat, 12),
            ToTokens(k, [(v, None), (r, ACT.Silu)]),
            Modulation(k, 0.5, False, Convolve(k, feat, u, y, extra, extra[:, n_tap:n_tap + 4])),
            Turn(k, [([y[:, c, t * P:(t + 1) * P] for c in range(4)],
                      y_tok[:, t, :].rearrange("p (c q) -> p c q", q=P)) for t in range(TT)]),
            ConvNorm(k, y_tok, k.h_tok[:, :, 0:512], norms[:, S + 512:S + 1024], norms[:, S + 1024:]),
            GlaDecays(k, extra[:, n_tap + 4 + S:], extra[0:16, n_tap + 4:n_tap + 4 + S], norms[:, 0:S], low, z, tmp,
                      b_t),
            GlaScale(k, feat[:, 8:10, :], feat[:, 10:12, :], b_t, ref, q_s, k_a, k_b),
            GlaAttend(k, q_s, k_a, k_b, w, v, o),
            HeadRms(k, [o[:, t, :] for t in range(TT)], second, GLA_DV, norms[:, S:S + 512], r,
                    [y[:, 2 * t:2 * t + 2, :].rearrange("p a b -> p (a b)") for t in range(TT)]),
            ToFeatures(k, k.h_tok, k.h_t, DC), SplitInput(k), OutProj(k), Post(k, False, False)]


def third_ffn(k, j, I=None):
    if I is not None:
        n = j + 1 if j == 0 else 2
        first = modulated(I["w_ada_3"][0], I["b_ada_3"][0], 2 * j) if j > 0 else []
        return first + [rows(I[f"norm_ffn{n}_3"][0]), ffn_halves(I[f"w_ffn{n}_gu_3"][0], I[f"w_ffn{n}_down_3"][0])]
    first = [modulation(k, 0.5, False)] if j > 0 else []
    return first + [Pre(k, True, True), ToFeatures(k, k.h_tok, k.h_t, DC), SplitInput(k), ffn_layers(k),
                    Post(k, False, True)]


def third_mix(k, I=None):
    H = ROPE_HEADS
    if I is not None:
        return modulated(I["w_ada_3"][0], I["b_ada_3"][0], 1) + [
            rows(I["norm_mix_3"][0]), by_columns(I["w_in_3"][0]),
            params(I["gmlp_w_s_3"][0].transpose(2, 0, 1).reshape(P, -1), I["gmlp_b_s_3"][0].T),
            rows(I["gmlp_ln_g_3"][0], I["gmlp_ln_b_3"][0], I["g_attn_out_3"][0], I["g_gmlp_out_3"][0]),
            by_rows(I["w_out_3"][0])]
    room = Room(k)
    qk, v, gu, gv = room(TT, D), room(TT, 512), room(TT, 512), room(TT, 512)
    extra, norms = room(D + H), room(SLOT)
    tmp, qk_t = room(TT, D), room(DC, S)
    p, p_t = room(3 * H, P), room(3 * H, P)
    top, total = room(TT * H), room(TT * H)
    mask = k.c("mask").rearrange("p (t q) -> p t q", t=TT)
    side = lambda first: lambda h: qk_t[64 * (h % 2):64 * (h % 2) + 64, first + h // 2, :]

    def how(t, h, n):
        return lambda dve, dst, bank: dve.scalar_tensor_tensor(dst, bank, HD ** -0.5, mask[:, t, 0:n], ALU.mult,
                                                               ALU.add)

    att = causal_attention(k, H, side(0), side(4), lambda h, a: v[:, a, h * HD:(h + 1) * HD], None, how, p, p_t,
                           top, total, total, k.h_tok, False)
    halves = [[k.h_tok[:, t, a * 512:(a + 1) * 512] for t in range(TT)] for a in range(2)]
    squares = [tmp[:, t, 0:512] for t in range(TT)]
    return [modulation(k, 1.0, False), Pre(k, True, True), ToFeatures(k, k.h_tok, k.h_t, DC), SplitInput(k),
            ToTokens(k, [(qk[:, :, 0:512], None), (qk[:, :, 512:], None), (v, None),
                         (gu, ACT.Gelu_apprx_tanh), (gv, ACT.Gelu_apprx_tanh)]),
            Keep(k, extra), Keep(k, norms), Rope(k, qk, tmp), ToFeatures(k, qk, qk_t, DC)] + att + [
            Spatial(k, gu, gv, extra[:, 0:D].rearrange("p (h t) -> p h t", t=P), extra[:, D:], norms[:, 0:512],
                    norms[:, 512:1024], k.h_tok[:, :, 512:]),
            HeadRms(k, halves[0], halves[0], 512, norms[:, 1024:1536], None, squares),
            HeadRms(k, halves[1], halves[1], 512, norms[:, 1536:], None, squares),
            ToFeatures(k, k.h_tok, k.h_t, DC), SplitInput(k), OutProj(k), Post(k, False, True)]


def final_norm(k, I=None):
    if I is not None:
        return [rows(I["norm_final_3"])]
    return [Pre(k, True, False, dst=k.x)]


def silu_c(k, name, I=None):
    if I is not None:
        return [params(columns(I[name][0]))]
    return [Silu_c(k, name)]


def layers(only=None):
    out = [("c0", silu_c, ("c",)), ("a0", first_ffn, (0, 0)), ("m0", retention, ()), ("b0", first_ffn, (0, 1)),
           ("a1", first_ffn, (1, 0)), ("m1", nsa, ()), ("b1", first_ffn, (1, 1)),
           ("c3", silu_c, ("c_3",)), ("ev", even, ()), ("p0", peer, (0,)), ("od", fox, ()), ("p1", peer, (1,)),
           ("t1", third_ffn, (0,)), ("t2", third_mix, ()), ("t3", third_ffn, (1,)),
           ("fin", final_norm, ())]
    return [x for x in out if only is None or x[0] in only]


def plan(k, only=None):
    stages = []
    for _, f, a in layers(only):
        k.last = stages[-1] if stages else None
        made = f(k, *a)
        if made[0] is not k.last and k.last is not None and made[0] is k.merged:
            stages.pop()
        stages += made
    return stages


def program(nc, x, const, stream, out, only=None):
    with ExitStack() as ctx:
        k = Chip(ctx, nc)
        stages = plan(k, only)
        total = k.n_slots
        assert total == stream.shape[0], (total, stream.shape)
        block = ctx.enter_context(nc.Block())

        @block.sync
        def _(sp):
            for s in range(total):
                if s >= RING:
                    sp.wait_ge(k.slots_used, s - RING + 1)
                sp.dma_start(k.slot(s), stream[s]).then_inc(k.slot_landed[s % RING], 16)

        def run(eng, name):
            eng.wait_ge(k.loaded, 32)
            for i, s in enumerate(stages):
                parts = {"tensor": s.tensor, "vector": s.vector, "scalar": s.scalar, "gpsimd": s.gpsimd}
                parts[name](eng)
                k.phase_end(eng, i)

        @block.tensor
        def _(pe):
            run(pe, "tensor")

        @block.vector
        def _(dve):
            run(dve, "vector")

        @block.gpsimd
        def _(pool):
            run(pool, "gpsimd")

        @block.scalar
        def _(act):
            act.dma_start(k.x[:, :, :], x.rearrange("b (t p) d -> p (b t) d", p=P)).then_inc(k.loaded, 16)
            act.dma_start(k.const[:, :], const).then_inc(k.loaded, 16)
            run(act, "scalar")
            act.dma_start(out.rearrange("b (t p) d -> p (b t) d", p=P), k.x[:, :, :]).then_inc(k.stored, 16)
            act.wait_ge(k.stored, 16)

        for g in k.signals:
            assert g.sent == g.seen, (g.name, g.sent, g.seen)


def stream_of(inputs, only=None):
    return np.concatenate([b for _, f, a in layers(only) for b in f(None, *a, I=inputs)])


def kernel(**inputs):
    import concourse.bacc as bacc
    from concourse.bass_utils import run_bass_kernel_spmd

    I = {n: np.asarray(v) for n, v in inputs.items()}
    arrays = {"x": I["x"], "const": np.concatenate(list(CONSTS.values()), axis=1), "stream": stream_of(I)}
    nc = bacc.Bacc("TRN2", target_bir_lowering=False, num_devices=1)
    args = [nc.dram_tensor(n, a.shape, F32, kind="ExternalInput").ap() for n, a in arrays.items()]
    out = nc.dram_tensor("out", (1, S, D), F32, kind="ExternalOutput").ap()
    program(nc, *args, out)
    r = run_bass_kernel_spmd(nc, [arrays], core_ids=[0])
    return r.results[0]["out"]
```
